# Optimizing a Trainium2 kernel written in Bass

```python
import jax, jax.numpy as jnp
from jax import lax
import numpy as np

D_MODEL = 2048
BATCH = 1
SEQ = 256
DEPTH = 2

GRID_W = 64
HEAD_DIM = 128
A_HEADS = 8
A_KV_HEADS = 2
B_HEADS = 4
B_Q_LORA = 512
B_KV_LORA = 256
B_NOPE = 128
B_ROPE = 64
B_V = 128
C_HEADS = 4
WIN_ROWS = 8
WIN_COLS = 16
D_MIX = A_HEADS * HEAD_DIM + B_HEADS * B_V + C_HEADS * HEAD_DIM
Q_BLOCK = 128
ROPE_THETA = 10000.0
NORM_EPS = 1e-6
IN_SPLITS = (
    A_HEADS * HEAD_DIM,
    A_KV_HEADS * HEAD_DIM,
    A_KV_HEADS * HEAD_DIM,
    A_HEADS * HEAD_DIM,
    B_Q_LORA,
    B_KV_LORA,
    B_ROPE,
    B_HEADS * B_V,
    C_HEADS * HEAD_DIM,
    C_HEADS * HEAD_DIM,
    C_HEADS * HEAD_DIM,
    C_HEADS * HEAD_DIM,
)
D_IN = sum(IN_SPLITS)


def _rms_norm(x, g):
    xf = x.astype(jnp.float32)
    y = xf * lax.rsqrt(jnp.mean(xf * xf, axis=-1, keepdims=True) + NORM_EPS)
    return (y * g.astype(jnp.float32)).astype(x.dtype)

def _rope_half(x, pos):
    n = x.shape[-1]
    inv_freq = 1.0 / (ROPE_THETA ** (jnp.arange(0, n, 2, dtype=jnp.float32) / n))
    ang = pos.astype(jnp.float32)[:, None] * inv_freq[None, :]
    cos = jnp.cos(ang)[:, None, :]
    sin = jnp.sin(ang)[:, None, :]
    xf = x.astype(jnp.float32)
    x1, x2 = xf[..., : n // 2], xf[..., n // 2:]
    out = jnp.concatenate([x1 * cos - x2 * sin, x2 * cos + x1 * sin], axis=-1)
    return out.astype(x.dtype)

def _rope_axial(x, row, col):
    h = x.shape[-1] // 2
    return jnp.concatenate([_rope_half(x[..., :h], row), _rope_half(x[..., h:], col)], axis=-1)

def _dense_block_attention(q, k, v):
    B, S, H, dq = q.shape
    Hk = k.shape[2]
    G = H // Hk
    dv = v.shape[-1]
    nb = S // Q_BLOCK
    scale = dq ** -0.5
    qb = q.reshape(B, nb, Q_BLOCK, Hk, G, dq).transpose(1, 0, 2, 3, 4, 5)

    def one(qblk):
        s = jnp.einsum('bqkgd,bskd->bkgqs', qblk, k).astype(jnp.float32) * scale
        p = jax.nn.softmax(s, axis=-1).astype(v.dtype)
        return jnp.einsum('bkgqs,bskd->bqkgd', p, v)

    o = lax.map(one, qb)
    return o.transpose(1, 0, 2, 3, 4, 5).reshape(B, S, H, dv)

def _neighbourhood_attention(q, k, v, rpb):
    B, S, H, d = q.shape
    rows = S // GRID_W
    kr = min(WIN_ROWS, rows)
    nk = kr * WIN_COLS
    t = jnp.arange(S)
    r = t // GRID_W
    c = t % GRID_W
    r0 = jnp.clip(r - kr // 2, 0, rows - kr)
    c0 = jnp.clip(c - WIN_COLS // 2, 0, GRID_W - WIN_COLS)
    key_r = r0[:, None, None] + jnp.arange(kr)[None, :, None]
    key_c = c0[:, None, None] + jnp.arange(WIN_COLS)[None, None, :]
    idx = (key_r * GRID_W + key_c).reshape(S, nk)
    dr = key_r - r[:, None, None] + (WIN_ROWS - 1)
    dc = key_c - c[:, None, None] + (WIN_COLS - 1)
    bias = rpb[:, dr, dc].reshape(H, S, nk)
    nb = S // Q_BLOCK
    scale = d ** -0.5
    qb = q.reshape(B, nb, Q_BLOCK, H, d).transpose(1, 0, 2, 3, 4)
    idxb = idx.reshape(nb, Q_BLOCK, nk)
    biasb = bias.reshape(H, nb, Q_BLOCK, nk).transpose(1, 0, 2, 3)

    def one(args):
        qblk, iblk, bblk = args
        kg = jnp.take(k, iblk, axis=1)
        vg = jnp.take(v, iblk, axis=1)
        s = jnp.einsum('bqhd,bqnhd->bhqn', qblk, kg).astype(jnp.float32) * scale
        s = s + bblk[None].astype(jnp.float32)
        p = jax.nn.softmax(s, axis=-1).astype(v.dtype)
        return jnp.einsum('bhqn,bqnhd->bqhd', p, vg)

    o = lax.map(one, (qb, idxb, biasb))
    return o.transpose(1, 0, 2, 3, 4).reshape(B, S, H, d)

def _layer(x, g_pre, g_post, w_in, a_qn, a_kn, b_qn, b_kvn, w_uq, w_ukv, rpb, w_out, row, col):
    B, S, _ = x.shape
    h = _rms_norm(x, g_pre)
    proj = jnp.einsum('bsd,de->bse', h, w_in)
    split_points = [int(p) for p in np.cumsum(IN_SPLITS)[:-1]]
    (a_q, a_k, a_v, a_g, b_cq, b_ckv, b_kr, b_g,
     c_q, c_k, c_v, c_g) = jnp.split(proj, split_points, axis=-1)

    qa = _rms_norm(a_q.reshape(B, S, A_HEADS, HEAD_DIM), a_qn)
    ka = _rms_norm(a_k.reshape(B, S, A_KV_HEADS, HEAD_DIM), a_kn)
    va = a_v.reshape(B, S, A_KV_HEADS, HEAD_DIM)
    qa = _rope_axial(qa, row, col)
    ka = _rope_axial(ka, row, col)
    o_a = _dense_block_attention(qa, ka, va).reshape(B, S, A_HEADS * HEAD_DIM) * jax.nn.silu(a_g)

    cq = _rms_norm(b_cq, b_qn)
    qb = jnp.einsum('bsr,re->bse', cq, w_uq).reshape(B, S, B_HEADS, B_NOPE + B_ROPE)
    q_nope, q_pe = qb[..., :B_NOPE], qb[..., B_NOPE:]
    q_pe = _rope_axial(q_pe, row, col)
    ckv = _rms_norm(b_ckv, b_kvn)
    kv = jnp.einsum('bsr,re->bse', ckv, w_ukv).reshape(B, S, B_HEADS, B_NOPE + B_V)
    k_nope, vb = kv[..., :B_NOPE], kv[..., B_NOPE:]
    k_pe = _rope_axial(b_kr.reshape(B, S, 1, B_ROPE), row, col)
    k_pe = jnp.broadcast_to(k_pe, (B, S, B_HEADS, B_ROPE))
    q_full = jnp.concatenate([q_nope, q_pe], axis=-1)
    k_full = jnp.concatenate([k_nope, k_pe], axis=-1)
    o_b = _dense_block_attention(q_full, k_full, vb).reshape(B, S, B_HEADS * B_V) * jax.nn.silu(b_g)

    qc = c_q.reshape(B, S, C_HEADS, HEAD_DIM)
    kc = c_k.reshape(B, S, C_HEADS, HEAD_DIM)
    vc = c_v.reshape(B, S, C_HEADS, HEAD_DIM)
    o_c = _neighbourhood_attention(qc, kc, vc, rpb).reshape(B, S, C_HEADS * HEAD_DIM) * jax.nn.silu(c_g)

    y = jnp.einsum('bse,ed->bsd', jnp.concatenate([o_a, o_b, o_c], axis=-1), w_out)
    return x + _rms_norm(y, g_post)

def first_inputs(seed: int = 0) -> dict:
    key = jax.random.key(seed)
    ks = jax.random.split(key, 13)
    f32 = jnp.float32

    def gain(k, n):
        return 1.0 + 0.05 * jax.random.normal(k, (DEPTH, n), f32)

    x = jax.random.normal(ks[0], (BATCH, SEQ, D_MODEL), f32)
    norm_pre = gain(ks[1], D_MODEL)
    norm_post = gain(ks[2], D_MODEL)
    w_in = jax.random.normal(ks[3], (DEPTH, D_MODEL, D_IN), f32) * D_MODEL ** -0.5
    a_q_norm = gain(ks[4], HEAD_DIM)
    a_k_norm = gain(ks[5], HEAD_DIM)
    b_q_norm = gain(ks[6], B_Q_LORA)
    b_kv_norm = gain(ks[7], B_KV_LORA)
    b_w_uq = jax.random.normal(ks[8], (DEPTH, B_Q_LORA, B_HEADS * (B_NOPE + B_ROPE)), f32) * B_Q_LORA ** -0.5
    b_w_ukv = jax.random.normal(ks[9], (DEPTH, B_KV_LORA, B_HEADS * (B_NOPE + B_V)), f32) * B_KV_LORA ** -0.5
    c_rpb = 0.1 * jax.random.normal(ks[10], (DEPTH, C_HEADS, 2 * WIN_ROWS - 1, 2 * WIN_COLS - 1), f32)
    w_out = jax.random.normal(ks[11], (DEPTH, D_MIX, D_MODEL), f32) * D_MIX ** -0.5
    return {"x": x, "norm_pre": norm_pre, "norm_post": norm_post, "w_in": w_in,
            "a_q_norm": a_q_norm, "a_k_norm": a_k_norm, "b_q_norm": b_q_norm,
            "b_kv_norm": b_kv_norm, "b_w_uq": b_w_uq, "b_w_ukv": b_w_ukv,
            "c_rpb": c_rpb, "w_out": w_out}

def first_block(x, norm_pre, norm_post, w_in, a_q_norm, a_k_norm, b_q_norm, b_kv_norm,
              b_w_uq, b_w_ukv, c_rpb, w_out):
    S = x.shape[1]
    t = jnp.arange(S)
    row = t // GRID_W
    col = t % GRID_W
    h = x
    for l in range(DEPTH):
        h = _layer(h, norm_pre[l], norm_post[l], w_in[l], a_q_norm[l], a_k_norm[l],
                   b_q_norm[l], b_kv_norm[l], b_w_uq[l], b_w_ukv[l], c_rpb[l], w_out[l],
                   row, col)
    return h


DEPTH_2 = 1

MIX_WIDTH = D_MODEL
NSA_HEAD_DIM = 64
NSA_HEADS = (MIX_WIDTH // 2) // NSA_HEAD_DIM
NSA_KV_HEADS = max(1, NSA_HEADS // 4)
NSA_GROUP = NSA_HEADS // NSA_KV_HEADS
NSA_WIDTH = NSA_HEADS * NSA_HEAD_DIM
NSA_KV_WIDTH = NSA_KV_HEADS * NSA_HEAD_DIM
CMP_LEN = 32
CMP_STRIDE = 16
CMP_HIDDEN = 128
SLC_BLOCK = 64
SLC_TOPK = 16
SLC_LOCAL = 2
WINDOW = 512
NSA_QBLOCK = 64
SLC_FORCE_SCORE = 1e4
NEG_INF = -1e30
RET_HEADS = 8
RET_WIDTH = MIX_WIDTH - NSA_WIDTH
RET_V_DIM = RET_WIDTH // RET_HEADS
RET_QK_DIM = RET_V_DIM
RET_CHUNK = 128
IN_SIZES = (NSA_WIDTH,) + (NSA_KV_WIDTH,) * 6 + (3 * NSA_HEADS, RET_HEADS * RET_QK_DIM, RET_HEADS * RET_QK_DIM, RET_WIDTH, RET_WIDTH)
IN_WIDTH = NSA_WIDTH + 6 * NSA_KV_WIDTH + 3 * NSA_HEADS + 2 * RET_HEADS * RET_QK_DIM + 2 * RET_WIDTH
PEER_HEADS = 8
PEER_N_KEYS = 128
PEER_EXPERTS = PEER_N_KEYS * PEER_N_KEYS
PEER_TOPK = 16
PEER_QUERY_DIM = 256
PEER_CHUNK = 128
EPS = 1e-6


F32 = jnp.float32

def rmsnorm(x, g):
    xf = x.astype(F32)
    y = xf * lax.rsqrt(jnp.mean(xf * xf, axis=-1, keepdims=True) + EPS)
    return (y * g.astype(F32)).astype(x.dtype)

def alibi_slopes(n):
    return jnp.exp2(-8.0 * (jnp.arange(n, dtype=F32) + 1.0) / n)

def split_cols(a, sizes):
    idx = []
    acc = 0
    for s in sizes[:-1]:
        acc += s
        idx.append(acc)
    return jnp.split(a, idx, axis=-1)

def nsa_compress(k, pe, w1, w2, idx):
    B, n_cmp, L = k.shape[0], idx.shape[0], idx.shape[1]
    blk = k[:, idx] + pe[:, None, :]
    blk = jnp.swapaxes(blk, 2, 3).reshape(B, n_cmp, NSA_KV_HEADS, L * NSA_HEAD_DIM)
    out = jax.nn.gelu(blk @ w1) @ w2
    return jnp.swapaxes(out, 1, 2)

def nsa_attention(q, kc, vc, ks, vs, kw, vw, gates, pe_k, pe_v, ck_w1, ck_w2, cv_w1, cv_w2):
    B, S = q.shape[0], q.shape[1]
    G, R, dk, QB = NSA_KV_HEADS, NSA_GROUP, NSA_HEAD_DIM, NSA_QBLOCK
    scale = dk ** -0.5
    dt = q.dtype
    n_cmp = (S - CMP_LEN) // CMP_STRIDE + 1
    cmp_idx = np.arange(n_cmp)[:, None] * CMP_STRIDE + np.arange(CMP_LEN)[None, :]
    cmp_end = jnp.asarray(cmp_idx[:, -1], jnp.int32)
    Kc = nsa_compress(kc, pe_k, ck_w1, ck_w2, cmp_idx)
    Vc = nsa_compress(vc, pe_v, cv_w1, cv_w2, cmp_idx)
    n_slc = S // SLC_BLOCK
    top_n = min(SLC_TOPK, n_slc)
    slc_start = np.arange(n_slc) * SLC_BLOCK
    overlap = jnp.asarray(((cmp_idx[:, :1] < slc_start[None, :] + SLC_BLOCK)
                           & (cmp_idx[:, -1:] >= slc_start[None, :])).astype(np.float32))
    Ks = ks.reshape(B, n_slc, SLC_BLOCK, G, dk).transpose(0, 3, 1, 2, 4)
    Vs = vs.reshape(B, n_slc, SLC_BLOCK, G, dk).transpose(0, 3, 1, 2, 4)
    Kw = jnp.pad(kw, ((0, 0), (WINDOW, 0), (0, 0), (0, 0)))
    Vw = jnp.pad(vw, ((0, 0), (WINDOW, 0), (0, 0), (0, 0)))
    slopes = alibi_slopes(NSA_HEADS).reshape(G, R)[:, :, None, None]
    nqb = S // QB
    qb = q.reshape(B, nqb, QB, G, R, dk).transpose(1, 0, 3, 4, 2, 5)
    gb = gates.reshape(B, nqb, QB, G, R, 3).transpose(1, 0, 3, 4, 2, 5)
    b_ix = jnp.arange(B)[:, None, None, None]
    g_ix = jnp.arange(G)[None, :, None, None]
    blk_ids = jnp.arange(n_slc)
    in_blk = jnp.arange(SLC_BLOCK)
    win_off = jnp.arange(WINDOW + QB)

    def query_block(args):
        i, qi, gi = args
        t = i * QB + jnp.arange(QB)
        d_c = t[:, None] - cmp_end[None, :]
        valid_c = d_c >= 0
        s_c = jnp.einsum('bgrqd,bgnd->bgrqn', qi, Kc).astype(F32) * scale - slopes * d_c.astype(F32)
        p_c = jnp.where(valid_c, jax.nn.softmax(jnp.where(valid_c, s_c, NEG_INF), axis=-1), 0.0)
        o_c = jnp.einsum('bgrqn,bgnd->bgrqd', p_c.astype(dt), Vc)
        imp = jnp.einsum('bgrqn,nm->bgqm', p_c, overlap)
        back = (t // SLC_BLOCK)[:, None] - blk_ids[None, :]
        valid_s = back >= 0
        forced = valid_s & ((blk_ids[None, :] == 0) | (back < SLC_LOCAL))
        imp = jnp.where(forced, SLC_FORCE_SCORE, jnp.where(valid_s, imp, -1.0))
        _, sel = lax.top_k(imp, top_n)
        K_sel = Ks[b_ix, g_ix, sel].reshape(B, G, QB, top_n * SLC_BLOCK, dk)
        V_sel = Vs[b_ix, g_ix, sel].reshape(B, G, QB, top_n * SLC_BLOCK, dk)
        pos_s = (sel[..., None] * SLC_BLOCK + in_blk).reshape(B, G, QB, top_n * SLC_BLOCK)
        d_s = (t[None, None, :, None] - pos_s)[:, :, None]
        s_s = jnp.einsum('bgrqd,bgqkd->bgrqk', qi, K_sel).astype(F32) * scale - slopes * d_s.astype(F32)
        p_s = jax.nn.softmax(jnp.where(d_s >= 0, s_s, NEG_INF), axis=-1)
        o_s = jnp.einsum('bgrqk,bgqkd->bgrqd', p_s.astype(dt), V_sel)
        K_w = lax.dynamic_slice_in_dim(Kw, i * QB, WINDOW + QB, axis=1)
        V_w = lax.dynamic_slice_in_dim(Vw, i * QB, WINDOW + QB, axis=1)
        pos_w = i * QB - WINDOW + win_off
        d_w = t[:, None] - pos_w[None, :]
        valid_w = (d_w >= 0) & (d_w < WINDOW) & (pos_w[None, :] >= 0)
        s_w = jnp.einsum('bgrqd,bkgd->bgrqk', qi, K_w).astype(F32) * scale - slopes * d_w.astype(F32)
        p_w = jax.nn.softmax(jnp.where(valid_w, s_w, NEG_INF), axis=-1)
        o_w = jnp.einsum('bgrqk,bkgd->bgrqd', p_w.astype(dt), V_w)
        gw = jax.nn.sigmoid(gi.astype(F32))
        o = gw[..., 0:1] * o_c + gw[..., 1:2] * o_s + gw[..., 2:3] * o_w
        return o.astype(dt)

    out = lax.map(query_block, (jnp.arange(nqb), qb, gb))
    return out.transpose(1, 0, 4, 2, 3, 5).reshape(B, S, NSA_HEADS, dk)

def retention(q, k, v, gate, g_out):
    B, S = q.shape[0], q.shape[1]
    H, dk, dv, C = RET_HEADS, RET_QK_DIM, RET_V_DIM, RET_CHUNK
    nC = S // C
    dt = q.dtype
    lg = jnp.log1p(-jnp.exp2(-5.0 - jnp.arange(H, dtype=F32)))
    pos = jnp.arange(C, dtype=F32)
    diff = pos[:, None] - pos[None, :]
    intra_decay = jnp.where(diff >= 0, jnp.exp(lg[:, None, None] * jnp.maximum(diff, 0.0)), 0.0)
    k_decay = jnp.exp(lg[:, None] * (C - 1.0 - pos))
    q_decay = jnp.exp(lg[:, None] * (pos + 1.0))
    chunk_decay = jnp.exp(lg * C)

    def to_chunks(a):
        return a.reshape(B, nC, C, H, a.shape[-1]).transpose(0, 3, 1, 2, 4).astype(F32)

    qc = to_chunks(q)
    kc = to_chunks(k) * (dk ** -0.5)
    vc = to_chunks(v)
    att = jnp.einsum('bhncd,bhnsd->bhncs', qc, kc) * intra_decay[:, None]
    o_intra = jnp.einsum('bhncs,bhnse->bhnce', att, vc)
    kv = jnp.einsum('bhncd,bhnce->nbhde', kc * k_decay[:, None, :, None], vc)

    def step(state, kv_n):
        return state * chunk_decay[None, :, None, None] + kv_n, state

    _, r_prev = lax.scan(step, jnp.zeros((B, H, dk, dv), F32), kv)
    o_cross = jnp.einsum('bhncd,nbhde->bhnce', qc * q_decay[:, None, :, None], r_prev)
    o = (o_intra + o_cross).transpose(0, 2, 3, 1, 4).reshape(B, S, H, dv)
    mu = jnp.mean(o, axis=-1, keepdims=True)
    var = jnp.mean(jnp.square(o - mu), axis=-1, keepdims=True)
    y = (o - mu) * lax.rsqrt(var + EPS) * g_out.astype(F32)
    return (jax.nn.silu(gate.astype(F32)) * y.reshape(B, S, H * dv)).astype(dt)

def peer_ffn(h, w_q, sub_keys, w_u, w_v):
    B, S, D = h.shape
    T = B * S
    K = PEER_TOPK
    dt = h.dtype
    hf = h.reshape(T, D)
    q = (hf @ w_q).reshape(T, PEER_HEADS, 2, PEER_QUERY_DIM // 2)
    s_half = jnp.einsum('thpd,hpkd->thpk', q, sub_keys).astype(F32)
    v_half, i_half = lax.top_k(s_half, K)
    cand_s = (v_half[:, :, 0, :, None] + v_half[:, :, 1, None, :]).reshape(T, PEER_HEADS, K * K)
    cand_i = (i_half[:, :, 0, :, None] * PEER_N_KEYS + i_half[:, :, 1, None, :]).reshape(T, PEER_HEADS, K * K)
    top_s, pick = lax.top_k(cand_s, K)
    experts = jnp.take_along_axis(cand_i, pick, axis=-1)
    gates = jax.nn.softmax(top_s, axis=-1)
    n_chunks = T // PEER_CHUNK
    E = PEER_HEADS * K

    def chunk(args):
        hc, ec, gc = args
        a = jnp.einsum('cd,ced->ce', hc, w_u[ec]).astype(F32)
        coef = (gc * jax.nn.gelu(a)).astype(dt)
        return jnp.einsum('ce,ced->cd', coef, w_v[ec])

    out = lax.map(chunk, (hf.reshape(n_chunks, PEER_CHUNK, D),
                          experts.reshape(n_chunks, PEER_CHUNK, E),
                          gates.reshape(n_chunks, PEER_CHUNK, E)))
    return out.reshape(B, S, D).astype(dt)

def second_inputs(seed: int = 0) -> dict:
    key = jax.random.key(seed)
    ks = jax.random.split(key, 24)
    L = DEPTH_2

    def nrm(k, shape, s):
        return jax.random.normal(k, shape, F32) * s

    return {
        "x": nrm(ks[0], (BATCH, SEQ, D_MODEL), 1.0),
        "c": nrm(ks[1], (BATCH, D_MODEL), 1.0),
        "w_ada": nrm(ks[2], (L, D_MODEL, 6 * D_MODEL), 0.5 * D_MODEL ** -0.5),
        "b_ada": nrm(ks[3], (L, 6 * D_MODEL), 0.01),
        "g_norm_mix": 1.0 + nrm(ks[4], (L, D_MODEL), 0.02),
        "g_norm_ffn": 1.0 + nrm(ks[5], (L, D_MODEL), 0.02),
        "g_norm_final": 1.0 + nrm(ks[6], (D_MODEL,), 0.02),
        "w_in": nrm(ks[7], (L, D_MODEL, IN_WIDTH), D_MODEL ** -0.5),
        "cmp_pe_k": nrm(ks[8], (L, CMP_LEN, NSA_HEAD_DIM), 0.1),
        "cmp_pe_v": nrm(ks[9], (L, CMP_LEN, NSA_HEAD_DIM), 0.1),
        "cmp_k_w1": nrm(ks[10], (L, CMP_LEN * NSA_HEAD_DIM, CMP_HIDDEN), (CMP_LEN * NSA_HEAD_DIM) ** -0.5),
        "cmp_k_w2": nrm(ks[11], (L, CMP_HIDDEN, NSA_HEAD_DIM), CMP_HIDDEN ** -0.5),
        "cmp_v_w1": nrm(ks[12], (L, CMP_LEN * NSA_HEAD_DIM, CMP_HIDDEN), (CMP_LEN * NSA_HEAD_DIM) ** -0.5),
        "cmp_v_w2": nrm(ks[13], (L, CMP_HIDDEN, NSA_HEAD_DIM), CMP_HIDDEN ** -0.5),
        "g_nsa_out": 1.0 + nrm(ks[14], (L, NSA_HEADS, NSA_HEAD_DIM), 0.02),
        "g_ret_out": 1.0 + nrm(ks[15], (L, RET_HEADS, RET_V_DIM), 0.02),
        "w_out": nrm(ks[16], (L, MIX_WIDTH, D_MODEL), MIX_WIDTH ** -0.5),
        "peer_w_q": nrm(ks[17], (L, D_MODEL, PEER_HEADS * PEER_QUERY_DIM), D_MODEL ** -0.5),
        "peer_sub_keys": nrm(ks[18], (L, PEER_HEADS, 2, PEER_N_KEYS, PEER_QUERY_DIM // 2), (PEER_QUERY_DIM // 2) ** -0.5),
        "peer_u": nrm(ks[19], (L, PEER_EXPERTS, D_MODEL), D_MODEL ** -0.5),
        "peer_v": nrm(ks[20], (L, PEER_EXPERTS, D_MODEL), 0.25),
    }

def second_block(x, c, w_ada, b_ada, g_norm_mix, g_norm_ffn, g_norm_final, w_in, cmp_pe_k, cmp_pe_v,
              cmp_k_w1, cmp_k_w2, cmp_v_w1, cmp_v_w2, g_nsa_out, g_ret_out, w_out,
              peer_w_q, peer_sub_keys, peer_u, peer_v):
    B, S, D = x.shape
    c_act = jax.nn.silu(c)
    for l in range(DEPTH_2):
        mod = (c_act @ w_ada[l] + b_ada[l]).reshape(B, 6, 1, D)
        shift1, scale1, gate1, shift2, scale2, gate2 = jnp.moveaxis(mod, 1, 0)
        h = rmsnorm(x, g_norm_mix[l]) * (1.0 + scale1) + shift1
        q_a, k_c, v_c, k_s, v_s, k_w, v_w, g_a, q_r, k_r, v_r, g_r = split_cols(h @ w_in[l], IN_SIZES)
        o_nsa = nsa_attention(q_a.reshape(B, S, NSA_HEADS, NSA_HEAD_DIM),
                              k_c.reshape(B, S, NSA_KV_HEADS, NSA_HEAD_DIM), v_c.reshape(B, S, NSA_KV_HEADS, NSA_HEAD_DIM),
                              k_s.reshape(B, S, NSA_KV_HEADS, NSA_HEAD_DIM), v_s.reshape(B, S, NSA_KV_HEADS, NSA_HEAD_DIM),
                              k_w.reshape(B, S, NSA_KV_HEADS, NSA_HEAD_DIM), v_w.reshape(B, S, NSA_KV_HEADS, NSA_HEAD_DIM),
                              g_a, cmp_pe_k[l], cmp_pe_v[l], cmp_k_w1[l], cmp_k_w2[l], cmp_v_w1[l], cmp_v_w2[l])
        o_nsa = rmsnorm(o_nsa, g_nsa_out[l]).reshape(B, S, NSA_WIDTH)
        o_ret = retention(q_r.reshape(B, S, RET_HEADS, RET_QK_DIM), k_r.reshape(B, S, RET_HEADS, RET_QK_DIM),
                          v_r.reshape(B, S, RET_HEADS, RET_V_DIM), g_r, g_ret_out[l])
        x = x + gate1 * (jnp.concatenate([o_nsa, o_ret], axis=-1) @ w_out[l])
        h2 = rmsnorm(x, g_norm_ffn[l]) * (1.0 + scale2) + shift2
        x = x + gate2 * peer_ffn(h2, peer_w_q[l], peer_sub_keys[l], peer_u[l], peer_v[l])
    return rmsnorm(x, g_norm_final)


def setup_inputs(seed=0):
    out = dict(first_inputs(seed))
    for name, value in second_inputs(seed + 1).items():
        if name != "x":
            out[name + "_2"] = value
    return out


def reference(
    x, norm_pre, norm_post, w_in, a_q_norm, a_k_norm, b_q_norm, b_kv_norm, b_w_uq, b_w_ukv,
    c_rpb, w_out, c_2, w_ada_2, b_ada_2, g_norm_mix_2, g_norm_ffn_2, g_norm_final_2, w_in_2,
    cmp_pe_k_2, cmp_pe_v_2, cmp_k_w1_2, cmp_k_w2_2, cmp_v_w1_2, cmp_v_w2_2, g_nsa_out_2,
    g_ret_out_2, w_out_2, peer_w_q_2, peer_sub_keys_2, peer_u_2, peer_v_2,
):
    x = first_block(
        x, norm_pre, norm_post, w_in, a_q_norm, a_k_norm, b_q_norm, b_kv_norm, b_w_uq, b_w_ukv,
        c_rpb, w_out,
    )
    return second_block(
        x, c_2, w_ada_2, b_ada_2, g_norm_mix_2, g_norm_ffn_2, g_norm_final_2, w_in_2,
        cmp_pe_k_2, cmp_pe_v_2, cmp_k_w1_2, cmp_k_w2_2, cmp_v_w1_2, cmp_v_w2_2, g_nsa_out_2,
        g_ret_out_2, w_out_2, peer_w_q_2, peer_sub_keys_2, peer_u_2, peer_v_2,
    )


_drawn_inputs = setup_inputs


def setup_inputs(seed=0):
    import zlib

    import numpy as np

    out = dict(_drawn_inputs(seed))
    spreads = {}
    factors = {'b_q_norm': 2.673,
     'b_ada_2': 7.85,
     'g_norm_mix_2': 8.0,
     'g_norm_ffn_2': 26.553,
     'g_norm_final_2': 8.058,
     'cmp_pe_k_2': 8.0,
     'cmp_pe_v_2': 43.693,
     'cmp_k_w1_2': 3.299,
     'cmp_k_w2_2': 3.147,
     'g_nsa_out_2': 64.0,
     'g_ret_out_2': 8.0,
     'peer_u_2': 2.669}
    for name, (base, spread) in spreads.items():
        noise = np.random.default_rng([zlib.crc32(name.encode()), seed]).standard_normal(out[name].shape)
        drawn = base * np.exp(spread * noise) if base else spread * noise
        out[name] = __import__('jax').numpy.asarray(drawn.astype(out[name].dtype))
    for name, factor in factors.items():
        out[name] = (out[name] * factor).astype(out[name].dtype)
    return out
```

```python
from contextlib import ExitStack

import numpy as np
import concourse.bass as bass
from concourse import mybir

P = 128
F32 = mybir.dt.float32
U32 = mybir.dt.uint32
ALU = mybir.AluOpType
ACT = mybir.ActivationFunctionType
AX = mybir.AxisListType.X

SEQ, DM = 256, 2048
T = SEQ // P
KD = DM // P
LAYERS = 2
HD = 128
GRID = 64
EPS = 1e-6
MASKED = -1e30
NSA_HEADS, NSA_GROUPS, NSA_D = 16, 4, 64
CMP_LEN, CMP_STRIDE = 32, 16
NCMP = (SEQ - CMP_LEN) // CMP_STRIDE + 1
RET_HEADS = 8
PEER_HEADS, KEYS, TOPK = 8, 128, 16
PAIRS = PEER_HEADS * TOPK
MODS = 6

R = 4
UNIT = 2048
TM_G, FM_G, LAT_G, WO_G = 6, 6, 1, 4
LAYER_G = TM_G + FM_G + LAT_G + WO_G
TM2_G, GATE_G, FM2_G, CMP_G, WQ_G, SK_G = 3, 1, 10, 1, 4, 1
G_TM2 = LAYERS * LAYER_G
G_GATE = G_TM2 + TM2_G
G_FM2 = G_GATE + GATE_G
G_CMP = G_FM2 + FM2_G
G_WO2 = G_CMP + CMP_G
G_WQ = G_WO2 + WO_G
G_SK = G_WQ + WQ_G
G_U = G_SK + SK_G
U_G = KEYS // R
G_V = G_U + U_G
GROUPS = G_V + U_G

ADA_CG = MODS * DM // 512
ADA_PER_LAYER = ADA_CG // LAYERS
ADA_H = KD // 2
ADA_UNIT = 2 * 512

A_Q, A_K, A_V, B_CQ, C_V, B_CKV, B_KR, TM_W = 0, 1024, 1280, 1536, 2048, 2560, 2816, 3072
QK_HEADS = 10
GATE_CHUNKS = 16
C_Q, C_K, FM_C = 16, 20, 24
V_S, V_W, V_R, TM2_W = 0, 256, 512, 1536
NQ, KC, VC, KS, KW, RQ, RK, RG, FM2_C = 0, 8, 10, 12, 14, 16, 24, 32, 40
NGATE = 3 * NSA_HEADS

SMALL = {}
_at = 0
for _name, _n in (("ident", P), ("one", 1), ("pow", 32), ("g_pre", 4 * KD), ("b_qn", 2 * 4), ("b_kvn", 2 * 2),
                  ("g_nsa", 8), ("g_ret", 8), ("cond", KD), ("b_ada", MODS * KD), ("iota", P),
                  ("row_ok", T), ("w2k", P), ("w2v", NSA_D), ("pe", 2 * CMP_LEN)):
    SMALL[_name] = (_at, _n)
    _at += _n
SMALL_W = _at
CONST1 = {}
_at = 0
for _name, _n in (("cos", T * 128), ("sin", T * 128), ("cos_b", T * 64), ("sin_b", T * 64),
                  ("g_qk", LAYERS * 2 * 128), ("nbr", SEQ)):
    CONST1[_name] = (_at, _n)
    _at += _n
CONST1_W = _at
CONST2 = {}
_at = 0
for _name, _n in (("dist", 3 * P), ("cmp_bias", NSA_HEADS * T * NCMP), ("decay", RET_HEADS * 3 * P)):
    CONST2[_name] = (_at, _n)
    _at += _n
CONST2_W = _at

SLOPES = np.exp2(-8.0 * (np.arange(NSA_HEADS, dtype=np.float32) + 1.0) / NSA_HEADS).astype(np.float32)


def nsa_chunk(h):
    g, r = h // 4, h % 4
    return (g // 2) * 4 + r, g % 2


class Steps:

    def __init__(self, eng, sem):
        self.eng, self.sem, self.base, self.n = eng, sem, 0, 0

    def region(self, base):
        self.base, self.n = base, 0

    def __call__(self, ins):
        ins.then_inc(self.sem, 1)
        self.n += 1

    def done(self):
        self.eng.wait_ge(self.sem, self.base + self.n)


DVE_STEPS, POOL_STEPS = 52, 5


def block(nc, stream, ada, small, const1, const2, nbr_bias, g_post, g_final, x, out):
    ctx = ExitStack()

    def sb(name, shape, dt=F32):
        return ctx.enter_context(nc.sbuf_tensor(name, shape, dt))

    def sem(name):
        return ctx.enter_context(nc.semaphore(name))

    with ctx:
        X = sb("X", [P, T, DM])
        hbuf = sb("hbuf", [P, KD * SEQ])
        ring = sb("ring", [P, R, UNIT])
        aring = sb("aring", [P, 2, ADA_UNIT])
        SM = sb("SM", [P, SMALL_W])
        mod = sb("mod", [P, MODS * KD])
        csilu = sb("csilu", [P, KD])
        gsc = sb("gsc", [P, 2, KD])
        stat = sb("stat", [P, 384])
        BIG = sb("BIG", [P, KEYS * SEQ])
        ps = ctx.enter_context(nc.psum_tensor("ps", [P, 8, 512], F32))

        def area(at, *dims, buf=BIG):
            n = int(np.prod(dims))
            v = buf[:, at:at + n]
            if len(dims) == 1:
                return v
            names = "abcd"[:len(dims)]
            spec = "p (" + " ".join(names) + ") -> p " + " ".join(names)
            return v.rearrange(spec, **dict(zip(names, dims)))

        def small_of(name, *dims):
            at, n = SMALL[name]
            return area(at, *(dims or (n,)), buf=SM)

        hT = area(0, KD, SEQ, buf=hbuf)
        ident, one, power = small_of("ident"), small_of("one"), small_of("pow")
        g_pre = small_of("g_pre", 4, KD)
        g_cq, g_ckv = small_of("b_qn", 2, 4), small_of("b_kvn", 2, 2)

        Xn = area(0, T, DM)
        Y = area(0, T, DM)
        PT = area(0, T, TM_W)
        PF = area(6144, FM_C, SEQ)
        acc = area(6144, ADA_PER_LAYER, 512)
        OT = area(12288, KD, SEQ)
        rot1, rot2 = area(12288, QK_HEADS, HD), area(12288 + 1280, QK_HEADS, HD)
        junk = area(12288 + 2560, 512)
        krot = area(12288 + 3072, 2, T, 64)
        nbias = area(16384, 4, T, SEQ)
        C1 = 18432
        gpost = area(C1 + CONST1_W, DM)
        qkT = area(23552, QK_HEADS, SEQ)
        cqT, ckvT = area(26112, 4, SEQ), area(27136, 2, SEQ)
        qnT, qpT = area(27648, 4, SEQ), area(28672, 4, SEQ)
        knT, kpT = area(29696, 4, SEQ), area(30720, SEQ)
        vB = area(30976, T, 512)
        qpe = area(22016, T, 4, 64)
        qpe2 = area(22016 + 512, T, 4, 64)
        prob = area(0, 4, T, SEQ, buf=hbuf)
        probT = area(2048, 4, T, SEQ, buf=hbuf)

        def c1(name, *dims):
            at, n = CONST1[name]
            return area(C1 + at, *(dims or (n,)))

        PT2 = area(0, T, TM2_W)
        PF2 = area(4096, FM2_C, SEQ)
        OT2 = area(14336, KD, SEQ)
        C2 = 18432
        kz = area(22368, 2, 4, SEQ)
        cmp_in = [area(24416, 4, CMP_LEN, NCMP), area(24416 + 1920, 4, CMP_LEN, NCMP)]
        kcz = area(28256, 4, 16)
        hid = area(28320, 2, 64)
        vcmp = area(28448, 4, NSA_D)
        onsa = area(28704, T * NSA_HEADS, NSA_D)
        yret = area(24416, T * RET_HEADS, HD)
        square = area(22368, 2048)
        nprobT = area(30752, 4, 3 * P)
        cprob = area(30752, T * NSA_HEADS, NCMP)
        cprobT = area(0, T * NSA_HEADS, P, buf=hbuf)
        nprob = [area(0, 4, 3 * P, buf=hbuf), area(1536, 4, 3 * P, buf=hbuf)]
        ntmp = area(3072, T, 4, NSA_D, buf=hbuf)

        def c2(name, *dims):
            at, n = CONST2[name]
            return area(C2 + at, *(dims or (n,)))

        act_e = area(0, KEYS, SEQ)
        qP = area(28672, 16, SEQ)
        RT = 16384
        score = area(RT, T, 16, KEYS)
        cand = area(RT + 4096, PEER_HEADS, TOPK, TOPK)
        match = area(RT + 6144, PEER_HEADS, TOPK, TOPK)
        half_v = area(RT + 8192, 16, TOPK)
        half_i = area(RT + 8448, 16, TOPK).bitcast(U32)
        half_f = area(RT + 8704, 16, TOPK)
        top_v = area(RT + 8960, PEER_HEADS, TOPK)
        pick = area(RT + 9088, PEER_HEADS, TOPK).bitcast(U32)
        pick_i = area(RT + 9216, PEER_HEADS, TOPK).bitcast(U32)
        pick_j = area(RT + 9344, PEER_HEADS, TOPK).bitcast(U32)
        pick_fi = area(RT + 9472, PEER_HEADS, TOPK)
        pick_fj = area(RT + 9600, PEER_HEADS, TOPK)
        route = area(0, 3, T, PAIRS, buf=aring[:, :, :].rearrange("p a b -> p (a b)"))
        routeT = area(768, 3, SEQ, buf=aring[:, :, :].rearrange("p a b -> p (a b)"))
        hot1 = area(0, 2, 4, KEYS, buf=hbuf)
        hot2 = area(1024, 2, 4, KEYS, buf=hbuf)
        stage = area(2048, R, SEQ, buf=hbuf)
        gate2row = area(0, DM, buf=hbuf)
        gfin = area(0, DM, buf=aring[:, :, :].rearrange("p a b -> p (a b)"))
        ysum = area(0, T, DM)
        squares = area(4096, T, DM)

        ss2, rstd2 = stat[:, 0:2], stat[:, 2:4]
        ssq, msq, rsq = stat[:, 4:28], stat[:, 28:52], stat[:, 52:76]
        mx, nb = area(76, 2, 8, buf=stat), area(92, 2, 8, buf=stat)
        rs, rinv = area(108, 2, 8, buf=stat), area(124, 2, 8, buf=stat)
        ms2 = stat[:, 140:142]
        gw = area(144, T, NGATE, buf=stat)
        cmx, crs = stat[:, 240:272], stat[:, 272:304]
        cw = stat[:, 304:336]
        hs = stat[:, 336:368]
        hcol = area(368, 2, 4, buf=stat)
        gcol, glat = gsc[:, 0, :], gsc[:, 1, 0:6]
        w_ready = [sem(f"w_ready{s}") for s in range(R)]
        unit_done = sem("unit_done")
        a_ready = [sem(f"a_ready{s}") for s in range(2)]
        a_used = sem("a_used")
        a_step = sem("a_step")
        loaded = sem("loaded")
        c1_ready, bias_ready, gpost_ready = sem("c1_ready"), sem("bias_ready"), sem("gpost_ready")
        bias_masked = sem("bias_masked")
        c_ready = sem("c_ready")
        x_done = sem("x_done")
        tm_free, fm_free = sem("tm_free"), sem("fm_free")
        sq_done, prs_done, xn_done = sem("sq_done"), sem("prs_done"), sem("xn_done")
        ht_full, ht_done = sem("ht_full"), sem("ht_done")
        mod_full, mod_done = sem("mod_full"), sem("mod_done")
        dve_step, pool_step, act_step = sem("dve_step"), sem("pool_step"), sem("act_step")
        qss_done, qrs_done = sem("qss_done"), sem("qrs_done")
        qk_ready, tr_full, tr_done = sem("qk_ready"), sem("tr_full"), sem("tr_done")
        lat_done, qpe_ready, kpe_full, kpe_done = sem("lat_done"), sem("qpe_ready"), sem("kpe_full"), sem("kpe_done")
        qpt_full, qpt_done = sem("qpt_full"), sem("qpt_done")
        s_full, nb_done, exp_done, p_ready = sem("s_full"), sem("nb_done"), sem("exp_done"), sem("p_ready")
        t_full, pt_done, pv_full, o_done = sem("t_full"), sem("pt_done"), sem("pv_full"), sem("o_done")
        s_masked = sem("s_masked")
        ysq_done, yrs_done = sem("ysq_done"), sem("yrs_done")
        pe_passed, pool_passed = sem("pe_passed"), sem("pool_passed")
        c2_ready, zeroed, gates_full, gw_done = sem("c2_ready"), sem("zeroed"), sem("gates_full"), sem("gw_done")
        gsc_done, kz_done, cin_done = sem("gsc_done"), sem("kz_done"), sem("cin_done")
        hid_done, kc_full, kc_done, vc_done = sem("hid_done"), sem("kc_full"), sem("kc_done"), sem("vc_done")
        cs_full, cs_done, ce_done, ct_full, ct_done = sem("cs_full"), sem("cs_done"), sem("ce_done"), sem("ct_full"), sem("ct_done")
        cpv_full, co_done = sem("cpv_full"), sem("co_done")
        n_full, n_nb, n_exp, n_t = sem("n_full"), sem("n_nb"), sem("n_exp"), sem("n_t")
        n_pt, n_pv, n_out = sem("n_pt"), sem("n_pv"), sem("n_out")
        r_ready, yret_done = sem("r_ready"), sem("yret_done")
        nss_done, nrs_done, n_normed, ot_full, ot_done = (sem("nss_done"), sem("nrs_done"), sem("n_normed"),
                                                          sem("ot_full"), sem("ot_done"))
        g1_full = sem("g1_full")
        sc_full, sc_done, routed, rexp_in, rexp_done = sem("sc_full"), sem("sc_done"), sem("routed"), sem("rexp_in"), sem("rexp_done")
        rt_full, rt_done = sem("rt_full"), sem("rt_done")
        hot1_done, hot2_done, g_full, g_used = sem("hot1_done"), sem("hot2_done"), sem("g_full"), sem("g_used")
        staged, hcol_done = sem("staged"), sem("hcol_done")
        g2_full, g2_done, y_full = sem("g2_full"), sem("g2_done"), sem("y_full")
        gfin_ready = sem("gfin_ready")
        frs_done, fss_done, out_done = sem("frs_done"), sem("fss_done"), sem("out_done")
        fin_ready = sem("fin_ready")

        TM_N = TM_G + WO_G
        N_TM2 = LAYERS * TM_N
        N_WO2 = N_TM2 + TM2_G
        N_FM = LAYERS * FM_G * R
        N_WQ = N_FM + FM2_G * R
        N_U = N_WQ + WQ_G * R

        blk = ctx.enter_context(nc.Block())

        @blk.sync
        def _(sp):
            sp.dma_start(SM[:, :], small).then_inc(loaded, 16)
            sp.dma_start(X[:, :, :], x.rearrange("b (t p) d -> p (b t) d", p=P)).then_inc(loaded, 16)
            for s in range(R):
                sp.dma_start(ring[:, s, :], stream[s]).then_inc(w_ready[s], 16)
            with sp.Fori(1, GROUPS) as g:
                for s in range(R):
                    sp.wait_ge(unit_done, g * R + (s + 1 - R))
                    sp.dma_start(ring[:, s, :], stream[g * R + s]).then_inc(w_ready[s], 16)
            sp.wait_ge(g_full, SEQ // 4)
            sp.dma_start(gfin, g_final).then_inc(gfin_ready, 16)
            for t in range(T):
                sp.wait_ge(fin_ready, t + 1)
                sp.dma_start(out[0, t * P:(t + 1) * P, :], X[:, t, :]).then_inc(out_done, 16)
            sp.wait_ge(out_done, 16 * T)

        @blk.tensor
        def _(pe):
            mm = pe.matmul

            def unit(g, s):
                pe.wait_ge(w_ready[s], 16 * (g + 1))

            def settle():
                pe.sem_inc(pe_passed, 1)

            def rows_group(lhs, g, n, pair):
                pe.wait_ge(tm_free, n + 1)
                for s in range(R):
                    unit(g, s)
                    for t in range(T):
                        for kk in range(4):
                            last = mm(ps[:, 2 * pair + t, :], lhs[:, 4 * s + kk, t * P:(t + 1) * P],
                                      ring[:, s, kk * 512:(kk + 1) * 512],
                                      start=(s == 0 and kk == 0), stop=(s == R - 1 and kk == 3))
                    last.then_inc(unit_done, 1)

            def cols_group(g, n, rhs):
                for c in range(R):
                    pe.wait_ge(fm_free, n + c + 1)
                    unit(g, c)
                    for k in range(KD):
                        last = mm(ps[:, 4 + c, 0:SEQ], ring[:, c, k * P:(k + 1) * P], rhs[:, k, :],
                                  start=(k == 0), stop=(k == KD - 1))
                    last.then_inc(unit_done, 1)

            def prenorm(i):
                pe.wait_ge(xn_done, T * (i + 1))
                for b in range(8):
                    for kk in range(2):
                        k = 2 * b + kk
                        for t in range(T):
                            last = pe.transpose(ps[:, b, kk * SEQ + t * P:kk * SEQ + (t + 1) * P],
                                                Xn[:, t, k * P:(k + 1) * P], ident)
                    last.then_inc(ht_full, 1)
                pe.wait_ge(ht_done, KD * (i + 1))
                settle()

            pe.wait_ge(loaded, 32)
            with pe.Fori(0, LAYERS) as l:
                prenorm(l)
                with pe.Fori(0, TM_G // 2) as i:
                    for p in range(2):
                        rows_group(hT, l * LAYER_G + i * 2 + p, l * TM_N + i * 2 + p, p)
                pe.wait_ge(a_used, (l + 1) * (ADA_PER_LAYER * ADA_H) + 2)
                for i in range(ADA_PER_LAYER):
                    for j in range(4):
                        last = mm(ps[:, 4, 4 * i + j:4 * i + j + 1], acc[:, i, j * P:(j + 1) * P], one,
                                  start=True, stop=True)
                last.then_inc(mod_full, 1)
                pe.wait_ge(mod_done, l + 1)
                settle()
                with pe.Fori(0, FM_G) as i:
                    cols_group(l * LAYER_G + i + TM_G, l * FM_C + i * R, hT)
                pe.wait_ge(qk_ready, 2 * (l + 1))
                pe.wait_ge(fm_free, (l + 1) * FM_C + R)
                for b in range(5):
                    for hh in range(2):
                        for t in range(T):
                            at = (2 * b + hh) * HD
                            last = pe.transpose(ps[:, b, hh * SEQ + t * P:hh * SEQ + (t + 1) * P],
                                                PT[:, t, at:at + HD], ident)
                    last.then_inc(tr_full, 1)
                for b in range(5, 8):
                    for hh in range(2):
                        k = 2 * (b - 5) + hh
                        at = B_CQ + k * P if k < 4 else B_CKV + (k - 4) * P
                        for t in range(T):
                            last = pe.transpose(ps[:, b, hh * SEQ + t * P:hh * SEQ + (t + 1) * P],
                                                PT[:, t, at:at + P], ident)
                    last.then_inc(tr_full, 1)
                pe.wait_ge(tr_done, 11 * (l + 1))
                gl = l * LAYER_G + TM_G + FM_G
                unit(gl, 0)
                for c in range(4):
                    for k in range(4):
                        last = mm(ps[:, c // 2, (c % 2) * SEQ:(c % 2 + 1) * SEQ],
                                  ring[:, 0, k * 512 + c * P:k * 512 + (c + 1) * P], cqT[:, k, :],
                                  start=(k == 0), stop=(k == 3))
                last.then_inc(unit_done, 1)
                unit(gl, 1)
                for t in range(T):
                    for k in range(4):
                        last = mm(ps[:, 4, t * 256:(t + 1) * 256], cqT[:, k, t * P:(t + 1) * P],
                                  ring[:, 1, k * 256:(k + 1) * 256], start=(k == 0), stop=(k == 3))
                last.then_inc(unit_done, 1)
                for t in range(T):
                    last = pe.transpose(ps[0:64, 7, t * P:(t + 1) * P], krot[:, 0, t, :], ident)
                last.then_inc(kpe_full, 1)
                unit(gl, 2)
                unit(gl, 3)
                for c in range(4):
                    for k in range(2):
                        last = mm(ps[:, 2 + c // 2, (c % 2) * SEQ:(c % 2 + 1) * SEQ],
                                  ring[:, 2, k * 1024 + c * P:k * 1024 + (c + 1) * P], ckvT[:, k, :],
                                  start=(k == 0), stop=(k == 1))
                for t in range(T):
                    for k in range(2):
                        last = mm(ps[:, 5 + t, :], ckvT[:, k, t * P:(t + 1) * P],
                                  ring[:, 2, k * 1024 + 512:(k + 1) * 1024], start=(k == 0), stop=(k == 1))
                last.then_inc(unit_done, 2)
                pe.wait_ge(qpe_ready, l + 1)
                pe.wait_ge(lat_done, 3 * (l + 1))
                settle()
                for h in range(4):
                    for t in range(T):
                        last = pe.transpose(ps[0:64, h // 2, (h % 2) * SEQ + t * P:(h % 2) * SEQ + (t + 1) * P],
                                            qpe[:, t, h, :], ident)
                last.then_inc(qpt_full, 1)
                pe.wait_ge(qpt_done, l + 1)
                pe.wait_ge(kpe_done, l + 1)

                def scores(i):
                    for h in range(4):
                        for t in range(T):
                            o = ps[:, h, t * SEQ:(t + 1) * SEQ]
                            q = slice(t * P, (t + 1) * P)
                            if i < 2:
                                last = mm(o, qkT[:, 4 * i + h, q], qkT[:, 8 + i, :], start=True, stop=True)
                            elif i == 2:
                                mm(o, qnT[:, h, q], knT[:, h, :], start=True, stop=False)
                                last = mm(o, qpT[0:64, h, q], kpT[0:64, :], start=False, stop=True)
                            else:
                                last = mm(o, PF[:, C_Q + h, q], PF[:, C_K + h, :], start=True, stop=True)
                    last.then_inc(s_full, 1)

                scores(0)
                for i in range(4):
                    pe.wait_ge(p_ready, 4 * l + (i + 1))
                    for h in range(4):
                        for kt in range(T):
                            for t in range(T):
                                last = pe.transpose(ps[:, 4 + h, kt * SEQ + t * P:kt * SEQ + (t + 1) * P],
                                                    prob[:, h, t, kt * P:(kt + 1) * P], ident)
                    last.then_inc(t_full, 1)
                    if i < 3:
                        scores(i + 1)
                    pe.wait_ge(pt_done, 8 * l + 2 * (i + 1))
                    for h in range(4):
                        for kt in range(T):
                            v = (PT[:, kt, A_V + i * HD:A_V + (i + 1) * HD] if i < 2 else
                                 vB[:, kt, h * HD:(h + 1) * HD] if i == 2 else
                                 PT[:, kt, C_V + h * HD:C_V + (h + 1) * HD])
                            last = mm(ps[:, 4 + h // 2, (h % 2) * SEQ:(h % 2 + 1) * SEQ], v, probT[:, h, kt, :],
                                      start=(kt == 0), stop=(kt == 1))
                    last.then_inc(pv_full, 1)
                    pe.wait_ge(o_done, 4 * l + (i + 1))
                settle()
                with pe.Fori(0, WO_G // 2) as i:
                    for p in range(2):
                        rows_group(OT, l * LAYER_G + i * 2 + (TM_G + FM_G + LAT_G + p),
                                   l * TM_N + i * 2 + (TM_G + p), p)

            prenorm(LAYERS)
            for i in range(TM2_G):
                rows_group(hT, G_TM2 + i, N_TM2 + i, i % 2)
            for s in range(R):
                unit(G_GATE, s)
            for t in range(T):
                for k in range(KD):
                    last = mm(ps[:, 4, t * NGATE:(t + 1) * NGATE], hT[:, k, t * P:(t + 1) * P],
                              ring[:, 0, k * NGATE:(k + 1) * NGATE], start=(k == 0), stop=(k == KD - 1))
            last.then_inc(unit_done, 4)
            pe.wait_ge(gw_done, 1)
            with pe.Fori(0, FM2_G) as i:
                cols_group(i + G_FM2, i * R + N_FM, hT)
            pe.wait_ge(fm_free, N_WQ + R)
            for w in range(2):
                pe.wait_ge(cin_done, w + 1)
                for u in range(2):
                    unit(G_CMP, 2 * w + u)
                    for j in range(16):
                        last = mm(ps[:, 4 + 3 * w, 0:4 * NCMP], ring[:, 2 * w + u, j * P:(j + 1) * P],
                                  cmp_in[w][:, :, 16 * u + j, :], start=(u == 0 and j == 0), stop=(u == 1 and j == 15))
                    last.then_inc(unit_done, 1)
            pe.wait_ge(hid_done, 1)
            mm(ps[:, 5, 0:4 * NCMP], small_of("w2k"), hid[:, 0, 0:4 * NCMP], start=True, stop=True).then_inc(kc_full, 1)
            pe.wait_ge(hid_done, 2)
            for q in range(4):
                last = mm(ps[0:NCMP, 6, q * NSA_D:(q + 1) * NSA_D], hid[:, 1, q * NCMP:(q + 1) * NCMP],
                          small_of("w2v"), start=True, stop=True)
            last.then_inc(kc_full, 1)
            pe.wait_ge(kc_done, 2)
            pe.wait_ge(vc_done, 1)
            for t in range(T):
                for h in range(NSA_HEADS):
                    c, half = nsa_chunk(h)
                    at = (t * NSA_HEADS + h) * NCMP
                    last = mm(ps[:, 7, at:at + NCMP], PF2[:, NQ + c, t * P:(t + 1) * P],
                              kcz[:, half * 2 + h // 8, 0:NCMP], start=True, stop=True)
            last.then_inc(cs_full, 1)
            pe.wait_ge(ce_done, 1)
            for j in range(T * NSA_HEADS):
                last = pe.transpose(ps[0:NCMP, j // 4, (j % 4) * P:(j % 4 + 1) * P], cprob[:, j, :], ident)
            last.then_inc(ct_full, 1)
            pe.wait_ge(ct_done, 2)
            for j in range(T * NSA_HEADS):
                h = j % NSA_HEADS
                last = mm(ps[:, j // 8, (j % 8) * NSA_D:(j % 8 + 1) * NSA_D], cprobT[0:NCMP, j, :],
                          vcmp[0:NCMP, nsa_chunk(h)[1] * 2 + h // 8, :], start=True, stop=True)
            last.then_inc(cpv_full, 1)
            pe.wait_ge(co_done, 1)
            pe.wait_ge(kz_done, 1)

            def nscores(i):
                g, br = i // 2, i % 2
                for r in range(4):
                    c, half = nsa_chunk(4 * g + r)
                    k = kz[:, br, half * 2 + g // 2, :]
                    mm(ps[:, r, 0:P], PF2[:, NQ + c, 0:P], k[:, 0:P], start=True, stop=True)
                    last = mm(ps[:, r, P:3 * P], PF2[:, NQ + c, P:SEQ], k, start=True, stop=True)
                last.then_inc(n_full, 1)

            def rscores(i):
                for r in range(4):
                    q, k = PF2[:, RQ + 4 * i + r, :], PF2[:, RK + 4 * i + r, :]
                    mm(ps[:, r, 0:SEQ], k[:, 0:P], q, start=True, stop=True)
                    last = mm(ps[:, r, SEQ:3 * P], k[:, P:SEQ], q[:, P:SEQ], start=True, stop=True)
                last.then_inc(n_full, 1)

            nscores(0)
            for i in range(8):
                g, br = i // 2, i % 2
                pe.wait_ge(n_exp, i + 1)
                for r in range(4):
                    for j in range(3):
                        last = pe.transpose(ps[:, 4 + r, j * P:(j + 1) * P], nprob[i % 2][:, r, j * P:(j + 1) * P], ident)
                last.then_inc(n_t, 1)
                if i < 7:
                    nscores(i + 1)
                else:
                    rscores(0)
                pe.wait_ge(n_pt, 2 * (i + 1))
                v = [PT2[:, kt, (V_W if br else V_S) + g * NSA_D:(V_W if br else V_S) + (g + 1) * NSA_D] for kt in range(2)]
                for r in range(4):
                    mm(ps[:, 4, r * NSA_D:(r + 1) * NSA_D], nprobT[:, r, 0:P], v[0], start=True, stop=True)
                    o = ps[:, 4, (4 + r) * NSA_D:(5 + r) * NSA_D]
                    mm(o, nprobT[:, r, P:2 * P], v[0], start=True, stop=False)
                    last = mm(o, nprobT[:, r, 2 * P:3 * P], v[1], start=False, stop=True)
                last.then_inc(n_pv, 1)
                pe.wait_ge(n_out, i + 1)
            for i in range(2):
                pe.wait_ge(r_ready, i + 1)
                if i == 0:
                    rscores(1)
                else:
                    pe.wait_ge(yret_done, 1)
                for r in range(4):
                    h = 4 * i + r
                    v = [PT2[:, st, V_R + h * HD:V_R + (h + 1) * HD] for st in range(2)]
                    o = ps[:, 4 + r // 2, (r % 2) * SEQ:(r % 2 + 1) * SEQ]
                    a = nprob[i % 2][:, r, :]
                    mm(o[:, 0:P], a[:, 0:P], v[0], start=True, stop=True)
                    mm(o[:, P:SEQ], a[:, P:SEQ], v[0], start=True, stop=False)
                    last = mm(o[:, P:SEQ], a[:, SEQ:3 * P], v[1], start=False, stop=True)
                last.then_inc(n_pv, 1)
            for kind in range(2):
                pe.wait_ge(n_normed, kind + 1)
                if kind == 0:
                    pe.wait_ge(yret_done, 2)
                for c in range(8):
                    for t in range(T):
                        src = (onsa[:, t * NSA_HEADS + 2 * c:t * NSA_HEADS + 2 * c + 2, :].rearrange("p a b -> p (a b)")
                               if kind == 0 else yret[:, t * RET_HEADS + c, :])
                        last = pe.transpose(ps[:, 4 * kind + c // 2, (c % 2) * SEQ + t * P:(c % 2) * SEQ + (t + 1) * P],
                                            src, ident)
                    if c % 2:
                        last.then_inc(ot_full, 1)
            pe.wait_ge(ot_done, 16)
            for i in range(WO_G):
                rows_group(OT2, G_WO2 + i, N_WO2 + i, i % 2)

            def gate_row(j):
                for k in range(KD):
                    last = mm(ps[:, 4 + k // 4, (k % 4) * P:(k % 4 + 1) * P],
                              mod[:, j * KD + k:j * KD + k + 1].to_broadcast([P, P]), ident, start=True, stop=True)
                return last

            gate_row(2).then_inc(g1_full, 1)
            prenorm(LAYERS + 1)
            with pe.Fori(0, WQ_G) as i:
                cols_group(i + G_WQ, i * R + N_WQ, hT)
            pe.wait_ge(fm_free, N_U + R)
            for s in range(R):
                unit(G_SK, s)
            for t in range(T):
                for j in range(16):
                    last = mm(ps[:, 4 * t + j // 4, (j % 4) * P:(j % 4 + 1) * P], qP[:, j, t * P:(t + 1) * P],
                              ring[:, 0, j * P:(j + 1) * P], start=True, stop=True)
            last.then_inc(sc_full, 1)
            pe.wait_ge(sc_done, 2)
            pe.sem_inc(unit_done, 4)
            with pe.Fori(0, U_G) as i:
                cols_group(i + G_U, i * R + N_U, hT)
            pe.wait_ge(routed, T)
            for a in range(3):
                for t in range(T):
                    last = pe.transpose(ps[:, a, t * P:(t + 1) * P], route[:, a, t, :], ident)
            last.then_inc(rt_full, 1)
            pe.wait_ge(rt_done, 1)
            with pe.Fori(0, SEQ // 8) as i:
                for b in range(2):
                    n = i * 2 + b
                    pe.wait_ge(g_used, n + 1)
                    pe.wait_ge(hot1_done, (n + 1) * 4)
                    pe.wait_ge(hot2_done, (n + 1) * 4)
                    for j in range(4):
                        last = mm(ps[:, b, j * P:(j + 1) * P], hot1[:, b, j, :], hot2[:, b, j, :], start=True, stop=True)
                    last.then_inc(g_full, 1)
            pe.wait_ge(g_used, SEQ // 4 + 2)
            pe.wait_ge(fm_free, N_U + U_G * R + R)
            gate_row(5).then_inc(g2_full, 1)
            pe.wait_ge(g2_done, 1)

            def down(g, first, last_group):
                for c in range(R):
                    unit(g, c)
                    pe.wait_ge(staged, (g - G_V) * R + (c + 1))
                    for t in range(T):
                        for d in range(4):
                            last = mm(ps[:, 4 * t + d, :], stage[:, c, t * P:(t + 1) * P],
                                      ring[:, c, d * 512:(d + 1) * 512], start=first and c == 0,
                                      stop=last_group and c == R - 1, skip_group_check=True)
                    last.then_inc(unit_done, 1)

            down(G_V, True, False)
            with pe.Fori(G_V + 1, GROUPS - 1) as g:
                down(g, False, False)
            down(GROUPS - 1, False, True)

        @blk.scalar
        def _(act):
            def f(o, i, func, **kw):
                return nc.scalar.activation(o, i, func, **kw)

            def prenorm(i, scale, shift=None):
                act.wait_ge(x_done, T * (i + 1))
                for t in range(T):
                    f(Xn[:, t, :], X[:, t, :], ACT.Square, accum_out=ss2[:, t:t + 1]).then_inc(sq_done, 1)
                for b in range(1, 8, 2):
                    act.wait_ge(ht_full, 8 * i + (b + 1))
                    for kk in range(2):
                        k = 2 * b + kk
                        o, src = hT[:, k, :], ps[:, b, kk * SEQ:(kk + 1) * SEQ]
                        if shift is None:
                            ins = f(o, src, ACT.Copy, scale=scale(k))
                        else:
                            ins = f(o, src, ACT.Identity, scale=scale(k), bias=shift(k))
                        ins.then_inc(ht_done, 1)

            def rows_out(dst, g, col, pair):
                act.wait_ge(unit_done, g * R + R)
                f(dst[:, :, bass.ds(col, 512)], ps[:, 2 * pair:2 * pair + 2, :], ACT.Copy).then_inc(tm_free, 1)

            def cols_out(dst, g, chunk, func):
                for c in range(R):
                    act.wait_ge(unit_done, g * R + (c + 1))
                    f(dst[:, chunk + c, :], ps[:, 4 + c, 0:SEQ], func).then_inc(fm_free, 1)

            act.wait_ge(loaded, 32)
            f(csilu[:, :], small_of("cond"), ACT.Silu).then_inc(c_ready, 1)
            with act.Fori(0, LAYERS) as l:
                prenorm(l, lambda k: gcol[:, k:k + 1])
                with act.Fori(0, TM_G // 2) as i:
                    for p in range(2):
                        rows_out(PT, l * LAYER_G + i * 2 + p, i * 1024 + p * 512, p)
                with act.Fori(0, GATE_CHUNKS // R) as i:
                    cols_out(PF, l * LAYER_G + i + TM_G, i * R, ACT.Silu)
                with act.Fori(GATE_CHUNKS // R, FM_G) as i:
                    cols_out(PF, l * LAYER_G + i + TM_G, i * R, ACT.Copy)
                for b in range(0, 5, 2):
                    act.wait_ge(tr_full, 8 * l + (b + 1))
                    f(qkT[:, 2 * b:2 * b + 2, :], ps[:, b, :], ACT.Copy).then_inc(tr_done, 1)
                gl = l * LAYER_G + TM_G + FM_G
                act.wait_ge(unit_done, gl * R + 1)
                f(qnT, ps[:, 0:2, :], ACT.Copy).then_inc(lat_done, 1)
                act.wait_ge(unit_done, gl * R + 4)
                f(knT, ps[:, 2:4, :], ACT.Copy).then_inc(lat_done, 1)
                f(vB, ps[:, 5:7, :], ACT.Copy).then_inc(lat_done, 1)

                def exps(i):
                    act.wait_ge(nb_done, 4 * l + (i + 1))
                    if i:
                        act.wait_ge(t_full, 4 * l + i)
                    scale = {0: HD ** -0.5, 1: HD ** -0.5, 2: (HD + 64) ** -0.5, 3: 1.0}[i]
                    for h in range(4):
                        for t in range(T):
                            src = prob[:, h, t, :] if i == 3 else ps[:, h, t * SEQ:(t + 1) * SEQ]
                            last = f(prob[:, h, t, :], src, ACT.Exp, scale=scale,
                                     bias=nb[:, i % 2, 2 * h + t:2 * h + t + 1],
                                     accum_out=rs[:, i % 2, 2 * h + t:2 * h + t + 1])
                    last.then_inc(exp_done, 1)

                exps(0)
                for i in range(4):
                    act.wait_ge(t_full, 4 * l + (i + 1))
                    f(probT[:, 0:2], ps[:, 4:6, :], ACT.Copy).then_inc(pt_done, 1)
                    if i < 3:
                        exps(i + 1)
                with act.Fori(0, WO_G // 2) as i:
                    for p in range(2):
                        rows_out(Y, l * LAYER_G + i * 2 + (TM_G + FM_G + LAT_G + p), i * 1024 + p * 512, p)
                act.wait_ge(tm_free, (l + 1) * TM_N + 2)
                for t in range(T):
                    f(squares[:, t, :], Y[:, t, :], ACT.Square, accum_out=ss2[:, t:t + 1]).then_inc(ysq_done, 1)

            act.wait_ge(gsc_done, 1)
            prenorm(LAYERS, lambda k: gsc[:, 0, k:k + 1], lambda k: mod[:, k:k + 1])
            for i in range(TM2_G):
                rows_out(PT2, G_TM2 + i, i * 512, i % 2)
            act.wait_ge(unit_done, G_GATE * R + 4)
            f(gw, ps[:, 4, 0:T * NGATE], ACT.Sigmoid).then_inc(gw_done, 1)
            with act.Fori(0, RG // R) as i:
                cols_out(PF2, i + G_FM2, i * R, ACT.Copy)
            with act.Fori(RG // R, FM2_G) as i:
                cols_out(PF2, i + G_FM2, i * R, ACT.Silu)
            for w in range(2):
                act.wait_ge(unit_done, G_CMP * R + 2 * (w + 1))
                f(hid[:, w, 0:4 * NCMP], ps[:, 4 + 3 * w, 0:4 * NCMP], ACT.Gelu_apprx_tanh).then_inc(hid_done, 1)
            act.wait_ge(cs_done, 1)
            f(cprob, cprob, ACT.Exp).then_inc(ce_done, 1)
            act.wait_ge(ct_full, 1)
            f(cprobT[0:NCMP, 0:16, :], ps[0:NCMP, 0:4, :], ACT.Copy).then_inc(ct_done, 1)

            def nexps(i):
                act.wait_ge(n_nb, i + 1)
                for t in range(T):
                    for r in range(4):
                        p = nprob[i % 2][:, r, 0:P] if t == 0 else nprob[i % 2][:, r, P:3 * P]
                        j = 4 * t + r
                        last = f(p, p, ACT.Exp, scale=NSA_D ** -0.5, bias=nb[:, i % 2, j:j + 1],
                                 accum_out=rs[:, i % 2, j:j + 1])
                last.then_inc(n_exp, 1)

            nexps(0)
            for i in range(8):
                act.wait_ge(n_t, i + 1)
                f(nprobT[:, 0:2, :], ps[:, 4:6, 0:3 * P], ACT.Copy).then_inc(n_pt, 1)
                if i < 7:
                    nexps(i + 1)
            for i in range(2):
                act.wait_ge(n_pv, 8 + i + 1)
                src = ps[:, 4:6, :].rearrange("p b (r t e) -> p t (b r) e", r=2, t=T)
                for t in range(T):
                    last = f(yret[:, t * RET_HEADS + 4 * i:t * RET_HEADS + 4 * i + 4, :], src[:, t], ACT.Copy)
                last.then_inc(yret_done, 1)
            for c in range(8):
                act.wait_ge(ot_full, c // 2 + 1)
                f(OT2[:, c, :], ps[:, c // 2, (c % 2) * SEQ:(c % 2 + 1) * SEQ], ACT.Copy,
                  scale=small_of("g_nsa")[:, c:c + 1]).then_inc(ot_done, 1)
            for i in range(WO_G):
                rows_out(Y, G_WO2 + i, i * 512, i % 2)
            act.wait_ge(gsc_done, 2)
            prenorm(LAYERS + 1, lambda k: gsc[:, 1, k:k + 1], lambda k: mod[:, 3 * KD + k:3 * KD + k + 1])
            with act.Fori(0, WQ_G) as i:
                cols_out(qP, i + G_WQ, i * R, ACT.Copy)
            act.wait_ge(sc_full, 1)
            f(score[:, 0], ps[:, 0:4, :], ACT.Copy).then_inc(sc_done, 1)
            with act.Fori(0, U_G // 2) as i:
                cols_out(act_e, i + G_U, i * R, ACT.Gelu_apprx_tanh)
            for t in range(T):
                act.wait_ge(rexp_in, t + 1)
                f(route[:, 2, t, :], route[:, 2, t, :], ACT.Exp).then_inc(rexp_done, 1)
            act.wait_ge(routed, T)
            with act.Fori(U_G // 2, U_G) as i:
                cols_out(act_e, i + G_U, i * R, ACT.Gelu_apprx_tanh)
            act.wait_ge(g2_full, 1)
            f(gate2row, ps[:, 4:8, :], ACT.Copy).then_inc(g2_done, 1)

            def stages(g, first):
                for c in range(R):
                    if not first:
                        act.wait_ge(unit_done, g * R + (c + 1 - R))
                    f(stage[:, c, :], act_e[:, (g - G_V) * R + c, :], ACT.Copy).then_inc(staged, 1)

            stages(G_V, True)
            with act.Fori(G_V + 1, GROUPS) as g:
                stages(g, False)
            act.wait_ge(x_done, T * (LAYERS + 3))
            for t in range(T):
                f(squares[:, t, :], X[:, t, :], ACT.Square, accum_out=ss2[:, t:t + 1]).then_inc(fss_done, 1)

        @blk.gpsimd
        def _(pool):
            steps = Steps(pool, pool_step)
            pl = nc.gpsimd

            def rsqrt(parts, mean, out_ap, signal):
                pool.sem_inc(pool_passed, 1)
                for o, src, n in parts:
                    steps(pl.tensor_scalar(o, src, 1.0 / n, EPS, ALU.mult, ALU.add))
                steps.done()
                pl.tensor_tensor(out_ap, mean, power[:, 0:mean.shape[-1]], ALU.pow).then_inc(signal, 1)

            def rstd_of(i, wait_sem, signal):
                pool.wait_ge(wait_sem, T * (i + 1))
                rsqrt([(ms2, ss2, DM)], ms2, rstd2, signal)

            pool.dma_start(area(C1, CONST1_W), const1).then_inc(c1_ready, 16)
            pool.wait_ge(loaded, 32)
            with pool.Fori(0, LAYERS) as l:
                steps.region(l * POOL_STEPS)
                pool.wait_ge(x_done, T * (l + 1))
                pool.dma_start(nbias, nbr_bias[l]).then_inc(bias_ready, 16)
                pool.dma_start(gpost, g_post[l]).then_inc(gpost_ready, 16)
                rstd_of(l, sq_done, prs_done)
                with pool.Fori(0, ADA_PER_LAYER) as i:
                    for h in range(ADA_H):
                        cg = l * ADA_PER_LAYER + i
                        pool.wait_ge(a_used, cg * ADA_H + (h + 1))
                        pool.dma_start(aring[:, h % 2, :], ada[cg, h]).then_inc(a_ready[h % 2], 16)
                pool.wait_ge(bias_ready, 16 * l + 16)
                pool.wait_ge(c1_ready, 16)
                nb8 = nbias.rearrange("p a b c -> p (a b) c")
                pl.tensor_tensor(nb8, nb8, c1("nbr")[:, None, :].to_broadcast([P, 8, SEQ]), ALU.add).then_inc(bias_masked, 1)
                pool.wait_ge(qss_done, l + 1)
                rsqrt([(msq[:, 0:20], ssq[:, 0:20], HD), (msq[:, 20:22], ssq[:, 20:22], 512),
                       (msq[:, 22:24], ssq[:, 22:24], 256)], msq, rsq, qrs_done)
                rstd_of(l, ysq_done, yrs_done)
                assert steps.n == POOL_STEPS, steps.n
            steps.region(LAYERS * POOL_STEPS)
            pool.wait_ge(x_done, T * (LAYERS + 1))
            pool.dma_start(area(C2, CONST2_W), const2).then_inc(c2_ready, 16)
            pl.memset(area(22368, 2048 + 3840 + 64), 0.0).then_inc(zeroed, 1)
            rstd_of(LAYERS, sq_done, prs_done)
            pool.wait_ge(nss_done, 1)
            rsqrt([(hs, hs, NSA_D)], hs, cw, nrs_done)
            pool.wait_ge(nss_done, 2)
            rsqrt([(hs[:, 0:16], hs[:, 0:16], HD)], hs[:, 0:16], cw[:, 0:16], nrs_done)
            rstd_of(LAYERS + 1, sq_done, prs_done)
            pool.wait_ge(rt_done, 1)
            with pool.Fori(0, SEQ // 8) as i:
                for b in range(2):
                    n = i * 2 + b
                    pool.wait_ge(g_used, n + 1)
                    pl.tensor_copy(hcol[:, b, :], routeT[:, 1, bass.ds(i * 8 + 4 * b, 4)]).then_inc(hcol_done, 1)
                    pool.wait_ge(hcol_done, n + 1)
                    pool.sem_inc(pool_passed, 1)
                    for j in range(4):
                        pl.tensor_scalar(hot2[:, b, j, :], small_of("iota"), hcol[:, b, j:j + 1], None,
                                         ALU.is_equal).then_inc(hot2_done, 1)
            pool.wait_ge(fss_done, T)
            rsqrt([(ms2, ss2, DM)], ms2, rstd2, frs_done)

        @blk.vector
        def _(dve):
            v = nc.vector
            st = Steps(dve, dve_step)
            tt, ts, stt = v.tensor_tensor, v.tensor_scalar, v.scalar_tensor_tensor

            def prenorm(i, scale, shift=None):
                dve.wait_ge(prs_done, i + 1)
                for t in range(T):
                    ts(Xn[:, t, :], X[:, t, :], rstd2[:, t:t + 1], None, ALU.mult).then_inc(xn_done, 1)
                for b in range(0, 8, 2):
                    dve.wait_ge(ht_full, 8 * i + (b + 1))
                    for kk in range(2):
                        k = 2 * b + kk
                        o, src = hT[:, k, :], ps[:, b, kk * SEQ:(kk + 1) * SEQ]
                        if shift is None:
                            ins = ts(o, src, scale(k), None, ALU.mult)
                        else:
                            ins = ts(o, src, scale(k), shift(k), ALU.mult, ALU.add)
                        ins.then_inc(ht_done, 1)

            def rotate(dst, src, tmp, cos, sin, heads, half):
                def split(a):
                    return a.rearrange("p h (a s n) -> p h a s n", a=2, s=2)
                n = cos.shape[-1]
                c3 = cos[:, None, :].to_broadcast([P, heads, n])
                s5 = sin.rearrange("p (a s n) -> p a s n", a=2, s=2)
                for s in range(2):
                    st(tt(split(tmp)[:, :, :, s, :], split(src)[:, :, :, 1 - s, :],
                          s5[:, None, :, s, :].to_broadcast([P, heads, 2, half]), ALU.mult))
                st.done()
                st(tt(dst, src, c3, ALU.mult))
                st.done()
                return tt(dst, dst, tmp, ALU.add)

            dve.wait_ge(loaded, 32)
            dve.sem_inc(tm_free, 2)
            dve.sem_inc(fm_free, 4)
            dve.sem_inc(a_used, 2)
            dve.sem_inc(x_done, 2)
            dve.sem_inc(g_used, 2)
            dve.wait_ge(c_ready, 1)
            dve.wait_ge(c1_ready, 16)
            with dve.Fori(0, LAYERS) as l:
                st.region(l * DVE_STEPS)
                st(v.tensor_copy(gcol, g_pre[:, l, :]))
                st(v.tensor_copy(glat[:, 0:4], g_cq[:, l, :]))
                st(v.tensor_copy(glat[:, 4:6], g_ckv[:, l, :]))
                st.done()
                prenorm(l, lambda k: gcol[:, k:k + 1])

                with dve.Fori(0, ADA_PER_LAYER) as i:
                    for h in range(ADA_H):
                        cg = l * ADA_PER_LAYER + i
                        dve.wait_ge(a_ready[h % 2], cg * 64 + 16 * (h // 2 + 1))
                        for kk in range(2):
                            w = aring[:, h % 2, kk * 512:(kk + 1) * 512]
                            k = 2 * h + kk
                            if k == 0:
                                ins = ts(acc[:, i, :], w, csilu[:, k:k + 1], None, ALU.mult)
                            else:
                                if kk:
                                    dve.wait_ge(a_step, cg * ADA_H + (h + 1))
                                else:
                                    dve.wait_ge(a_used, cg * ADA_H + (h + 2))
                                ins = stt(acc[:, i, :], w, csilu[:, k:k + 1], acc[:, i, :], ALU.mult, ALU.add)
                            ins.then_inc(a_used if kk else a_step, 1)
                dve.wait_ge(mod_full, l + 1)
                tt(mod[:, bass.ds(l * 48, 48)], ps[:, 4, 0:48], small_of("b_ada")[:, bass.ds(l * 48, 48)],
                   ALU.add).then_inc(mod_done, 1)

                dve.wait_ge(tm_free, l * TM_N + (TM_G + 2))
                for t, sq in ((0, rot1), (1, rot2)):
                    qk = PT[:, t, 0:QK_HEADS * HD].rearrange("p (h d) -> p h d", d=HD)
                    st(tt(sq, qk, qk, ALU.mult))
                    cq, ckv = PT[:, t, B_CQ:B_CQ + 512], PT[:, t, B_CKV:B_CKV + 256]
                    st(stt(junk, cq, 1.0, cq, ALU.mult, ALU.mult, accum_out=ssq[:, 20 + t:21 + t]))
                    st.done()
                    st(stt(junk[:, 0:256], ckv, 1.0, ckv, ALU.mult, ALU.mult, accum_out=ssq[:, 22 + t:23 + t]))
                    st(v.tensor_reduce(ssq[:, 10 * t:10 * t + 10], sq, AX, ALU.add))
                    st.done()
                dve.sem_inc(qss_done, 1)
                dve.wait_ge(qrs_done, l + 1)
                for t in range(T):
                    for at, n, j in ((B_CQ, 512, 20), (B_CKV, 256, 22)):
                        st(ts(PT[:, t, at:at + n], PT[:, t, at:at + n], rsq[:, j + t:j + t + 1], None, ALU.mult))
                for t in range(T):
                    rotate(krot[:, 0, t:t + 1, :], PT[:, t:t + 1, B_KR:B_KR + 64], krot[:, 1, t:t + 1, :],
                           c1("cos_b", T, 64)[:, t, :], c1("sin_b", T, 64)[:, t, :], 1, 16).then_inc(dve_step, 1)
                    st.n += 1
                g_qk = c1("g_qk", LAYERS, 2, HD)
                for t in range(T):
                    qk = PT[:, t, 0:QK_HEADS * HD].rearrange("p (h d) -> p h d", d=HD)
                    st(tt(rot1, qk, rsq[:, 10 * t:10 * t + 10].unsqueeze(2).to_broadcast([P, QK_HEADS, HD]), ALU.mult))
                    st.done()
                    st(tt(rot1[:, 0:8], rot1[:, 0:8], g_qk[:, l, 0, :].unsqueeze(1).to_broadcast([P, 8, HD]), ALU.mult))
                    st(tt(rot1[:, 8:10], rot1[:, 8:10], g_qk[:, l, 1, :].unsqueeze(1).to_broadcast([P, 2, HD]), ALU.mult))
                    st.done()
                    rotate(qk, rot1, rot2, c1("cos", T, HD)[:, t, :], c1("sin", T, HD)[:, t, :], QK_HEADS, 32).then_inc(qk_ready, 1)
                    if t == 0:
                        dve.wait_ge(qk_ready, l * 2 + 1)
                for b in (1, 3):
                    dve.wait_ge(tr_full, 8 * l + (b + 1))
                    v.tensor_copy(qkT[:, 2 * b:2 * b + 2, :], ps[:, b, :].rearrange("p (a b) -> p a b", a=2)).then_inc(tr_done, 1)
                for k in range(6):
                    dve.wait_ge(tr_full, 8 * l + (6 + k // 2))
                    o = cqT[:, k, :] if k < 4 else ckvT[:, k - 4, :]
                    ts(o, ps[:, 5 + k // 2, (k % 2) * SEQ:(k % 2 + 1) * SEQ], glat[:, k:k + 1], None,
                       ALU.mult).then_inc(tr_done, 1)
                gl = l * LAYER_G + TM_G + FM_G
                dve.wait_ge(unit_done, gl * R + 2)
                for t in range(T):
                    ins = rotate(qpe[:, t], ps[:, 4, t * 256:(t + 1) * 256].rearrange("p (h n) -> p h n", h=4), qpe2[:, t],
                                 c1("cos_b", T, 64)[:, t, :], c1("sin_b", T, 64)[:, t, :], 4, 16)
                    if t < T - 1:
                        st(ins)
                    else:
                        st.done()
                        ins.then_inc(qpe_ready, 1)
                dve.wait_ge(kpe_full, l + 1)
                v.tensor_copy(kpT[0:64, :], ps[0:64, 7, 0:SEQ]).then_inc(kpe_done, 1)
                dve.wait_ge(qpt_full, l + 1)
                v.tensor_copy(qpT[0:64].rearrange("p a b -> p (a b)"), ps[0:64, 0:2, :].rearrange("p a b -> p (a b)")).then_inc(qpt_done, 1)

                def maxima(i):
                    dve.wait_ge(s_full, 4 * l + (i + 1))
                    src = ps[:, 0:4, :].rearrange("p h (t k) -> p (h t) k", t=T)
                    p8 = prob.rearrange("p h t k -> p (h t) k")
                    scale = {0: HD ** -0.5, 1: HD ** -0.5, 2: (HD + 64) ** -0.5, 3: 1.0}[i]
                    if i == 3:
                        dve.wait_ge(bias_masked, l + 1)
                        dve.wait_ge(t_full, 4 * l + 3)
                        stt(prob.rearrange("p h t k -> p (h t k)"), ps[:, 0:4, :].rearrange("p h k -> p (h k)"), HD ** -0.5,
                            nbias.rearrange("p h t k -> p (h t k)"), ALU.mult, ALU.add).then_inc(s_masked, 1)
                        dve.wait_ge(s_masked, l + 1)
                        src = p8
                    st(v.tensor_reduce(mx[:, i % 2, :], src, AX, ALU.max))
                    st.done()
                    ts(nb[:, i % 2, :], mx[:, i % 2, :], -scale, None, ALU.mult).then_inc(nb_done, 1)

                maxima(0)
                for i in range(4):
                    dve.wait_ge(exp_done, 4 * l + (i + 1))
                    st(v.reciprocal(rinv[:, i % 2, :], rs[:, i % 2, :]))
                    st.done()
                    p8 = prob.rearrange("p h t k -> p (h t) k")
                    tt(p8, p8, rinv[:, i % 2, :].unsqueeze(2).to_broadcast([P, 8, SEQ]), ALU.mult).then_inc(p_ready, 1)
                    dve.wait_ge(t_full, 4 * l + (i + 1))
                    v.tensor_copy(probT[:, 2:4].rearrange("p h t k -> p (h t k)"),
                                  ps[:, 6:8, :].rearrange("p h k -> p (h k)")).then_inc(pt_done, 1)
                    if i < 3:
                        maxima(i + 1)
                    dve.wait_ge(pv_full, 4 * l + (i + 1))
                    heads = slice(4 * i, 4 * i + 4)
                    tt(OT[:, heads, :].rearrange("p h k -> p (h k)"), ps[:, 4:6, :].rearrange("p h k -> p (h k)"),
                       PF[:, heads, :].rearrange("p h k -> p (h k)"), ALU.mult).then_inc(o_done, 1)

                dve.wait_ge(yrs_done, l + 1)
                dve.wait_ge(gpost_ready, 16 * l + 16)
                for t in range(T):
                    st(stt(Y[:, t, :], Y[:, t, :], rstd2[:, t:t + 1], gpost, ALU.mult, ALU.mult))
                st.done()
                for t in range(T):
                    tt(X[:, t, :], X[:, t, :], Y[:, t, :], ALU.add).then_inc(x_done, 1)
                dve.wait_ge(x_done, T * l + 2 * T)
                assert st.n == DVE_STEPS, st.n

            st.region(LAYERS * DVE_STEPS)
            dve.wait_ge(mod_done, LAYERS)
            for a, (row, j) in enumerate(((LAYERS, 1), (LAYERS + 1, 4))):
                stt(gsc[:, a, :], mod[:, j * KD:(j + 1) * KD], 1.0, g_pre[:, row, :], ALU.add, ALU.mult).then_inc(gsc_done, 1)
            dve.wait_ge(gsc_done, 2)
            prenorm(LAYERS, lambda k: gsc[:, 0, k:k + 1], lambda k: mod[:, k:k + 1])
            dve.wait_ge(c2_ready, 16)
            dve.wait_ge(zeroed, 1)
            dve.wait_ge(fm_free, N_WQ + R)
            pe_cols = small_of("pe", 2, CMP_LEN)
            for w, chunk in ((0, KC), (1, VC)):
                for half in range(2):
                    rows = slice(half * 64, half * 64 + 64)
                    for gp in range(2):
                        for a in range(2):
                            src = PF2[rows, chunk + gp, :].rearrange("p (n b) -> p b n", b=16)[:, :, a:a + NCMP]
                            last = tt(cmp_in[w][rows, half * 2 + gp, 16 * a:16 * a + 16, :], src,
                                      pe_cols[rows, w, 16 * a:16 * a + 16].unsqueeze(2).to_broadcast([64, 16, NCMP]), ALU.add)
                last.then_inc(cin_done, 1)
            for br, chunk in ((0, KS), (1, KW)):
                for half in range(2):
                    rows = slice(half * 64, half * 64 + 64)
                    last = v.tensor_copy(kz[rows, br, half * 2:half * 2 + 2, :], PF2[rows, chunk:chunk + 2, :])
            last.then_inc(kz_done, 1)
            dve.wait_ge(kc_full, 1)
            for half in range(2):
                rows = slice(half * 64, half * 64 + 64)
                v.tensor_copy(kcz[rows, half * 2:half * 2 + 2, 0:NCMP],
                              ps[rows, 5, half * 2 * NCMP:(half * 2 + 2) * NCMP].rearrange("p (a b) -> p a b", a=2)).then_inc(kc_done, 1)
            dve.wait_ge(kc_full, 2)
            v.tensor_copy(vcmp[0:NCMP].rearrange("p a b -> p (a b)"), ps[0:NCMP, 6, 0:4 * NSA_D]).then_inc(vc_done, 1)
            dve.wait_ge(cs_full, 1)
            cp = cprob.rearrange("p a b -> p (a b)")
            st(stt(cp, ps[:, 7, 0:T * NSA_HEADS * NCMP], NSA_D ** -0.5, c2("cmp_bias"), ALU.mult, ALU.add))
            st.done()
            st(v.tensor_reduce(cmx, cprob, AX, ALU.max))
            st.done()
            tt(cprob, cprob, cmx.unsqueeze(2).to_broadcast([P, 32, NCMP]), ALU.subtract).then_inc(cs_done, 1)
            dve.wait_ge(ce_done, 1)
            dve.wait_ge(gw_done, 1)
            st(v.tensor_reduce(crs, cprob, AX, ALU.add))
            st.done()
            st(v.reciprocal(cmx, crs))
            st.done()
            gwv = gw.rearrange("p t (h b) -> p t h b", b=3)
            for t in range(T):
                cols = slice(t * NSA_HEADS, (t + 1) * NSA_HEADS)
                st(stt(cw[:, cols], cmx[:, cols], small_of("row_ok")[:, t:t + 1], gwv[:, t, :, 0], ALU.mult, ALU.mult))
            dve.wait_ge(ct_full, 1)
            v.tensor_copy(cprobT[0:NCMP, 16:32, :].rearrange("p a b -> p (a b)"),
                          ps[0:NCMP, 4:8, :].rearrange("p a b -> p (a b)")).then_inc(ct_done, 1)
            dve.wait_ge(cpv_full, 1)
            st.done()
            tt(onsa, ps[:, 0:4, :].rearrange("p b (j d) -> p (b j) d", d=NSA_D),
               cw.unsqueeze(2).to_broadcast([P, 32, NSA_D]), ALU.mult).then_inc(co_done, 1)
            dve.wait_ge(co_done, 1)

            dist = c2("dist")

            def nmax(i):
                g = i // 2
                dve.wait_ge(n_full, i + 1)
                if i >= 2:
                    dve.wait_ge(n_t, i - 1)
                buf = nprob[i % 2]
                for r in range(4):
                    st(stt(buf[:, r, :], dist, float(-SLOPES[4 * g + r] * NSA_D ** 0.5), ps[:, r, 0:3 * P], ALU.mult, ALU.add))
                st.done()
                st(v.tensor_reduce(mx[:, i % 2, 0:4], buf[:, :, 0:P], AX, ALU.max))
                st(v.tensor_reduce(mx[:, i % 2, 4:8], buf[:, :, P:3 * P], AX, ALU.max))
                st.done()
                ts(nb[:, i % 2, :], mx[:, i % 2, :], -NSA_D ** -0.5, None, ALU.mult).then_inc(n_nb, 1)

            def retain(i):
                dve.wait_ge(n_full, 8 + i + 1)
                dve.wait_ge(n_t, 7 + i)
                decay = c2("decay", RET_HEADS, 3 * P)[:, 4 * i:4 * i + 4, :]
                tt(nprob[i % 2], ps[:, 0:4, 0:3 * P], decay, ALU.mult).then_inc(r_ready, 1)

            nmax(0)
            for i in range(8):
                g, br = i // 2, i % 2
                dve.wait_ge(n_exp, i + 1)
                st(v.reciprocal(rinv[:, i % 2, :], rs[:, i % 2, :]))
                st.done()
                wts = rinv[:, i % 2, :].rearrange("p (t r) -> p t r", t=T)
                st(tt(wts, wts, gwv[:, :, 4 * g:4 * g + 4, 1 + br], ALU.mult))
                dve.wait_ge(n_t, i + 1)
                v.tensor_copy(nprobT[:, 2:4, :], ps[:, 6:8, 0:3 * P]).then_inc(n_pt, 1)
                if i < 7:
                    nmax(i + 1)
                else:
                    retain(0)
                dve.wait_ge(n_pv, i + 1)
                st.done()
                st(tt(ntmp.rearrange("p t r d -> p (t r) d"), ps[:, 4, :].rearrange("p (j d) -> p j d", d=NSA_D),
                      rinv[:, i % 2, :].unsqueeze(2).to_broadcast([P, 8, NSA_D]), ALU.mult))
                st.done()
                o = onsa.rearrange("p (t h) d -> p t (h d)", t=T)[:, :, 4 * g * NSA_D:(4 * g + 4) * NSA_D]
                tt(o, o, ntmp.rearrange("p t r d -> p t (r d)"), ALU.add).then_inc(n_out, 1)
                dve.wait_ge(n_out, i + 1)
            retain(1)
            sq32 = area(22368, 32, NSA_D)
            st(tt(sq32, onsa, onsa, ALU.mult))
            st.done()
            v.tensor_reduce(hs, sq32, AX, ALU.add).then_inc(nss_done, 1)
            dve.wait_ge(nrs_done, 1)
            tt(onsa, onsa, cw.unsqueeze(2).to_broadcast([P, 32, NSA_D]), ALU.mult).then_inc(n_normed, 1)
            dve.wait_ge(yret_done, 2)
            st(v.tensor_reduce(crs[:, 0:16], yret, AX, ALU.add))
            st.done()
            st(ts(crs[:, 0:16], crs[:, 0:16], 1.0 / HD, None, ALU.mult))
            st.done()
            st(tt(yret, yret, crs[:, 0:16].unsqueeze(2).to_broadcast([P, 16, HD]), ALU.subtract))
            st.done()
            dve.wait_ge(n_normed, 1)
            sq16 = area(22368, 16, HD)
            st(tt(sq16, yret, yret, ALU.mult))
            st.done()
            v.tensor_reduce(hs[:, 0:16], sq16, AX, ALU.add).then_inc(nss_done, 1)
            dve.wait_ge(nrs_done, 2)
            tt(yret, yret, cw[:, 0:16].unsqueeze(2).to_broadcast([P, 16, HD]), ALU.mult).then_inc(n_normed, 1)
            for c in range(8):
                dve.wait_ge(ot_full, 4 + c // 2 + 1)
                stt(OT2[:, 8 + c, :], ps[:, 4 + c // 2, (c % 2) * SEQ:(c % 2 + 1) * SEQ], small_of("g_ret")[:, c:c + 1],
                    PF2[:, RG + c, :], ALU.mult, ALU.mult).then_inc(ot_done, 1)
            dve.wait_ge(tm_free, N_WO2 + WO_G + 2)
            dve.wait_ge(g1_full, 1)
            row = ps[:, 4:8, :].rearrange("p a b -> p (a b)")
            for t in range(T):
                st(tt(Y[:, t, :], Y[:, t, :], row, ALU.mult))
            st.done()
            for t in range(T):
                tt(X[:, t, :], X[:, t, :], Y[:, t, :], ALU.add).then_inc(x_done, 1)
            dve.wait_ge(x_done, T * (LAYERS + 2))

            prenorm(LAYERS + 1, lambda k: gsc[:, 1, k:k + 1], lambda k: mod[:, 3 * KD + k:3 * KD + k + 1])
            dve.wait_ge(sc_full, 1)
            v.tensor_copy(score[:, 1].rearrange("p a b -> p (a b)"), ps[:, 4:8, :].rearrange("p a b -> p (a b)")).then_inc(sc_done, 1)
            dve.wait_ge(sc_done, 2)

            def top16(rows, values, indices):
                n = len(rows)
                for j in range(n):
                    st(v.max(values[j][:, 0:8], rows[j]))
                st.done()
                for j in range(n):
                    st(v.max_index(indices[j][:, 0:8], values[j][:, 0:8], rows[j]))
                st.done()
                for j in range(n):
                    st(v.match_replace(rows[j], values[j][:, 0:8], rows[j], -3.0e38))
                st.done()
                for j in range(n):
                    st(v.max(values[j][:, 8:16], rows[j]))
                st.done()
                for j in range(n):
                    st(v.max_index(indices[j][:, 8:16], values[j][:, 8:16], rows[j]))
                st.done()

            iota16 = small_of("iota")[:, 0:TOPK]
            for t in range(T):
                top16([score[:, t, j, :] for j in range(16)], [half_v[:, j, :] for j in range(16)],
                      [half_i[:, j, :] for j in range(16)])
                st(v.tensor_copy(half_f, half_i))
                hv = half_v.rearrange("p (h s) k -> p h s k", s=2)
                st(tt(cand, hv[:, :, 0, :].unsqueeze(3).to_broadcast([P, PEER_HEADS, TOPK, TOPK]),
                      hv[:, :, 1, :].unsqueeze(2).to_broadcast([P, PEER_HEADS, TOPK, TOPK]), ALU.add))
                st.done()
                top16([cand[:, h].rearrange("p a b -> p (a b)") for h in range(PEER_HEADS)],
                      [top_v[:, h, :] for h in range(PEER_HEADS)], [pick[:, h, :] for h in range(PEER_HEADS)])
                st(ts(pick_i, pick, 4, None, ALU.logical_shift_right))
                st(ts(pick_j, pick, 15, None, ALU.bitwise_and))
                st.done()
                st(v.tensor_copy(pick_fi, pick_i))
                st(v.tensor_copy(pick_fj, pick_j))
                st.done()
                hf = half_f.rearrange("p (h s) k -> p h s k", s=2)
                for s, which in ((0, pick_fi), (1, pick_fj)):
                    shape = [P, PEER_HEADS * TOPK, TOPK]
                    m3 = match.rearrange("p h a b -> p (h a) b")
                    st(tt(m3, which.rearrange("p h k -> p (h k)").unsqueeze(2).to_broadcast(shape),
                          iota16[:, None, :].to_broadcast(shape), ALU.is_equal))
                    st.done()
                    st(tt(match, match, hf[:, :, s, :].unsqueeze(2).to_broadcast([P, PEER_HEADS, TOPK, TOPK]), ALU.mult))
                    st.done()
                    st(v.tensor_reduce(route[:, s, t, :], m3, AX, ALU.add))
                    st.done()
                gates = route[:, 2, t, :].rearrange("p (h k) -> p h k", h=PEER_HEADS)
                tt(gates, top_v, top_v[:, :, 0:1].to_broadcast([P, PEER_HEADS, TOPK]), ALU.subtract).then_inc(rexp_in, 1)
            for t in range(T):
                gates = route[:, 2, t, :].rearrange("p (h k) -> p h k", h=PEER_HEADS)
                dve.wait_ge(rexp_done, t + 1)
                st(v.tensor_reduce(hs[:, 0:8], gates, AX, ALU.add))
                st.done()
                st(v.reciprocal(hs[:, 8:16], hs[:, 0:8]))
                st.done()
                tt(gates, gates, hs[:, 8:16].unsqueeze(2).to_broadcast([P, PEER_HEADS, TOPK]), ALU.mult).then_inc(routed, 1)
                dve.wait_ge(routed, t + 1)
            dve.wait_ge(rt_full, 1)
            for a in range(3):
                st(v.tensor_copy(routeT[:, a, :], ps[:, a, 0:SEQ]))
            st.done()
            dve.sem_inc(rt_done, 1)
            dve.wait_ge(fm_free, N_U + U_G * R + R)

            def first_hot(t0, b):
                for j in range(4):
                    ts(hot1[:, b, j, :], small_of("iota"), routeT[:, 0, bass.ds(t0 + j, 1)], routeT[:, 2, bass.ds(t0 + j, 1)],
                       ALU.is_equal, ALU.mult).then_inc(hot1_done, 1)

            def gated(n, t0, b):
                dve.wait_ge(g_full, n + 1)
                o = act_e[:, :, bass.ds(t0, 4)].rearrange("p i t -> p t i")
                tt(o, o, ps[:, b, :].rearrange("p (t i) -> p t i", t=4), ALU.mult).then_inc(g_used, 1)

            first_hot(0, 0)
            with dve.Fori(0, SEQ // 8 - 1) as i:
                first_hot(i * 8 + 4, 1)
                gated(i * 2, i * 8, 0)
                first_hot(i * 8 + 8, 0)
                gated(i * 2 + 1, i * 8 + 4, 1)
            first_hot(SEQ - 4, 1)
            gated(SEQ // 4 - 2, SEQ - 8, 0)
            gated(SEQ // 4 - 1, SEQ - 4, 1)

            dve.wait_ge(unit_done, GROUPS * R)
            dve.wait_ge(g2_done, 1)
            for t in range(T):
                st(tt(ysum[:, t, :], ps[:, 4 * t:4 * t + 4, :].rearrange("p a b -> p (a b)"), gate2row, ALU.mult))
            st.done()
            for t in range(T):
                tt(X[:, t, :], X[:, t, :], ysum[:, t, :], ALU.add).then_inc(x_done, 1)
            dve.wait_ge(frs_done, 1)
            dve.wait_ge(gfin_ready, 16)
            for t in range(T):
                stt(X[:, t, :], X[:, t, :], rstd2[:, t:t + 1], gfin, ALU.mult, ALU.mult).then_inc(fin_ready, 1)


def rows_units(w):
    g = w.shape[1] // 512
    return w.reshape(4, 4, P, g, 512).transpose(3, 0, 2, 1, 4).reshape(4 * g, P, UNIT)


def cols_units(w):
    c = w.shape[1] // P
    return w.reshape(KD, P, c, P).transpose(2, 1, 0, 3).reshape(c, P, UNIT)


def padded(*parts):
    u = np.zeros((1, P, UNIT), np.float32)
    at = 0
    for p in parts:
        p = p.reshape(P, -1)
        u[0, :, at:at + p.shape[1]] = p
        at += p.shape[1]
    return u


def by_tile(w):
    return w.reshape(-1, P, w.shape[1]).transpose(1, 0, 2)


def col(vec):
    v = vec.reshape(-1, P)
    return np.ascontiguousarray(v.T)


def weight_stream(a):
    empty = np.zeros((1, P, UNIT), np.float32)
    units = []
    for l in range(LAYERS):
        w = a["w_in"][l]
        (aq, ak, av, ag, cq, ckv, kr, bg, q3, k3, v3, g3) = np.split(
            w, np.cumsum([1024, 256, 256, 1024, 512, 256, 64, 512, 512, 512, 512])[:11], axis=1)
        pad = np.zeros((DM, TM_W - 2880), np.float32)
        units.append(rows_units(np.concatenate([aq, ak, av, cq, v3, ckv, kr, pad], axis=1)))
        units.append(cols_units(np.concatenate([ag, bg, g3, q3, k3], axis=1)))
        uq = a["b_w_uq"][l].reshape(512, 4, 192)
        ukv = a["b_w_ukv"][l].reshape(256, 4, 256)
        units.append(padded(by_tile(uq[:, :, :128].reshape(512, 512))))
        units.append(padded(by_tile(uq[:, :, 128:].reshape(512, 256))))
        units.append(padded(by_tile(np.concatenate([ukv[:, :, :128].reshape(256, 512),
                                                    ukv[:, :, 128:].reshape(256, 512)], axis=1))))
        units.append(empty)
        units.append(rows_units(a["w_out"][l]))
    w = a["w_in_2"][0]
    (q, kc, vc, ks, vs, kw, vw, ga, qr, kr, vr, gr) = np.split(
        w, np.cumsum([1024] + [256] * 6 + [48, 1024, 1024, 1024])[:11], axis=1)
    units.append(rows_units(np.concatenate([vs, vw, vr], axis=1)))
    units += [padded(by_tile(ga)), empty, empty, empty]
    order = np.zeros((8, 2), np.int64)
    for h in range(NSA_HEADS):
        order[nsa_chunk(h)] = h
    qo = q.reshape(DM, NSA_HEADS, NSA_D)[:, order.reshape(-1)].reshape(DM, 1024)
    units.append(cols_units(np.concatenate([qo, kc, vc, ks, kw, qr, kr, gr], axis=1)))
    for name in ("cmp_k_w1_2", "cmp_v_w1_2"):
        w1 = a[name][0].reshape(2, 16, NSA_D, P).transpose(0, 2, 1, 3).reshape(2, NSA_D, UNIT)
        units.append(np.concatenate([w1, w1], axis=1))
    units.append(rows_units(a["w_out_2"][0]))
    units.append(cols_units(a["peer_w_q_2"][0]))
    units += [padded(a["peer_sub_keys_2"][0].reshape(16, KEYS, P).transpose(2, 0, 1)), empty, empty, empty]
    u = a["peer_u_2"][0].reshape(KEYS, KEYS, KD, P)
    units.append(u.transpose(1, 3, 2, 0).reshape(KEYS, P, UNIT))
    units.append(a["peer_v_2"][0].reshape(KEYS, KEYS, DM).transpose(1, 0, 2))
    s = np.concatenate(units, axis=0)
    assert s.shape[0] == GROUPS * R, (s.shape, GROUPS * R)
    return s


def fill(spec, width, values):
    o = np.zeros((P, width), np.float32)
    for name, (at, n) in spec.items():
        o[:, at:at + n] = values[name]
    return o


def rotary(n):
    half = n // 2
    inv = (1.0 / (np.float32(10000.0) ** (np.arange(0, half, 2, dtype=np.float32) / np.float32(half)))).astype(np.float32)
    t = np.arange(SEQ)
    cos, sin = [], []
    for pos in (t // GRID, t % GRID):
        ang = pos.astype(np.float32)[:, None] * inv[None, :]
        cos += [np.cos(ang), np.cos(ang)]
        sin += [-np.sin(ang), np.sin(ang)]
    return [np.concatenate(z, axis=1).astype(np.float32) for z in (cos, sin)]


def tiles(m):
    return m.reshape(T, P, -1).transpose(1, 0, 2).reshape(P, -1)


def host(a):
    rep = lambda r: np.broadcast_to(r.reshape(1, -1), (P, r.size))
    b_ada = a["b_ada_2"][0]
    t = np.arange(SEQ)
    small = fill(SMALL, SMALL_W, {
        "ident": np.eye(P, dtype=np.float32), "one": 1.0, "pow": -0.5,
        "g_pre": np.concatenate([col(a["norm_pre"]), col(a["g_norm_mix_2"]), col(a["g_norm_ffn_2"])], axis=1),
        "b_qn": col(a["b_q_norm"]), "b_kvn": col(a["b_kv_norm"]),
        "g_nsa": col(a["g_nsa_out_2"]), "g_ret": col(a["g_ret_out_2"]),
        "cond": col(a["c_2"]), "b_ada": col(b_ada), "iota": np.arange(P, dtype=np.float32)[None, :],
        "row_ok": (t >= CMP_LEN - 1).astype(np.float32).reshape(T, P).T,
        "w2k": np.concatenate([a["cmp_k_w2_2"][0]] * 2, axis=1), "w2v": a["cmp_v_w2_2"][0],
        "pe": np.concatenate([np.concatenate([a[n][0].T] * 2, axis=0) for n in ("cmp_pe_k_2", "cmp_pe_v_2")], axis=1),
    })
    cos, sin = rotary(HD)
    cos_b, sin_b = rotary(64)
    c0 = np.clip(t % GRID - 8, 0, GRID - 16)
    kc = t % GRID
    near = (kc[None, :] >= c0[:P, None]) & (kc[None, :] < c0[:P, None] + 16)
    g_qk = np.stack([a["a_q_norm"], a["a_k_norm"]], axis=1).reshape(1, -1)
    const1 = fill(CONST1, CONST1_W, {
        "cos": tiles(cos), "sin": tiles(sin), "cos_b": tiles(cos_b), "sin_b": tiles(sin_b),
        "g_qk": rep(g_qk), "nbr": np.where(near, 0.0, MASKED)})
    d = (t[:, None] - t[None, :]).astype(np.float32)
    dist = np.where(d >= 0, d, np.float32(-MASKED))
    dc = (t[:, None] - (np.arange(NCMP) * CMP_STRIDE + CMP_LEN - 1)[None, :]).astype(np.float32)
    cb = np.where(dc[:, None, :] >= 0, -SLOPES[None, :, None] * dc[:, None, :], np.float32(MASKED))
    lg = np.log1p(-np.exp2(-5.0 - np.arange(RET_HEADS, dtype=np.float64)))
    dd = (t[None, :] - t[:, None]).astype(np.float64)
    decay = np.where(dd >= 0, np.exp(lg[:, None, None] * np.maximum(dd, 0)), 0.0) * HD ** -0.5
    decay = np.concatenate([decay[:, 0:P, :], decay[:, P:, P:]], axis=2).transpose(1, 0, 2).reshape(P, -1)
    const2 = fill(CONST2, CONST2_W, {
        "dist": np.concatenate([dist[0:P, 0:P], dist[P:, :]], axis=1),
        "cmp_bias": tiles(cb.reshape(SEQ, -1)), "decay": decay})
    rpb = np.pad(a["c_rpb"], ((0, 0), (0, 0), (0, 0), (48, 48)))
    win = np.stack([rpb[..., GRID - 1 - c:2 * GRID - 1 - c] for c in range(GRID)], axis=3)
    rows = t // GRID
    nbr = np.zeros((LAYERS, 2, GRID, 4, T, 4, GRID), np.float32)
    for qr in range(4):
        for kr in range(4):
            nbr[:, qr % 2, :, :, qr // 2, kr, :] = win[:, :, kr - qr + 7].transpose(0, 2, 1, 3)
    ada = a["w_ada_2"][0].reshape(ADA_H, 2, P, ADA_CG, 512).transpose(3, 0, 2, 1, 4).reshape(ADA_CG, ADA_H, P, ADA_UNIT)
    return {
        "stream": weight_stream(a), "ada": np.ascontiguousarray(ada), "small": small, "const1": const1,
        "const2": const2, "nbr_bias": nbr.reshape(LAYERS, P, -1),
        "g_post": np.ascontiguousarray(np.broadcast_to(a["norm_post"][:, None, :], (LAYERS, P, DM))),
        "g_final": np.ascontiguousarray(rep(a["g_norm_final_2"])), "x": np.ascontiguousarray(a["x"]),
    }


def kernel(**inputs):
    import concourse.bacc as bacc
    from concourse.bass_utils import run_bass_kernel_spmd

    arrays = host({k: np.asarray(v) for k, v in inputs.items()})
    nc = bacc.Bacc("TRN2", target_bir_lowering=False, num_devices=1)
    args = [nc.dram_tensor(f"in_{n}", v.shape, F32, kind="ExternalInput").ap() for n, v in arrays.items()]
    out = nc.dram_tensor("out", (1, SEQ, DM), F32, kind="ExternalOutput").ap()
    block(nc, *args, out)
    r = run_bass_kernel_spmd(nc, [{f"in_{n}": v for n, v in arrays.items()}], core_ids=[0])
    return r.results[0]["out"]
```

```python
from contextlib import ExitStack

import numpy as np
import concourse.bass as bass
from concourse import mybir

P = 128
F32 = mybir.dt.float32
F32R = mybir.dt.float32r
U32 = mybir.dt.uint32
ALU = mybir.AluOpType
ACT = mybir.ActivationFunctionType
AX = mybir.AxisListType.X

SEQ, DM = 256, 2048
T = SEQ // P
KD = DM // P
LAYERS = 2
HD = 128
GRID = 64
EPS = 1e-6
MASKED = -1e30
NSA_HEADS, NSA_GROUPS, NSA_D = 16, 4, 64
CMP_LEN, CMP_STRIDE = 32, 16
NCMP = (SEQ - CMP_LEN) // CMP_STRIDE + 1
RET_HEADS = 8
PEER_HEADS, KEYS, TOPK = 8, 128, 16
PAIRS = PEER_HEADS * TOPK
MODS = 6

R = 4
UNIT = 2048
TM_G, FM_G, LAT_G, WO_G = 6, 6, 1, 4
LAYER_G = TM_G + FM_G + LAT_G + WO_G
TM2_G, GATE_G, FM2_G, CMP_G, WQ_G = 3, 1, 10, 1, 4
G_TM2 = LAYERS * LAYER_G
G_GATE = G_TM2 + TM2_G
G_FM2 = G_GATE + GATE_G
G_CMP = G_FM2 + FM2_G
G_WO2 = G_CMP + CMP_G
G_WQ = G_WO2 + WO_G
G_EXP = G_WQ + WQ_G
PARTS = 4
PART = KEYS // PARTS
PART_G = PART // R
EXPERT_ORDER = ("U0", "U1", "V0", "U2", "V1", "U3", "V2", "V3")
G_OF = {name: G_EXP + i * PART_G for i, name in enumerate(EXPERT_ORDER)}
GROUPS = G_EXP + len(EXPERT_ORDER) * PART_G
BATCH = 8
assert SEQ // BATCH == PART

ADA_CG = MODS * DM // 512
ADA_PER_LAYER = ADA_CG // LAYERS
ADA_H = KD // 2
ADA_EARLY = 6
ADA_UNIT = 2 * 512

A_Q, A_K, A_V, B_CQ, C_V, B_CKV, B_KR, TM_W = 0, 1024, 1280, 1536, 2048, 2560, 2816, 3072
QK_HEADS = 10
GATE_CHUNKS = 16
C_Q, C_K, FM_C = 16, 20, 24
V_S, V_W, V_R, TM2_W = 0, 256, 512, 1536
NQ, KC, VC, KS, KW, RQ, RK, RG, FM2_C = 0, 8, 10, 12, 14, 16, 24, 32, 40
NGATE = 3 * NSA_HEADS

SMALL = {}
_at = 0
for _name, _n in (("ident", P), ("one", 1), ("pow", 32), ("g_pre", 4 * KD), ("b_qn", 2 * 4), ("b_kvn", 2 * 2),
                  ("cond", KD), ("b_ada", MODS * KD), ("iota", P)):
    SMALL[_name] = (_at, _n)
    _at += _n
SMALL_W = _at
CONST1 = {}
_at = 0
for _name, _n in (("cos", T * 128), ("sin", T * 128), ("cos_b", T * 64), ("sin_b", T * 64),
                  ("g_qk", LAYERS * 2 * 128), ("nbr", SEQ)):
    CONST1[_name] = (_at, _n)
    _at += _n
CONST1_W = _at
CONST2 = {}
_at = 0
for _name, _n in (("dist", 3 * P), ("cmp_bias", NSA_HEADS * T * NCMP), ("decay", RET_HEADS * 3 * P)):
    CONST2[_name] = (_at, _n)
    _at += _n
CONST2_W = _at
CONST3 = {}
_at = 0
for _name, _n in (("row_ok", T), ("w2k", P), ("w2v", NSA_D), ("pe", 2 * CMP_LEN), ("g_nsa", 8), ("g_ret", 8)):
    CONST3[_name] = (_at, _n)
    _at += _n
CONST3_W = _at

SLOPES = np.exp2(-8.0 * (np.arange(NSA_HEADS, dtype=np.float32) + 1.0) / NSA_HEADS).astype(np.float32)


def nsa_chunk(h):
    g, r = h // 4, h % 4
    return (g // 2) * 4 + r, g % 2


class Steps:

    def __init__(self, eng, sem):
        self.eng, self.sem, self.base, self.n = eng, sem, 0, 0

    def region(self, base):
        self.base, self.n = base, 0

    def __call__(self, ins):
        ins.then_inc(self.sem, 1)
        self.n += 1

    def done(self):
        self.eng.wait_ge(self.sem, self.base + self.n)


DVE_STEPS, POOL_STEPS = 52, 5


def block(nc, stream, ada, small, const1, const2, const3, keys, nbr_bias, g_post, g_final, x, out):
    ctx = ExitStack()

    def sb(name, shape, dt=F32):
        return ctx.enter_context(nc.sbuf_tensor(name, shape, dt))

    def sem(name):
        return ctx.enter_context(nc.semaphore(name))

    with ctx:
        X = sb("X", [P, T, DM])
        ring = sb("ring", [P, R, UNIT])
        aring = sb("aring", [P, 2, ADA_UNIT])
        SM = sb("SM", [P, SMALL_W])
        mod = sb("mod", [P, MODS * KD])
        csilu = sb("csilu", [P, KD])
        gsc = sb("gsc", [P, 2, KD])
        stat = sb("stat", [P, 384])
        with ExitStack() as before_experts:
            hbuf = before_experts.enter_context(nc.sbuf_tensor("hbuf", [P, KD * SEQ], F32))
            BIG = before_experts.enter_context(nc.sbuf_tensor("BIG", [P, 32768], F32))
        stage_h, stage_l = sb("stage_h", [P, 2, SEQ], F32R), sb("stage_l", [P, 2, SEQ], F32R)
        tables = sb("tables", [P, 2 * BATCH * (KEYS + PART) + 3 * SEQ])
        hh, hl = sb("hh", [P, KD, SEQ], F32R), sb("hl", [P, KD, SEQ], F32R)
        wh, wl = sb("wh", [P, 2, UNIT], F32R), sb("wl", [P, 2, UNIT], F32R)
        act_e = [sb("act0", [P, PART, SEQ]), sb("act1", [P, PART, SEQ])]
        ps = ctx.enter_context(nc.psum_tensor("ps", [P, 8, 512], F32))

        def area(at, *dims, buf=BIG):
            n = int(np.prod(dims))
            v = buf[:, at:at + n]
            if len(dims) == 1:
                return v
            names = "abcd"[:len(dims)]
            spec = "p (" + " ".join(names) + ") -> p " + " ".join(names)
            return v.rearrange(spec, **dict(zip(names, dims)))

        def small_of(name, *dims):
            at, n = SMALL[name]
            return area(at, *(dims or (n,)), buf=SM)

        hT = area(0, KD, SEQ, buf=hbuf)
        ident, one, power = small_of("ident"), small_of("one"), small_of("pow")
        g_pre = small_of("g_pre", 4, KD)
        g_cq, g_ckv = small_of("b_qn", 2, 4), small_of("b_kvn", 2, 2)

        Xn = area(0, T, DM)
        Y = area(0, T, DM)
        PT = area(0, T, TM_W)
        PF = area(6144, FM_C, SEQ)
        acc = area(23552, ADA_PER_LAYER, 512)
        OT = area(12288, KD, SEQ)
        rot1, rot2 = area(12288, QK_HEADS, HD), area(12288 + 1280, QK_HEADS, HD)
        junk = area(12288 + 2560, 512)
        krot = area(12288 + 3072, 2, T, 64)
        nbias = area(16384, 4, T, SEQ)
        C1 = 18432
        gpost = area(C1 + CONST1_W, DM)
        qkT = area(23552, QK_HEADS, SEQ)
        cqT, ckvT = area(26112, 4, SEQ), area(27136, 2, SEQ)
        qnT, qpT = area(27648, 4, SEQ), area(28672, 4, SEQ)
        knT, kpT = area(29696, 4, SEQ), area(30720, SEQ)
        vB = area(30976, T, 512)
        qpe = area(22016, T, 4, 64)
        qpe2 = area(22016 + 512, T, 4, 64)
        prob = area(0, 4, T, SEQ, buf=hbuf)
        probT = area(2048, 4, T, SEQ, buf=hbuf)

        def c1(name, *dims):
            at, n = CONST1[name]
            return area(C1 + at, *(dims or (n,)))

        PT2 = area(0, T, TM2_W)
        PF2 = area(4096, FM2_C, SEQ)
        OT2 = area(14336, KD, SEQ)
        C2, C3 = 18432, 32288
        kz = area(22368, 2, 4, SEQ)
        cmp_in = [area(24416, 4, CMP_LEN, NCMP), area(24416 + 1920, 4, CMP_LEN, NCMP)]
        kcz = area(28256, 4, 16)
        hid = area(28320, 2, 64)
        vcmp = area(28448, 4, NSA_D)
        onsa = area(28704, T * NSA_HEADS, NSA_D)
        yret = area(24416, T * RET_HEADS, HD)
        square = area(22368, 2048)
        nprobT = area(30752, 4, 3 * P)
        cprob = area(30752, T * NSA_HEADS, NCMP)
        cprobT = area(0, T * NSA_HEADS, P, buf=hbuf)
        nprob = [area(0, 4, 3 * P, buf=hbuf), area(1536, 4, 3 * P, buf=hbuf)]
        ntmp = area(3072, T, 4, NSA_D, buf=hbuf)

        def c2(name, *dims):
            at, n = CONST2[name]
            return area(C2 + at, *(dims or (n,)))

        def c3(name, *dims):
            at, n = CONST3[name]
            return area(C3 + at, *(dims or (n,)))

        flat = [act_e[i][:, :, :].rearrange("p a b -> p (a b)") for i in range(2)]
        table = tables[:, :]
        side = aring[:, :, :].rearrange("p a b -> p (a b)")
        qP = area(0, 16, SEQ, buf=flat[0])
        score = area(0, T, 16, KEYS, buf=flat[1])
        cand = area(4096, PEER_HEADS, TOPK, TOPK, buf=flat[1])
        match = area(6144, PEER_HEADS, TOPK, TOPK, buf=flat[1])
        half_v = area(0, 16, TOPK, buf=table)
        half_i = area(256, 16, TOPK, buf=table).bitcast(U32)
        half_f = area(512, 16, TOPK, buf=table)
        top_v = area(768, PEER_HEADS, TOPK, buf=table)
        pick = area(896, PEER_HEADS, TOPK, buf=table).bitcast(U32)
        pick_i = area(1024, PEER_HEADS, TOPK, buf=table).bitcast(U32)
        pick_j = area(1152, PEER_HEADS, TOPK, buf=table).bitcast(U32)
        pick_fi = area(1280, PEER_HEADS, TOPK, buf=table)
        pick_fj = area(1408, PEER_HEADS, TOPK, buf=table)
        route = area(1536, 3, T, PAIRS, buf=table)
        HOT2 = 2 * BATCH * KEYS
        hot1 = area(0, 2, BATCH, KEYS, buf=table)
        hot2 = area(HOT2, 2, BATCH, PART, buf=table)
        routeT = area(HOT2 + 2 * BATCH * PART, 3, SEQ, buf=table)
        keyT = area(0, 16, KEYS, buf=side)
        gate2row = side
        gfin = area(0, DM, buf=flat[0])
        ysum = [area(4096, T, DM, buf=flat[i]) for i in range(2)]
        squares = area(0, T, DM, buf=flat[1])
        lsquares = area(4096, T, DM)

        ss2, rstd2 = stat[:, 0:2], stat[:, 2:4]
        ssq, msq, rsq = stat[:, 4:28], stat[:, 28:52], stat[:, 52:76]
        mx, nb = area(76, 2, 8, buf=stat), area(92, 2, 8, buf=stat)
        rs, rinv = area(108, 2, 8, buf=stat), area(124, 2, 8, buf=stat)
        ms2 = stat[:, 140:142]
        gw = area(144, T, NGATE, buf=stat)
        cmx, crs = stat[:, 240:272], stat[:, 272:304]
        cw = stat[:, 304:336]
        hs = stat[:, 336:368]
        gcol, glat = gsc[:, 0, :], gsc[:, 1, 0:6]
        w_ready = [sem(f"w_ready{s}") for s in range(R)]
        unit_done = sem("unit_done")
        a_ready = [sem(f"a_ready{s}") for s in range(2)]
        a_used = sem("a_used")
        a_step = sem("a_step")
        loaded = sem("loaded")
        c1_ready, bias_ready, gpost_ready = sem("c1_ready"), sem("bias_ready"), sem("gpost_ready")
        bias_masked = sem("bias_masked")
        c_ready = sem("c_ready")
        x_done = sem("x_done")
        tm_free, fm_free = sem("tm_free"), sem("fm_free")
        sq_done, prs_done, xn_done = sem("sq_done"), sem("prs_done"), sem("xn_done")
        ht_full, ht_done = sem("ht_full"), sem("ht_done")
        mod_full, mod_done = sem("mod_full"), sem("mod_done")
        dve_step, pool_step, act_step = sem("dve_step"), sem("pool_step"), sem("act_step")
        qss_done, qrs_done = sem("qss_done"), sem("qrs_done")
        qk_ready, tr_full, tr_done = sem("qk_ready"), sem("tr_full"), sem("tr_done")
        lat_done, qpe_ready, kpe_full, kpe_done = sem("lat_done"), sem("qpe_ready"), sem("kpe_full"), sem("kpe_done")
        qpt_full, qpt_done = sem("qpt_full"), sem("qpt_done")
        s_full, nb_done, exp_done, p_ready = sem("s_full"), sem("nb_done"), sem("exp_done"), sem("p_ready")
        t_full, pt_done, pv_full, o_done = sem("t_full"), sem("pt_done"), sem("pv_full"), sem("o_done")
        s_masked = sem("s_masked")
        ysq_done, yrs_done = sem("ysq_done"), sem("yrs_done")
        pe_passed, pool_passed = sem("pe_passed"), sem("pool_passed")
        c2_ready, zeroed, gates_full, gw_done = sem("c2_ready"), sem("zeroed"), sem("gates_full"), sem("gw_done")
        gsc_done, kz_done, cin_done = sem("gsc_done"), sem("kz_done"), sem("cin_done")
        hid_done, kc_full, kc_done, vc_done = sem("hid_done"), sem("kc_full"), sem("kc_done"), sem("vc_done")
        cs_full, cs_done, ce_done, ct_full, ct_done = sem("cs_full"), sem("cs_done"), sem("ce_done"), sem("ct_full"), sem("ct_done")
        cpv_full, co_done = sem("cpv_full"), sem("co_done")
        n_full, n_nb, n_exp, n_t = sem("n_full"), sem("n_nb"), sem("n_exp"), sem("n_t")
        n_pt, n_pv, n_out = sem("n_pt"), sem("n_pv"), sem("n_out")
        r_ready, yret_done = sem("r_ready"), sem("yret_done")
        nss_done, nrs_done, n_normed, ot_full, ot_done = (sem("nss_done"), sem("nrs_done"), sem("n_normed"),
                                                          sem("ot_full"), sem("ot_done"))
        g1_full = sem("g1_full")
        sc_full, sc_done, routed, rexp_in, rexp_done = sem("sc_full"), sem("sc_done"), sem("routed"), sem("rexp_in"), sem("rexp_done")
        rt_full = sem("rt_full")
        keys_ready = sem("keys_ready")
        hi_done, lo_done = sem("hi_done"), sem("lo_done")
        hh_done, hl_done = sem("hh_done"), sem("hl_done")
        hot_done, g_full, g_used = sem("hot_done"), sem("g_full"), sem("g_used")
        g2_full, g2_done = sem("g2_full"), sem("g2_done")
        y_used = sem("y_used")
        gfin_ready = sem("gfin_ready")
        frs_done, fss_done, out_done = sem("frs_done"), sem("fss_done"), sem("out_done")
        fin_ready = sem("fin_ready")

        TM_N = TM_G + WO_G
        N_TM2 = LAYERS * TM_N
        N_WO2 = N_TM2 + TM2_G
        N_FM = LAYERS * FM_G * R
        N_WQ = N_FM + FM2_G * R
        N_U = N_WQ + WQ_G * R

        blk = ctx.enter_context(nc.Block())

        @blk.sync
        def _(sp):
            sp.dma_start(SM[:, :], small).then_inc(loaded, 16)
            sp.dma_start(X[:, :, :], x.rearrange("b (t p) d -> p (b t) d", p=P)).then_inc(loaded, 16)
            for s in range(R):
                sp.dma_start(ring[:, s, :], stream[s]).then_inc(w_ready[s], 16)
            with sp.Fori(1, G_WQ + 1) as g:
                for s in range(R):
                    sp.wait_ge(unit_done, g * R + (s + 1 - R))
                    sp.dma_start(ring[:, s, :], stream[g * R + s]).then_inc(w_ready[s], 16)
            sp.wait_ge(a_used, ADA_CG * ADA_H + 2)
            sp.dma_start(side, keys).then_inc(keys_ready, 16)
            with sp.Fori(G_WQ + 1, GROUPS) as g:
                for s in range(R):
                    sp.wait_ge(lo_done, (g - G_WQ) * R + (s + 1 - R))
                    sp.dma_start(ring[:, s, :], stream[g * R + s]).then_inc(w_ready[s], 16)
            sp.wait_ge(unit_done, G_OF["V3"] * R)
            sp.dma_start(gfin, g_final).then_inc(gfin_ready, 16)
            for t in range(T):
                sp.wait_ge(fin_ready, t + 1)
                sp.dma_start(out[0, t * P:(t + 1) * P, :], X[:, t, :]).then_inc(out_done, 16)
            sp.wait_ge(out_done, 16 * T)

        @blk.tensor
        def _(pe):
            mm = pe.matmul

            def unit(g, s):
                pe.wait_ge(w_ready[s], 16 * (g + 1))

            def settle():
                pe.sem_inc(pe_passed, 1)

            def rows_group(lhs, g, n, pair):
                pe.wait_ge(tm_free, n + 1)
                for s in range(R):
                    unit(g, s)
                    for t in range(T):
                        for kk in range(4):
                            last = mm(ps[:, 2 * pair + t, :], lhs[:, 4 * s + kk, t * P:(t + 1) * P],
                                      ring[:, s, kk * 512:(kk + 1) * 512],
                                      start=(s == 0 and kk == 0), stop=(s == R - 1 and kk == 3))
                    last.then_inc(unit_done, 1)

            def cols_group(g, n, rhs):
                for c in range(R):
                    pe.wait_ge(fm_free, n + c + 1)
                    unit(g, c)
                    for k in range(KD):
                        last = mm(ps[:, 4 + c, 0:SEQ], ring[:, c, k * P:(k + 1) * P], rhs[:, k, :],
                                  start=(k == 0), stop=(k == KD - 1))
                    last.then_inc(unit_done, 1)

            def prenorm(i):
                pe.wait_ge(xn_done, T * (i + 1))
                for b in range(8):
                    for kk in range(2):
                        k = 2 * b + kk
                        for t in range(T):
                            last = pe.transpose(ps[:, b, kk * SEQ + t * P:kk * SEQ + (t + 1) * P],
                                                Xn[:, t, k * P:(k + 1) * P], ident)
                    last.then_inc(ht_full, 1)
                pe.wait_ge(ht_done, KD * (i + 1))
                settle()

            pe.wait_ge(loaded, 32)
            with pe.Fori(0, LAYERS) as l:
                prenorm(l)
                with pe.Fori(0, TM_G // 2) as i:
                    for p in range(2):
                        rows_group(hT, l * LAYER_G + i * 2 + p, l * TM_N + i * 2 + p, p)
                with pe.Fori(0, FM_G) as i:
                    cols_group(l * LAYER_G + i + TM_G, l * FM_C + i * R, hT)
                pe.wait_ge(qk_ready, 2 * (l + 1))
                pe.wait_ge(fm_free, (l + 1) * FM_C + R)
                pe.wait_ge(a_used, (l + 1) * (ADA_PER_LAYER * ADA_H) + 2)
                for i in range(ADA_PER_LAYER):
                    for j in range(4):
                        last = mm(ps[:, 4, 4 * i + j:4 * i + j + 1], acc[:, i, j * P:(j + 1) * P], one,
                                  start=True, stop=True)
                last.then_inc(mod_full, 1)
                pe.wait_ge(mod_done, l + 1)
                for b in range(5):
                    for half in range(2):
                        for t in range(T):
                            at = (2 * b + half) * HD
                            last = pe.transpose(ps[:, b, half * SEQ + t * P:half * SEQ + (t + 1) * P],
                                                PT[:, t, at:at + HD], ident)
                    last.then_inc(tr_full, 1)
                for b in range(5, 8):
                    for half in range(2):
                        k = 2 * (b - 5) + half
                        at = B_CQ + k * P if k < 4 else B_CKV + (k - 4) * P
                        for t in range(T):
                            last = pe.transpose(ps[:, b, half * SEQ + t * P:half * SEQ + (t + 1) * P],
                                                PT[:, t, at:at + P], ident)
                    last.then_inc(tr_full, 1)
                pe.wait_ge(tr_done, 11 * (l + 1))
                gl = l * LAYER_G + TM_G + FM_G
                unit(gl, 0)
                for c in range(4):
                    for k in range(4):
                        last = mm(ps[:, c // 2, (c % 2) * SEQ:(c % 2 + 1) * SEQ],
                                  ring[:, 0, k * 512 + c * P:k * 512 + (c + 1) * P], cqT[:, k, :],
                                  start=(k == 0), stop=(k == 3))
                last.then_inc(unit_done, 1)
                unit(gl, 1)
                for t in range(T):
                    for k in range(4):
                        last = mm(ps[:, 4, t * 256:(t + 1) * 256], cqT[:, k, t * P:(t + 1) * P],
                                  ring[:, 1, k * 256:(k + 1) * 256], start=(k == 0), stop=(k == 3))
                last.then_inc(unit_done, 1)
                for t in range(T):
                    last = pe.transpose(ps[0:64, 7, t * P:(t + 1) * P], krot[:, 0, t, :], ident)
                last.then_inc(kpe_full, 1)
                unit(gl, 2)
                unit(gl, 3)
                for c in range(4):
                    for k in range(2):
                        last = mm(ps[:, 2 + c // 2, (c % 2) * SEQ:(c % 2 + 1) * SEQ],
                                  ring[:, 2, k * 1024 + c * P:k * 1024 + (c + 1) * P], ckvT[:, k, :],
                                  start=(k == 0), stop=(k == 1))
                for t in range(T):
                    for k in range(2):
                        last = mm(ps[:, 5 + t, :], ckvT[:, k, t * P:(t + 1) * P],
                                  ring[:, 2, k * 1024 + 512:(k + 1) * 1024], start=(k == 0), stop=(k == 1))
                last.then_inc(unit_done, 2)
                pe.wait_ge(qpe_ready, l + 1)
                pe.wait_ge(lat_done, 3 * (l + 1))
                settle()
                for h in range(4):
                    for t in range(T):
                        last = pe.transpose(ps[0:64, h // 2, (h % 2) * SEQ + t * P:(h % 2) * SEQ + (t + 1) * P],
                                            qpe[:, t, h, :], ident)
                last.then_inc(qpt_full, 1)
                pe.wait_ge(qpt_done, l + 1)
                pe.wait_ge(kpe_done, l + 1)

                def scores(i):
                    for h in range(4):
                        for t in range(T):
                            o = ps[:, h, t * SEQ:(t + 1) * SEQ]
                            q = slice(t * P, (t + 1) * P)
                            if i < 2:
                                last = mm(o, qkT[:, 4 * i + h, q], qkT[:, 8 + i, :], start=True, stop=True)
                            elif i == 2:
                                mm(o, qnT[:, h, q], knT[:, h, :], start=True, stop=False)
                                last = mm(o, qpT[0:64, h, q], kpT[0:64, :], start=False, stop=True)
                            else:
                                last = mm(o, PF[:, C_Q + h, q], PF[:, C_K + h, :], start=True, stop=True)
                    last.then_inc(s_full, 1)

                scores(0)
                for i in range(4):
                    pe.wait_ge(p_ready, 4 * l + (i + 1))
                    for h in range(4):
                        for kt in range(T):
                            for t in range(T):
                                last = pe.transpose(ps[:, 4 + h, kt * SEQ + t * P:kt * SEQ + (t + 1) * P],
                                                    prob[:, h, t, kt * P:(kt + 1) * P], ident)
                    last.then_inc(t_full, 1)
                    if i < 3:
                        scores(i + 1)
                    pe.wait_ge(pt_done, 8 * l + 2 * (i + 1))
                    for h in range(4):
                        for kt in range(T):
                            v = (PT[:, kt, A_V + i * HD:A_V + (i + 1) * HD] if i < 2 else
                                 vB[:, kt, h * HD:(h + 1) * HD] if i == 2 else
                                 PT[:, kt, C_V + h * HD:C_V + (h + 1) * HD])
                            last = mm(ps[:, 4 + h // 2, (h % 2) * SEQ:(h % 2 + 1) * SEQ], v, probT[:, h, kt, :],
                                      start=(kt == 0), stop=(kt == 1))
                    last.then_inc(pv_full, 1)
                    pe.wait_ge(o_done, 4 * l + (i + 1))
                settle()
                with pe.Fori(0, WO_G // 2) as i:
                    for p in range(2):
                        rows_group(OT, l * LAYER_G + i * 2 + (TM_G + FM_G + LAT_G + p),
                                   l * TM_N + i * 2 + (TM_G + p), p)

            prenorm(LAYERS)
            for i in range(TM2_G):
                rows_group(hT, G_TM2 + i, N_TM2 + i, i % 2)
            for s in range(R):
                unit(G_GATE, s)
            for t in range(T):
                for k in range(KD):
                    last = mm(ps[:, 4, t * NGATE:(t + 1) * NGATE], hT[:, k, t * P:(t + 1) * P],
                              ring[:, 0, k * NGATE:(k + 1) * NGATE], start=(k == 0), stop=(k == KD - 1))
            last.then_inc(unit_done, 4)
            pe.wait_ge(gw_done, 1)
            with pe.Fori(0, FM2_G) as i:
                cols_group(i + G_FM2, i * R + N_FM, hT)
            pe.wait_ge(fm_free, N_WQ + R)
            for w in range(2):
                pe.wait_ge(cin_done, w + 1)
                for u in range(2):
                    unit(G_CMP, 2 * w + u)
                    for j in range(16):
                        last = mm(ps[:, 4 + 3 * w, 0:4 * NCMP], ring[:, 2 * w + u, j * P:(j + 1) * P],
                                  cmp_in[w][:, :, 16 * u + j, :], start=(u == 0 and j == 0), stop=(u == 1 and j == 15))
                    last.then_inc(unit_done, 1)
            pe.wait_ge(hid_done, 1)
            mm(ps[:, 5, 0:4 * NCMP], c3("w2k"), hid[:, 0, 0:4 * NCMP], start=True, stop=True).then_inc(kc_full, 1)
            pe.wait_ge(hid_done, 2)
            for q in range(4):
                last = mm(ps[0:NCMP, 6, q * NSA_D:(q + 1) * NSA_D], hid[:, 1, q * NCMP:(q + 1) * NCMP],
                          c3("w2v"), start=True, stop=True)
            last.then_inc(kc_full, 1)
            pe.wait_ge(kc_done, 2)
            pe.wait_ge(vc_done, 1)
            for t in range(T):
                for h in range(NSA_HEADS):
                    c, half = nsa_chunk(h)
                    at = (t * NSA_HEADS + h) * NCMP
                    last = mm(ps[:, 7, at:at + NCMP], PF2[:, NQ + c, t * P:(t + 1) * P],
                              kcz[:, half * 2 + h // 8, 0:NCMP], start=True, stop=True)
            last.then_inc(cs_full, 1)
            pe.wait_ge(ce_done, 1)
            for j in range(T * NSA_HEADS):
                last = pe.transpose(ps[0:NCMP, j // 4, (j % 4) * P:(j % 4 + 1) * P], cprob[:, j, :], ident)
            last.then_inc(ct_full, 1)
            pe.wait_ge(ct_done, 2)
            for j in range(T * NSA_HEADS):
                h = j % NSA_HEADS
                last = mm(ps[:, j // 8, (j % 8) * NSA_D:(j % 8 + 1) * NSA_D], cprobT[0:NCMP, j, :],
                          vcmp[0:NCMP, nsa_chunk(h)[1] * 2 + h // 8, :], start=True, stop=True)
            last.then_inc(cpv_full, 1)
            pe.wait_ge(co_done, 1)
            pe.wait_ge(kz_done, 1)

            def nscores(i):
                g, br = i // 2, i % 2
                for r in range(4):
                    c, half = nsa_chunk(4 * g + r)
                    k = kz[:, br, half * 2 + g // 2, :]
                    mm(ps[:, r, 0:P], PF2[:, NQ + c, 0:P], k[:, 0:P], start=True, stop=True)
                    last = mm(ps[:, r, P:3 * P], PF2[:, NQ + c, P:SEQ], k, start=True, stop=True)
                last.then_inc(n_full, 1)

            def rscores(i):
                for r in range(4):
                    q, k = PF2[:, RQ + 4 * i + r, :], PF2[:, RK + 4 * i + r, :]
                    mm(ps[:, r, 0:SEQ], k[:, 0:P], q, start=True, stop=True)
                    last = mm(ps[:, r, SEQ:3 * P], k[:, P:SEQ], q[:, P:SEQ], start=True, stop=True)
                last.then_inc(n_full, 1)

            nscores(0)
            for i in range(8):
                g, br = i // 2, i % 2
                pe.wait_ge(n_exp, i + 1)
                for r in range(4):
                    for j in range(3):
                        last = pe.transpose(ps[:, 4 + r, j * P:(j + 1) * P], nprob[i % 2][:, r, j * P:(j + 1) * P], ident)
                last.then_inc(n_t, 1)
                if i < 7:
                    nscores(i + 1)
                else:
                    rscores(0)
                pe.wait_ge(n_pt, 2 * (i + 1))
                v = [PT2[:, kt, (V_W if br else V_S) + g * NSA_D:(V_W if br else V_S) + (g + 1) * NSA_D] for kt in range(2)]
                for r in range(4):
                    mm(ps[:, 4, r * NSA_D:(r + 1) * NSA_D], nprobT[:, r, 0:P], v[0], start=True, stop=True)
                    o = ps[:, 4, (4 + r) * NSA_D:(5 + r) * NSA_D]
                    mm(o, nprobT[:, r, P:2 * P], v[0], start=True, stop=False)
                    last = mm(o, nprobT[:, r, 2 * P:3 * P], v[1], start=False, stop=True)
                last.then_inc(n_pv, 1)
                pe.wait_ge(n_out, i + 1)
            for i in range(2):
                pe.wait_ge(r_ready, i + 1)
                if i == 0:
                    rscores(1)
                else:
                    pe.wait_ge(yret_done, 1)
                for r in range(4):
                    h = 4 * i + r
                    v = [PT2[:, st, V_R + h * HD:V_R + (h + 1) * HD] for st in range(2)]
                    o = ps[:, 4 + r // 2, (r % 2) * SEQ:(r % 2 + 1) * SEQ]
                    a = nprob[i % 2][:, r, :]
                    mm(o[:, 0:P], a[:, 0:P], v[0], start=True, stop=True)
                    mm(o[:, P:SEQ], a[:, P:SEQ], v[0], start=True, stop=False)
                    last = mm(o[:, P:SEQ], a[:, SEQ:3 * P], v[1], start=False, stop=True)
                last.then_inc(n_pv, 1)
            for kind in range(2):
                pe.wait_ge(n_normed, kind + 1)
                if kind == 0:
                    pe.wait_ge(yret_done, 2)
                for c in range(8):
                    for t in range(T):
                        src = (onsa[:, t * NSA_HEADS + 2 * c:t * NSA_HEADS + 2 * c + 2, :].rearrange("p a b -> p (a b)")
                               if kind == 0 else yret[:, t * RET_HEADS + c, :])
                        last = pe.transpose(ps[:, 4 * kind + c // 2, (c % 2) * SEQ + t * P:(c % 2) * SEQ + (t + 1) * P],
                                            src, ident)
                    if c % 2:
                        last.then_inc(ot_full, 1)
            pe.wait_ge(ot_done, 16)
            for i in range(WO_G):
                rows_group(OT2, G_WO2 + i, N_WO2 + i, i % 2)

            def gate_row(j, bank):
                for k in range(KD):
                    last = mm(ps[:, bank + k // 4, (k % 4) * P:(k % 4 + 1) * P],
                              mod[:, j * KD + k:j * KD + k + 1].to_broadcast([P, P]), ident, start=True, stop=True)
                return last

            gate_row(2, 4).then_inc(g1_full, 1)
            prenorm(LAYERS + 1)

            def split(g, c):
                pe.wait_ge(lo_done, (g - G_WQ) * R + (c + 1))

            def up(g, c, n):
                pe.wait_ge(fm_free, n + 1)
                split(g, c)
                o = ps[:, 4 + c, 0:SEQ]
                for k in range(KD):
                    w = slice(k * P, (k + 1) * P)
                    mm(o, wh[:, c % 2, w], hh[:, k, :], start=(k == 0), stop=False)
                    mm(o, wh[:, c % 2, w], hl[:, k, :], start=False, stop=False)
                    last = mm(o, wl[:, c % 2, w], hh[:, k, :], start=False, stop=(k == KD - 1))
                last.then_inc(unit_done, 1)

            def batch(n, b):
                pe.wait_ge(hot_done, n + 1)
                for j in range(BATCH):
                    last = mm(ps[:, b, j * PART:(j + 1) * PART], hot1[:, b, j, :], hot2[:, b, j, :], start=True, stop=True)
                last.then_inc(g_full, 1)

            def up_quarter(q):
                g0, n0 = G_OF[f"U{q}"], N_U + q * PART
                b0 = (q - 1) * PART
                if q > 1:
                    pe.wait_ge(y_used, 2 * (q - 1))
                with pe.Fori(0, PART_G) as i:
                    for c in range(R):
                        if q:
                            batch(i * R + (b0 + c), c % 2)
                        up(i + g0, c, i * R + (n0 + c))

            def down(g, c, first, last_unit):
                split(g, c)
                for t in range(T):
                    tok = slice(t * P, (t + 1) * P)
                    passes = [(stage_h, wh), (stage_h, wl), (stage_l, wh)]
                    for j, (lhs, rhs) in enumerate(passes):
                        for d in range(4):
                            last = mm(ps[:, 4 * t + d, :], lhs[:, c % 2, tok], rhs[:, c % 2, d * 512:(d + 1) * 512],
                                      start=first and j == 0, stop=last_unit and j == 2, skip_group_check=True)
                last.then_inc(unit_done, 1)

            def down_quarter(q):
                pe.wait_ge(g_used, (q + 1) * PART)
                pe.wait_ge(fm_free, N_U + min(q + 2, PARTS) * PART + R)
                g0 = G_OF[f"V{q}"]
                for c in range(R):
                    down(g0, c, c == 0, False)
                with pe.Fori(g0 + 1, g0 + PART_G - 1) as g:
                    for c in range(R):
                        down(g, c, False, False)
                for c in range(R):
                    down(g0 + PART_G - 1, c, False, c == R - 1)

            pe.wait_ge(hl_done, 2)
            with pe.Fori(0, WQ_G) as i:
                for c in range(R):
                    up(i + G_WQ, c, i * R + (N_WQ + c))
            pe.wait_ge(fm_free, N_U + R)
            pe.wait_ge(keys_ready, 16)
            for t in range(T):
                for j in range(16):
                    last = mm(ps[:, 4 * t + j // 4, (j % 4) * P:(j % 4 + 1) * P], qP[:, j, t * P:(t + 1) * P],
                              keyT[:, j, :], start=True, stop=True)
            last.then_inc(sc_full, 1)
            pe.wait_ge(sc_done, 2)
            gate_row(5, 0).then_inc(g2_full, 1)
            up_quarter(0)
            pe.wait_ge(g2_done, 1)
            pe.wait_ge(routed, T)
            for a in range(3):
                for t in range(T):
                    last = pe.transpose(ps[:, a, t * P:(t + 1) * P], route[:, a, t, :], ident)
            last.then_inc(rt_full, 1)
            up_quarter(1)
            down_quarter(0)
            up_quarter(2)
            down_quarter(1)
            up_quarter(3)
            down_quarter(2)
            pe.wait_ge(y_used, 2 * (PARTS - 1))
            with pe.Fori(0, PART // 2) as i:
                for b in range(2):
                    batch(i * 2 + ((PARTS - 1) * PART + b), b)
            down_quarter(PARTS - 1)

        @blk.scalar
        def _(act):
            def f(o, i, func, **kw):
                return nc.scalar.activation(o, i, func, **kw)

            def prenorm(i, scale, shift=None):
                act.wait_ge(x_done, T * (i + 1))
                for t in range(T):
                    f(Xn[:, t, :], X[:, t, :], ACT.Square, accum_out=ss2[:, t:t + 1]).then_inc(sq_done, 1)
                for b in range(1, 8, 2):
                    act.wait_ge(ht_full, 8 * i + (b + 1))
                    for kk in range(2):
                        k = 2 * b + kk
                        o, src = hT[:, k, :], ps[:, b, kk * SEQ:(kk + 1) * SEQ]
                        if shift is None:
                            ins = f(o, src, ACT.Copy, scale=scale(k))
                        else:
                            ins = f(o, src, ACT.Identity, scale=scale(k), bias=shift(k))
                        ins.then_inc(ht_done, 1)

            def rows_out(dst, g, col, pair):
                act.wait_ge(unit_done, g * R + R)
                f(dst[:, :, bass.ds(col, 512)], ps[:, 2 * pair:2 * pair + 2, :], ACT.Copy).then_inc(tm_free, 1)

            def cols_out(dst, g, chunk, func):
                for c in range(R):
                    act.wait_ge(unit_done, g * R + (c + 1))
                    f(dst[:, chunk + c, :], ps[:, 4 + c, 0:SEQ], func).then_inc(fm_free, 1)

            act.wait_ge(loaded, 32)
            f(csilu[:, :], small_of("cond"), ACT.Silu).then_inc(c_ready, 1)
            with act.Fori(0, LAYERS) as l:
                prenorm(l, lambda k: gcol[:, k:k + 1])
                with act.Fori(0, TM_G // 2) as i:
                    for p in range(2):
                        rows_out(PT, l * LAYER_G + i * 2 + p, i * 1024 + p * 512, p)
                with act.Fori(0, GATE_CHUNKS // R) as i:
                    cols_out(PF, l * LAYER_G + i + TM_G, i * R, ACT.Silu)
                with act.Fori(GATE_CHUNKS // R, FM_G) as i:
                    cols_out(PF, l * LAYER_G + i + TM_G, i * R, ACT.Copy)
                for b in range(0, 5, 2):
                    act.wait_ge(tr_full, 8 * l + (b + 1))
                    f(qkT[:, 2 * b:2 * b + 2, :], ps[:, b, :], ACT.Copy).then_inc(tr_done, 1)
                gl = l * LAYER_G + TM_G + FM_G
                act.wait_ge(unit_done, gl * R + 1)
                f(qnT, ps[:, 0:2, :], ACT.Copy).then_inc(lat_done, 1)
                act.wait_ge(unit_done, gl * R + 4)
                f(knT, ps[:, 2:4, :], ACT.Copy).then_inc(lat_done, 1)
                f(vB, ps[:, 5:7, :], ACT.Copy).then_inc(lat_done, 1)

                def exps(i):
                    act.wait_ge(nb_done, 4 * l + (i + 1))
                    if i:
                        act.wait_ge(t_full, 4 * l + i)
                    scale = {0: HD ** -0.5, 1: HD ** -0.5, 2: (HD + 64) ** -0.5, 3: 1.0}[i]
                    for h in range(4):
                        for t in range(T):
                            src = prob[:, h, t, :] if i == 3 else ps[:, h, t * SEQ:(t + 1) * SEQ]
                            last = f(prob[:, h, t, :], src, ACT.Exp, scale=scale,
                                     bias=nb[:, i % 2, 2 * h + t:2 * h + t + 1],
                                     accum_out=rs[:, i % 2, 2 * h + t:2 * h + t + 1])
                    last.then_inc(exp_done, 1)

                exps(0)
                for i in range(4):
                    act.wait_ge(t_full, 4 * l + (i + 1))
                    f(probT[:, 0:2], ps[:, 4:6, :], ACT.Copy).then_inc(pt_done, 1)
                    if i < 3:
                        exps(i + 1)
                with act.Fori(0, WO_G // 2) as i:
                    for p in range(2):
                        rows_out(Y, l * LAYER_G + i * 2 + (TM_G + FM_G + LAT_G + p), i * 1024 + p * 512, p)
                act.wait_ge(tm_free, (l + 1) * TM_N + 2)
                for t in range(T):
                    f(lsquares[:, t, :], Y[:, t, :], ACT.Square, accum_out=ss2[:, t:t + 1]).then_inc(ysq_done, 1)

            act.wait_ge(gsc_done, 1)
            prenorm(LAYERS, lambda k: gsc[:, 0, k:k + 1], lambda k: mod[:, k:k + 1])
            for i in range(TM2_G):
                rows_out(PT2, G_TM2 + i, i * 512, i % 2)
            act.wait_ge(unit_done, G_GATE * R + 4)
            f(gw, ps[:, 4, 0:T * NGATE], ACT.Sigmoid).then_inc(gw_done, 1)
            with act.Fori(0, RG // R) as i:
                cols_out(PF2, i + G_FM2, i * R, ACT.Copy)
            with act.Fori(RG // R, FM2_G) as i:
                cols_out(PF2, i + G_FM2, i * R, ACT.Silu)
            for w in range(2):
                act.wait_ge(unit_done, G_CMP * R + 2 * (w + 1))
                f(hid[:, w, 0:4 * NCMP], ps[:, 4 + 3 * w, 0:4 * NCMP], ACT.Gelu_apprx_tanh).then_inc(hid_done, 1)
            act.wait_ge(cs_done, 1)
            f(cprob, cprob, ACT.Exp).then_inc(ce_done, 1)
            act.wait_ge(ct_full, 1)
            f(cprobT[0:NCMP, 0:16, :], ps[0:NCMP, 0:4, :], ACT.Copy).then_inc(ct_done, 1)

            def nexps(i):
                act.wait_ge(n_nb, i + 1)
                for t in range(T):
                    for r in range(4):
                        p = nprob[i % 2][:, r, 0:P] if t == 0 else nprob[i % 2][:, r, P:3 * P]
                        j = 4 * t + r
                        last = f(p, p, ACT.Exp, scale=NSA_D ** -0.5, bias=nb[:, i % 2, j:j + 1],
                                 accum_out=rs[:, i % 2, j:j + 1])
                last.then_inc(n_exp, 1)

            nexps(0)
            for i in range(8):
                act.wait_ge(n_t, i + 1)
                f(nprobT[:, 0:2, :], ps[:, 4:6, 0:3 * P], ACT.Copy).then_inc(n_pt, 1)
                if i < 7:
                    nexps(i + 1)
            for i in range(2):
                act.wait_ge(n_pv, 8 + i + 1)
                src = ps[:, 4:6, :].rearrange("p b (r t e) -> p t (b r) e", r=2, t=T)
                for t in range(T):
                    last = f(yret[:, t * RET_HEADS + 4 * i:t * RET_HEADS + 4 * i + 4, :], src[:, t], ACT.Copy)
                last.then_inc(yret_done, 1)
            for c in range(8):
                act.wait_ge(ot_full, c // 2 + 1)
                f(OT2[:, c, :], ps[:, c // 2, (c % 2) * SEQ:(c % 2 + 1) * SEQ], ACT.Copy,
                  scale=c3("g_nsa")[:, c:c + 1]).then_inc(ot_done, 1)
            for i in range(WO_G):
                rows_out(Y, G_WO2 + i, i * 512, i % 2)
            act.wait_ge(gsc_done, 2)
            prenorm(LAYERS + 1, lambda k: gsc[:, 1, k:k + 1], lambda k: mod[:, 3 * KD + k:3 * KD + k + 1])
            act.wait_ge(ht_done, KD * (LAYERS + 2))
            for half in range(2):
                k = slice(half * 8, half * 8 + 8)
                f(hh[:, k, :], hT[:, k, :], ACT.Copy).then_inc(hh_done, 1)

            def high(g, c):
                act.wait_ge(w_ready[c], 16 * (g + 1))
                act.wait_ge(unit_done, g * R + (c - 1))
                return f(wh[:, c % 2, :], ring[:, c, :], ACT.Copy)

            def high_v(g, c, q):
                high(g, c)
                chunk = (g - G_OF[f"V{q}"]) * R + c
                f(stage_h[:, c % 2, :], act_e[q % 2][:, chunk, :], ACT.Copy).then_inc(hi_done, 1)

            def up_out(dst, g, c, chunk, func):
                act.wait_ge(unit_done, g * R + (c + 1))
                f(dst[:, chunk, :], ps[:, 4 + c, 0:SEQ], func).then_inc(fm_free, 1)

            def up_slots(dst, g, chunk, func):
                for c in range(R):
                    high(g + (c + 1) // R, (c + 1) % R).then_inc(hi_done, 1)
                    up_out(dst, g, c, chunk + c, func)

            def down_slots(g, q):
                for c in range(R):
                    high_v(g + (c + 1) // R, (c + 1) % R, q)

            def up_quarter(q):
                g0, dst = G_OF[f"U{q}"], act_e[q % 2]
                if q > 1:
                    act.wait_ge(unit_done, g0 * R)
                    f(ysum[q % 2][:, 0, :], ps[:, 0:4, :], ACT.Copy).then_inc(y_used, 1)
                up_slots(dst, g0, 0, ACT.Gelu_apprx_tanh)
                if q == 0:
                    act.wait_ge(g2_full, 1)
                    f(gate2row, ps[:, 0:4, :], ACT.Copy).then_inc(g2_done, 1)
                with act.Fori(1, PART_G - 1) as i:
                    up_slots(dst, i + g0, i * R, ACT.Gelu_apprx_tanh)
                g, chunk = g0 + PART_G - 1, PART - R
                for c in range(R - 1):
                    high(g, c + 1).then_inc(hi_done, 1)
                    up_out(dst, g, c, chunk + c, ACT.Gelu_apprx_tanh)
                if q == 0:
                    high(g + 1, 0).then_inc(hi_done, 1)
                    for t in range(T):
                        act.wait_ge(rexp_in, t + 1)
                        f(route[:, 2, t, :], route[:, 2, t, :], ACT.Exp).then_inc(rexp_done, 1)
                    act.wait_ge(unit_done, g * R + R)
                else:
                    high(g + 1, 0)
                    act.wait_ge(g_used, q * PART)
                    f(stage_h[:, 0, :], act_e[(q - 1) % 2][:, 0, :], ACT.Copy).then_inc(hi_done, 1)
                up_out(dst, g, R - 1, chunk + R - 1, ACT.Gelu_apprx_tanh)

            def down_quarter(q):
                g0 = G_OF[f"V{q}"]
                with act.Fori(g0, g0 + PART_G - 1) as g:
                    down_slots(g, q)
                g = g0 + PART_G - 1
                for c in range(R - 1):
                    high_v(g, c + 1, q)
                if q < PARTS - 2:
                    high(g + 1, 0).then_inc(hi_done, 1)

            high(G_WQ, 0).then_inc(hi_done, 1)
            with act.Fori(0, WQ_G) as i:
                up_slots(qP, i + G_WQ, i * R, ACT.Copy)
            act.wait_ge(sc_full, 1)
            f(score[:, 0], ps[:, 0:4, :], ACT.Copy).then_inc(sc_done, 1)
            up_quarter(0)
            act.wait_ge(routed, T)
            up_quarter(1)
            down_quarter(0)
            up_quarter(2)
            down_quarter(1)
            up_quarter(3)
            down_quarter(2)
            act.wait_ge(unit_done, G_OF["V3"] * R)
            f(ysum[0][:, 0, :], ps[:, 0:4, :], ACT.Copy).then_inc(y_used, 1)
            high(G_OF["V3"], 0)
            act.wait_ge(g_used, PARTS * PART)
            f(stage_h[:, 0, :], act_e[1][:, 0, :], ACT.Copy).then_inc(hi_done, 1)
            down_quarter(3)
            act.wait_ge(unit_done, GROUPS * R)
            f(ysum[1][:, 0, :], ps[:, 0:4, :], ACT.Copy).then_inc(y_used, 1)
            act.wait_ge(x_done, T * (LAYERS + 2 + PARTS))
            for t in range(T):
                f(squares[:, t, :], X[:, t, :], ACT.Square, accum_out=ss2[:, t:t + 1]).then_inc(fss_done, 1)

        @blk.gpsimd
        def _(pool):
            steps = Steps(pool, pool_step)
            pl = nc.gpsimd

            def rsqrt(parts, mean, out_ap, signal):
                pool.sem_inc(pool_passed, 1)
                for o, src, n in parts:
                    steps(pl.tensor_scalar(o, src, 1.0 / n, EPS, ALU.mult, ALU.add))
                steps.done()
                pl.tensor_tensor(out_ap, mean, power[:, 0:mean.shape[-1]], ALU.pow).then_inc(signal, 1)

            def rstd_of(i, wait_sem, signal):
                pool.wait_ge(wait_sem, T * (i + 1))
                rsqrt([(ms2, ss2, DM)], ms2, rstd2, signal)

            pool.dma_start(area(C1, CONST1_W), const1).then_inc(c1_ready, 16)
            pool.wait_ge(loaded, 32)
            with pool.Fori(0, LAYERS) as l:
                steps.region(l * POOL_STEPS)
                pool.wait_ge(x_done, T * (l + 1))
                pool.dma_start(nbias, nbr_bias[l]).then_inc(bias_ready, 16)
                pool.dma_start(gpost, g_post[l]).then_inc(gpost_ready, 16)
                rstd_of(l, sq_done, prs_done)

                def modulation(first, end):
                    with pool.Fori(first, end) as i:
                        for h in range(ADA_H):
                            cg = l * ADA_PER_LAYER + i
                            pool.wait_ge(a_used, cg * ADA_H + (h + 1))
                            pool.dma_start(aring[:, h % 2, :], ada[cg, h]).then_inc(a_ready[h % 2], 16)

                modulation(0, ADA_EARLY)
                pool.wait_ge(bias_ready, 16 * l + 16)
                pool.wait_ge(c1_ready, 16)
                nb8 = nbias.rearrange("p a b c -> p (a b) c")
                pl.tensor_tensor(nb8, nb8, c1("nbr")[:, None, :].to_broadcast([P, 8, SEQ]), ALU.add).then_inc(bias_masked, 1)
                pool.wait_ge(qss_done, l + 1)
                rsqrt([(msq[:, 0:20], ssq[:, 0:20], HD), (msq[:, 20:22], ssq[:, 20:22], 512),
                       (msq[:, 22:24], ssq[:, 22:24], 256)], msq, rsq, qrs_done)
                modulation(ADA_EARLY, ADA_PER_LAYER)
                rstd_of(l, ysq_done, yrs_done)
                assert steps.n == POOL_STEPS, steps.n
            steps.region(LAYERS * POOL_STEPS)
            pool.wait_ge(x_done, T * (LAYERS + 1))
            pool.dma_start(area(C2, CONST2_W), const2).then_inc(c2_ready, 16)
            pool.dma_start(area(C3, CONST3_W), const3).then_inc(c2_ready, 16)
            pl.memset(area(22368, 2048 + 3840 + 64), 0.0).then_inc(zeroed, 1)
            rstd_of(LAYERS, sq_done, prs_done)
            pool.wait_ge(nss_done, 1)
            rsqrt([(hs, hs, NSA_D)], hs, cw, nrs_done)
            pool.wait_ge(nss_done, 2)
            rsqrt([(hs[:, 0:16], hs[:, 0:16], HD)], hs[:, 0:16], cw[:, 0:16], nrs_done)
            rstd_of(LAYERS + 1, sq_done, prs_done)
            pool.wait_ge(fss_done, T)
            rsqrt([(ms2, ss2, DM)], ms2, rstd2, frs_done)

        @blk.vector
        def _(dve):
            v = nc.vector
            st = Steps(dve, dve_step)
            tt, ts, stt = v.tensor_tensor, v.tensor_scalar, v.scalar_tensor_tensor

            def prenorm(i, scale, shift=None):
                dve.wait_ge(prs_done, i + 1)
                for t in range(T):
                    ts(Xn[:, t, :], X[:, t, :], rstd2[:, t:t + 1], None, ALU.mult).then_inc(xn_done, 1)
                for b in range(0, 8, 2):
                    dve.wait_ge(ht_full, 8 * i + (b + 1))
                    for kk in range(2):
                        k = 2 * b + kk
                        o, src = hT[:, k, :], ps[:, b, kk * SEQ:(kk + 1) * SEQ]
                        if shift is None:
                            ins = ts(o, src, scale(k), None, ALU.mult)
                        else:
                            ins = ts(o, src, scale(k), shift(k), ALU.mult, ALU.add)
                        ins.then_inc(ht_done, 1)

            def rotate(dst, src, tmp, cos, sin, heads, half):
                def split(a):
                    return a.rearrange("p h (a s n) -> p h a s n", a=2, s=2)
                n = cos.shape[-1]
                c3 = cos[:, None, :].to_broadcast([P, heads, n])
                s5 = sin.rearrange("p (a s n) -> p a s n", a=2, s=2)
                for s in range(2):
                    st(tt(split(tmp)[:, :, :, s, :], split(src)[:, :, :, 1 - s, :],
                          s5[:, None, :, s, :].to_broadcast([P, heads, 2, half]), ALU.mult))
                st.done()
                st(tt(dst, src, c3, ALU.mult))
                st.done()
                return tt(dst, dst, tmp, ALU.add)

            dve.wait_ge(loaded, 32)
            dve.sem_inc(tm_free, 2)
            dve.sem_inc(fm_free, 4)
            dve.sem_inc(a_used, 2)
            dve.sem_inc(x_done, 2)
            dve.wait_ge(c_ready, 1)
            dve.wait_ge(c1_ready, 16)
            with dve.Fori(0, LAYERS) as l:
                st.region(l * DVE_STEPS)
                st(v.tensor_copy(gcol, g_pre[:, l, :]))
                st(v.tensor_copy(glat[:, 0:4], g_cq[:, l, :]))
                st(v.tensor_copy(glat[:, 4:6], g_ckv[:, l, :]))
                st.done()
                prenorm(l, lambda k: gcol[:, k:k + 1])

                def modulation(first, end):
                    with dve.Fori(first, end) as i:
                        for h in range(ADA_H):
                            cg = l * ADA_PER_LAYER + i
                            dve.wait_ge(a_ready[h % 2], cg * 64 + 16 * (h // 2 + 1))
                            for kk in range(2):
                                w = aring[:, h % 2, kk * 512:(kk + 1) * 512]
                                k = 2 * h + kk
                                if k == 0:
                                    ins = ts(acc[:, i, :], w, csilu[:, k:k + 1], None, ALU.mult)
                                else:
                                    if kk:
                                        dve.wait_ge(a_step, cg * ADA_H + (h + 1))
                                    else:
                                        dve.wait_ge(a_used, cg * ADA_H + (h + 2))
                                    ins = stt(acc[:, i, :], w, csilu[:, k:k + 1], acc[:, i, :], ALU.mult, ALU.add)
                                ins.then_inc(a_used if kk else a_step, 1)

                modulation(0, ADA_EARLY)

                dve.wait_ge(tm_free, l * TM_N + (TM_G + 2))
                for t, sq in ((0, rot1), (1, rot2)):
                    qk = PT[:, t, 0:QK_HEADS * HD].rearrange("p (h d) -> p h d", d=HD)
                    st(tt(sq, qk, qk, ALU.mult))
                    cq, ckv = PT[:, t, B_CQ:B_CQ + 512], PT[:, t, B_CKV:B_CKV + 256]
                    st(stt(junk, cq, 1.0, cq, ALU.mult, ALU.mult, accum_out=ssq[:, 20 + t:21 + t]))
                    st.done()
                    st(stt(junk[:, 0:256], ckv, 1.0, ckv, ALU.mult, ALU.mult, accum_out=ssq[:, 22 + t:23 + t]))
                    st(v.tensor_reduce(ssq[:, 10 * t:10 * t + 10], sq, AX, ALU.add))
                    st.done()
                dve.sem_inc(qss_done, 1)
                dve.wait_ge(qrs_done, l + 1)
                for t in range(T):
                    for at, n, j in ((B_CQ, 512, 20), (B_CKV, 256, 22)):
                        st(ts(PT[:, t, at:at + n], PT[:, t, at:at + n], rsq[:, j + t:j + t + 1], None, ALU.mult))
                for t in range(T):
                    rotate(krot[:, 0, t:t + 1, :], PT[:, t:t + 1, B_KR:B_KR + 64], krot[:, 1, t:t + 1, :],
                           c1("cos_b", T, 64)[:, t, :], c1("sin_b", T, 64)[:, t, :], 1, 16).then_inc(dve_step, 1)
                    st.n += 1
                g_qk = c1("g_qk", LAYERS, 2, HD)
                for t in range(T):
                    qk = PT[:, t, 0:QK_HEADS * HD].rearrange("p (h d) -> p h d", d=HD)
                    st(tt(rot1, qk, rsq[:, 10 * t:10 * t + 10].unsqueeze(2).to_broadcast([P, QK_HEADS, HD]), ALU.mult))
                    st.done()
                    st(tt(rot1[:, 0:8], rot1[:, 0:8], g_qk[:, l, 0, :].unsqueeze(1).to_broadcast([P, 8, HD]), ALU.mult))
                    st(tt(rot1[:, 8:10], rot1[:, 8:10], g_qk[:, l, 1, :].unsqueeze(1).to_broadcast([P, 2, HD]), ALU.mult))
                    st.done()
                    rotate(qk, rot1, rot2, c1("cos", T, HD)[:, t, :], c1("sin", T, HD)[:, t, :], QK_HEADS, 32).then_inc(qk_ready, 1)
                    if t == 0:
                        dve.wait_ge(qk_ready, l * 2 + 1)
                modulation(ADA_EARLY, ADA_PER_LAYER)
                dve.wait_ge(mod_full, l + 1)
                tt(mod[:, bass.ds(l * 48, 48)], ps[:, 4, 0:48], small_of("b_ada")[:, bass.ds(l * 48, 48)],
                   ALU.add).then_inc(mod_done, 1)
                for b in (1, 3):
                    dve.wait_ge(tr_full, 8 * l + (b + 1))
                    v.tensor_copy(qkT[:, 2 * b:2 * b + 2, :], ps[:, b, :].rearrange("p (a b) -> p a b", a=2)).then_inc(tr_done, 1)
                for k in range(6):
                    dve.wait_ge(tr_full, 8 * l + (6 + k // 2))
                    o = cqT[:, k, :] if k < 4 else ckvT[:, k - 4, :]
                    ts(o, ps[:, 5 + k // 2, (k % 2) * SEQ:(k % 2 + 1) * SEQ], glat[:, k:k + 1], None,
                       ALU.mult).then_inc(tr_done, 1)
                gl = l * LAYER_G + TM_G + FM_G
                dve.wait_ge(unit_done, gl * R + 2)
                for t in range(T):
                    ins = rotate(qpe[:, t], ps[:, 4, t * 256:(t + 1) * 256].rearrange("p (h n) -> p h n", h=4), qpe2[:, t],
                                 c1("cos_b", T, 64)[:, t, :], c1("sin_b", T, 64)[:, t, :], 4, 16)
                    if t < T - 1:
                        st(ins)
                    else:
                        st.done()
                        ins.then_inc(qpe_ready, 1)
                dve.wait_ge(kpe_full, l + 1)
                v.tensor_copy(kpT[0:64, :], ps[0:64, 7, 0:SEQ]).then_inc(kpe_done, 1)
                dve.wait_ge(qpt_full, l + 1)
                v.tensor_copy(qpT[0:64].rearrange("p a b -> p (a b)"), ps[0:64, 0:2, :].rearrange("p a b -> p (a b)")).then_inc(qpt_done, 1)

                def maxima(i):
                    dve.wait_ge(s_full, 4 * l + (i + 1))
                    src = ps[:, 0:4, :].rearrange("p h (t k) -> p (h t) k", t=T)
                    p8 = prob.rearrange("p h t k -> p (h t) k")
                    scale = {0: HD ** -0.5, 1: HD ** -0.5, 2: (HD + 64) ** -0.5, 3: 1.0}[i]
                    if i == 3:
                        dve.wait_ge(bias_masked, l + 1)
                        dve.wait_ge(t_full, 4 * l + 3)
                        stt(prob.rearrange("p h t k -> p (h t k)"), ps[:, 0:4, :].rearrange("p h k -> p (h k)"), HD ** -0.5,
                            nbias.rearrange("p h t k -> p (h t k)"), ALU.mult, ALU.add).then_inc(s_masked, 1)
                        dve.wait_ge(s_masked, l + 1)
                        src = p8
                    st(v.tensor_reduce(mx[:, i % 2, :], src, AX, ALU.max))
                    st.done()
                    ts(nb[:, i % 2, :], mx[:, i % 2, :], -scale, None, ALU.mult).then_inc(nb_done, 1)

                maxima(0)
                for i in range(4):
                    dve.wait_ge(exp_done, 4 * l + (i + 1))
                    st(v.reciprocal(rinv[:, i % 2, :], rs[:, i % 2, :]))
                    st.done()
                    p8 = prob.rearrange("p h t k -> p (h t) k")
                    tt(p8, p8, rinv[:, i % 2, :].unsqueeze(2).to_broadcast([P, 8, SEQ]), ALU.mult).then_inc(p_ready, 1)
                    dve.wait_ge(t_full, 4 * l + (i + 1))
                    v.tensor_copy(probT[:, 2:4].rearrange("p h t k -> p (h t k)"),
                                  ps[:, 6:8, :].rearrange("p h k -> p (h k)")).then_inc(pt_done, 1)
                    if i < 3:
                        maxima(i + 1)
                    dve.wait_ge(pv_full, 4 * l + (i + 1))
                    heads = slice(4 * i, 4 * i + 4)
                    tt(OT[:, heads, :].rearrange("p h k -> p (h k)"), ps[:, 4:6, :].rearrange("p h k -> p (h k)"),
                       PF[:, heads, :].rearrange("p h k -> p (h k)"), ALU.mult).then_inc(o_done, 1)

                dve.wait_ge(yrs_done, l + 1)
                dve.wait_ge(gpost_ready, 16 * l + 16)
                for t in range(T):
                    st(stt(Y[:, t, :], Y[:, t, :], rstd2[:, t:t + 1], gpost, ALU.mult, ALU.mult))
                st.done()
                for t in range(T):
                    tt(X[:, t, :], X[:, t, :], Y[:, t, :], ALU.add).then_inc(x_done, 1)
                dve.wait_ge(x_done, T * l + 2 * T)
                assert st.n == DVE_STEPS, st.n

            st.region(LAYERS * DVE_STEPS)
            dve.wait_ge(mod_done, LAYERS)
            for a, (row, j) in enumerate(((LAYERS, 1), (LAYERS + 1, 4))):
                stt(gsc[:, a, :], mod[:, j * KD:(j + 1) * KD], 1.0, g_pre[:, row, :], ALU.add, ALU.mult).then_inc(gsc_done, 1)
            dve.wait_ge(gsc_done, 2)
            prenorm(LAYERS, lambda k: gsc[:, 0, k:k + 1], lambda k: mod[:, k:k + 1])
            dve.wait_ge(c2_ready, 32)
            dve.wait_ge(zeroed, 1)
            dve.wait_ge(fm_free, N_WQ + R)
            pe_cols = c3("pe", 2, CMP_LEN)
            for w, chunk in ((0, KC), (1, VC)):
                for half in range(2):
                    rows = slice(half * 64, half * 64 + 64)
                    for gp in range(2):
                        for a in range(2):
                            src = PF2[rows, chunk + gp, :].rearrange("p (n b) -> p b n", b=16)[:, :, a:a + NCMP]
                            last = tt(cmp_in[w][rows, half * 2 + gp, 16 * a:16 * a + 16, :], src,
                                      pe_cols[rows, w, 16 * a:16 * a + 16].unsqueeze(2).to_broadcast([64, 16, NCMP]), ALU.add)
                last.then_inc(cin_done, 1)
            for br, chunk in ((0, KS), (1, KW)):
                for half in range(2):
                    rows = slice(half * 64, half * 64 + 64)
                    last = v.tensor_copy(kz[rows, br, half * 2:half * 2 + 2, :], PF2[rows, chunk:chunk + 2, :])
            last.then_inc(kz_done, 1)
            dve.wait_ge(kc_full, 1)
            for half in range(2):
                rows = slice(half * 64, half * 64 + 64)
                v.tensor_copy(kcz[rows, half * 2:half * 2 + 2, 0:NCMP],
                              ps[rows, 5, half * 2 * NCMP:(half * 2 + 2) * NCMP].rearrange("p (a b) -> p a b", a=2)).then_inc(kc_done, 1)
            dve.wait_ge(kc_full, 2)
            v.tensor_copy(vcmp[0:NCMP].rearrange("p a b -> p (a b)"), ps[0:NCMP, 6, 0:4 * NSA_D]).then_inc(vc_done, 1)
            dve.wait_ge(cs_full, 1)
            cp = cprob.rearrange("p a b -> p (a b)")
            st(stt(cp, ps[:, 7, 0:T * NSA_HEADS * NCMP], NSA_D ** -0.5, c2("cmp_bias"), ALU.mult, ALU.add))
            st.done()
            st(v.tensor_reduce(cmx, cprob, AX, ALU.max))
            st.done()
            tt(cprob, cprob, cmx.unsqueeze(2).to_broadcast([P, 32, NCMP]), ALU.subtract).then_inc(cs_done, 1)
            dve.wait_ge(ce_done, 1)
            dve.wait_ge(gw_done, 1)
            st(v.tensor_reduce(crs, cprob, AX, ALU.add))
            st.done()
            st(v.reciprocal(cmx, crs))
            st.done()
            gwv = gw.rearrange("p t (h b) -> p t h b", b=3)
            for t in range(T):
                cols = slice(t * NSA_HEADS, (t + 1) * NSA_HEADS)
                st(stt(cw[:, cols], cmx[:, cols], c3("row_ok")[:, t:t + 1], gwv[:, t, :, 0], ALU.mult, ALU.mult))
            dve.wait_ge(ct_full, 1)
            v.tensor_copy(cprobT[0:NCMP, 16:32, :].rearrange("p a b -> p (a b)"),
                          ps[0:NCMP, 4:8, :].rearrange("p a b -> p (a b)")).then_inc(ct_done, 1)
            dve.wait_ge(cpv_full, 1)
            st.done()
            tt(onsa, ps[:, 0:4, :].rearrange("p b (j d) -> p (b j) d", d=NSA_D),
               cw.unsqueeze(2).to_broadcast([P, 32, NSA_D]), ALU.mult).then_inc(co_done, 1)
            dve.wait_ge(co_done, 1)

            dist = c2("dist")

            def nmax(i):
                g = i // 2
                dve.wait_ge(n_full, i + 1)
                if i >= 2:
                    dve.wait_ge(n_t, i - 1)
                buf = nprob[i % 2]
                for r in range(4):
                    st(stt(buf[:, r, :], dist, float(-SLOPES[4 * g + r] * NSA_D ** 0.5), ps[:, r, 0:3 * P], ALU.mult, ALU.add))
                st.done()
                st(v.tensor_reduce(mx[:, i % 2, 0:4], buf[:, :, 0:P], AX, ALU.max))
                st(v.tensor_reduce(mx[:, i % 2, 4:8], buf[:, :, P:3 * P], AX, ALU.max))
                st.done()
                ts(nb[:, i % 2, :], mx[:, i % 2, :], -NSA_D ** -0.5, None, ALU.mult).then_inc(n_nb, 1)

            def retain(i):
                dve.wait_ge(n_full, 8 + i + 1)
                dve.wait_ge(n_t, 7 + i)
                decay = c2("decay", RET_HEADS, 3 * P)[:, 4 * i:4 * i + 4, :]
                tt(nprob[i % 2], ps[:, 0:4, 0:3 * P], decay, ALU.mult).then_inc(r_ready, 1)

            nmax(0)
            for i in range(8):
                g, br = i // 2, i % 2
                dve.wait_ge(n_exp, i + 1)
                st(v.reciprocal(rinv[:, i % 2, :], rs[:, i % 2, :]))
                st.done()
                wts = rinv[:, i % 2, :].rearrange("p (t r) -> p t r", t=T)
                st(tt(wts, wts, gwv[:, :, 4 * g:4 * g + 4, 1 + br], ALU.mult))
                dve.wait_ge(n_t, i + 1)
                v.tensor_copy(nprobT[:, 2:4, :], ps[:, 6:8, 0:3 * P]).then_inc(n_pt, 1)
                if i < 7:
                    nmax(i + 1)
                else:
                    retain(0)
                dve.wait_ge(n_pv, i + 1)
                st.done()
                st(tt(ntmp.rearrange("p t r d -> p (t r) d"), ps[:, 4, :].rearrange("p (j d) -> p j d", d=NSA_D),
                      rinv[:, i % 2, :].unsqueeze(2).to_broadcast([P, 8, NSA_D]), ALU.mult))
                st.done()
                o = onsa.rearrange("p (t h) d -> p t (h d)", t=T)[:, :, 4 * g * NSA_D:(4 * g + 4) * NSA_D]
                tt(o, o, ntmp.rearrange("p t r d -> p t (r d)"), ALU.add).then_inc(n_out, 1)
                dve.wait_ge(n_out, i + 1)
            retain(1)
            sq32 = area(22368, 32, NSA_D)
            st(tt(sq32, onsa, onsa, ALU.mult))
            st.done()
            v.tensor_reduce(hs, sq32, AX, ALU.add).then_inc(nss_done, 1)
            dve.wait_ge(nrs_done, 1)
            tt(onsa, onsa, cw.unsqueeze(2).to_broadcast([P, 32, NSA_D]), ALU.mult).then_inc(n_normed, 1)
            dve.wait_ge(yret_done, 2)
            st(v.tensor_reduce(crs[:, 0:16], yret, AX, ALU.add))
            st.done()
            st(ts(crs[:, 0:16], crs[:, 0:16], 1.0 / HD, None, ALU.mult))
            st.done()
            st(tt(yret, yret, crs[:, 0:16].unsqueeze(2).to_broadcast([P, 16, HD]), ALU.subtract))
            st.done()
            dve.wait_ge(n_normed, 1)
            sq16 = area(22368, 16, HD)
            st(tt(sq16, yret, yret, ALU.mult))
            st.done()
            v.tensor_reduce(hs[:, 0:16], sq16, AX, ALU.add).then_inc(nss_done, 1)
            dve.wait_ge(nrs_done, 2)
            tt(yret, yret, cw[:, 0:16].unsqueeze(2).to_broadcast([P, 16, HD]), ALU.mult).then_inc(n_normed, 1)
            for c in range(8):
                dve.wait_ge(ot_full, 4 + c // 2 + 1)
                stt(OT2[:, 8 + c, :], ps[:, 4 + c // 2, (c % 2) * SEQ:(c % 2 + 1) * SEQ], c3("g_ret")[:, c:c + 1],
                    PF2[:, RG + c, :], ALU.mult, ALU.mult).then_inc(ot_done, 1)
            dve.wait_ge(tm_free, N_WO2 + WO_G + 2)
            dve.wait_ge(g1_full, 1)
            row = ps[:, 4:8, :].rearrange("p a b -> p (a b)")
            for t in range(T):
                st(tt(Y[:, t, :], Y[:, t, :], row, ALU.mult))
            st.done()
            for t in range(T):
                tt(X[:, t, :], X[:, t, :], Y[:, t, :], ALU.add).then_inc(x_done, 1)
            dve.wait_ge(x_done, T * (LAYERS + 2))

            prenorm(LAYERS + 1, lambda k: gsc[:, 1, k:k + 1], lambda k: mod[:, 3 * KD + k:3 * KD + k + 1])

            def low(g, c):
                dve.wait_ge(hi_done, (g - G_WQ) * R + (c + 1))
                return tt(wl[:, c % 2, :], ring[:, c, :], wh[:, c % 2, :].bitcast(F32), ALU.subtract)

            def low_v(g, c, q):
                low(g, c)
                chunk = (g - G_OF[f"V{q}"]) * R + c
                tt(stage_l[:, c % 2, :], act_e[q % 2][:, chunk, :], stage_h[:, c % 2, :].bitcast(F32),
                   ALU.subtract).then_inc(lo_done, 1)

            dve.wait_ge(ht_done, KD * (LAYERS + 2))
            for half in range(2):
                k = slice(half * 8, half * 8 + 8)
                dve.wait_ge(hh_done, half + 1)
                tt(hl[:, k, :], hT[:, k, :], hh[:, k, :].bitcast(F32), ALU.subtract).then_inc(hl_done, 1)
            low(G_WQ, 0).then_inc(lo_done, 1)
            with dve.Fori(G_WQ, G_WQ + WQ_G) as g:
                for c in range(R):
                    low(g + (c + 1) // R, (c + 1) % R).then_inc(lo_done, 1)
            dve.wait_ge(sc_full, 1)
            v.tensor_copy(score[:, 1].rearrange("p a b -> p (a b)"), ps[:, 4:8, :].rearrange("p a b -> p (a b)")).then_inc(sc_done, 1)
            dve.wait_ge(sc_done, 2)

            ahead_n = [0]

            def ahead():
                if ahead_n[0] < PART:
                    ahead_n[0] += 1
                    u = G_OF["U0"] * R + ahead_n[0]
                    low(u // R, u % R).then_inc(lo_done, 1)

            def top16(rows, values, indices):
                n = len(rows)
                for j in range(n):
                    st(v.max(values[j][:, 0:8], rows[j]))
                ahead()
                st.done()
                for j in range(n):
                    st(v.max_index(indices[j][:, 0:8], values[j][:, 0:8], rows[j]))
                ahead()
                st.done()
                for j in range(n):
                    st(v.match_replace(rows[j], values[j][:, 0:8], rows[j], -3.0e38))
                ahead()
                st.done()
                for j in range(n):
                    st(v.max(values[j][:, 8:16], rows[j]))
                ahead()
                st.done()
                for j in range(n):
                    st(v.max_index(indices[j][:, 8:16], values[j][:, 8:16], rows[j]))
                ahead()
                st.done()

            iota16 = small_of("iota")[:, 0:TOPK]
            for t in range(T):
                top16([score[:, t, j, :] for j in range(16)], [half_v[:, j, :] for j in range(16)],
                      [half_i[:, j, :] for j in range(16)])
                st(v.tensor_copy(half_f, half_i))
                hv = half_v.rearrange("p (h s) k -> p h s k", s=2)
                st(tt(cand, hv[:, :, 0, :].unsqueeze(3).to_broadcast([P, PEER_HEADS, TOPK, TOPK]),
                      hv[:, :, 1, :].unsqueeze(2).to_broadcast([P, PEER_HEADS, TOPK, TOPK]), ALU.add))
                st.done()
                top16([cand[:, h].rearrange("p a b -> p (a b)") for h in range(PEER_HEADS)],
                      [top_v[:, h, :] for h in range(PEER_HEADS)], [pick[:, h, :] for h in range(PEER_HEADS)])
                st(ts(pick_i, pick, 4, None, ALU.logical_shift_right))
                st(ts(pick_j, pick, 15, None, ALU.bitwise_and))
                st.done()
                st(v.tensor_copy(pick_fi, pick_i))
                st(v.tensor_copy(pick_fj, pick_j))
                st.done()
                hf = half_f.rearrange("p (h s) k -> p h s k", s=2)
                for s, which in ((0, pick_fi), (1, pick_fj)):
                    shape = [P, PEER_HEADS * TOPK, TOPK]
                    m3 = match.rearrange("p h a b -> p (h a) b")
                    st(tt(m3, which.rearrange("p h k -> p (h k)").unsqueeze(2).to_broadcast(shape),
                          iota16[:, None, :].to_broadcast(shape), ALU.is_equal))
                    st.done()
                    st(tt(match, match, hf[:, :, s, :].unsqueeze(2).to_broadcast([P, PEER_HEADS, TOPK, TOPK]), ALU.mult))
                    st.done()
                    st(v.tensor_reduce(route[:, s, t, :], m3, AX, ALU.add))
                    ahead()
                    st.done()
                gates = route[:, 2, t, :].rearrange("p (h k) -> p h k", h=PEER_HEADS)
                tt(gates, top_v, top_v[:, :, 0:1].to_broadcast([P, PEER_HEADS, TOPK]), ALU.subtract).then_inc(rexp_in, 1)
            while ahead_n[0] < PART:
                ahead()
            for t in range(T):
                gates = route[:, 2, t, :].rearrange("p (h k) -> p h k", h=PEER_HEADS)
                dve.wait_ge(rexp_done, t + 1)
                st(v.tensor_reduce(hs[:, 0:8], gates, AX, ALU.add))
                st.done()
                st(v.reciprocal(hs[:, 8:16], hs[:, 0:8]))
                st.done()
                tt(gates, gates, hs[:, 8:16].unsqueeze(2).to_broadcast([P, PEER_HEADS, TOPK]), ALU.mult).then_inc(routed, 1)
                dve.wait_ge(routed, t + 1)
            dve.wait_ge(rt_full, 1)
            for a in range(3):
                st(v.tensor_copy(routeT[:, a, :], ps[:, a, 0:SEQ]))
            st.done()

            def hot(q, t0, b):
                for j in range(BATCH):
                    ts(hot1[:, b, j, :], small_of("iota"), routeT[:, 0, bass.ds(t0 + j, 1)], routeT[:, 2, bass.ds(t0 + j, 1)],
                       ALU.is_equal, ALU.mult)
                shape = [P, BATCH, PART]
                tt(hot2[:, b], routeT[:, 1, bass.ds(t0, BATCH)].unsqueeze(2).to_broadcast(shape),
                   small_of("iota")[:, None, q * PART:(q + 1) * PART].to_broadcast(shape), ALU.is_equal).then_inc(hot_done, 1)

            def gated(q, n, t0, b):
                dve.wait_ge(g_full, n + 1)
                o = act_e[q % 2][:, :, bass.ds(t0, BATCH)].rearrange("p i t -> p t i")
                tt(o, o, ps[:, b, 0:BATCH * PART].rearrange("p (t i) -> p t i", t=BATCH), ALU.mult).then_inc(g_used, 1)

            def gate_slots(q, g, i):
                for c in range(R):
                    hot(q, i * R * BATCH + (c + 1) * BATCH, (c + 1) % 2)
                    gated(q, i * R + (q * PART + c), i * R * BATCH + c * BATCH, c % 2)
                    low(g + (c + 1) // R, (c + 1) % R).then_inc(lo_done, 1)

            def take_sum(q):
                y = ysum[q % 2]
                dve.wait_ge(g2_done, 1)
                tt(y[:, 1, :], ps[:, 4:8, :].rearrange("p a b -> p (a b)"), gate2row, ALU.mult).then_inc(y_used, 1)

            def add_sum(q):
                y = ysum[q % 2]
                dve.wait_ge(y_used, 2 * (q + 1))
                st(tt(y[:, 0, :], y[:, 0, :], gate2row, ALU.mult))
                st.done()
                for t in range(T):
                    tt(X[:, t, :], X[:, t, :], y[:, t, :], ALU.add).then_inc(x_done, 1)
                dve.wait_ge(x_done, T * (LAYERS + 3 + q))

            def up_quarter(q):
                g0 = G_OF[f"U{q}"]
                if q > 1:
                    dve.wait_ge(unit_done, g0 * R)
                    take_sum(q - 2)
                dve.wait_ge(fm_free, N_U + q * PART + R)
                gate_slots(q - 1, g0, 0)
                if q > 1:
                    add_sum(q - 2)
                with dve.Fori(1, PART_G - 1) as i:
                    gate_slots(q - 1, i + g0, i)
                g, n, t0 = g0 + PART_G - 1, q * PART - R, SEQ - R * BATCH
                for c in range(R - 1):
                    hot(q - 1, t0 + (c + 1) * BATCH, (c + 1) % 2)
                    gated(q - 1, n + c, t0 + c * BATCH, c % 2)
                    low(g, c + 1).then_inc(lo_done, 1)
                gated(q - 1, n + R - 1, t0 + (R - 1) * BATCH, (R - 1) % 2)
                dve.wait_ge(g_used, q * PART)
                low_v(g + 1, 0, q - 1)

            def down_quarter(q):
                g0 = G_OF[f"V{q}"]
                with dve.Fori(g0, g0 + PART_G - 1) as g:
                    for c in range(R):
                        low_v(g + (c + 1) // R, (c + 1) % R, q)
                for c in range(R - 1):
                    low_v(g0 + PART_G - 1, c + 1, q)
                if q < PARTS - 1:
                    hot(q + 1, 0, 0)
                if q < PARTS - 2:
                    low(g0 + PART_G, 0).then_inc(lo_done, 1)

            hot(0, 0, 0)
            up_quarter(1)
            down_quarter(0)
            up_quarter(2)
            down_quarter(1)
            up_quarter(3)
            down_quarter(2)
            dve.wait_ge(fm_free, N_U + PARTS * PART + R)
            dve.wait_ge(unit_done, G_OF["V3"] * R)
            take_sum(2)
            q, n = PARTS - 1, (PARTS - 1) * PART
            with dve.Fori(0, PART // 2 - 1) as i:
                for b in range(2):
                    hot(q, i * 2 * BATCH + (b + 1) * BATCH, (b + 1) % 2)
                    gated(q, i * 2 + (n + b), i * 2 * BATCH + b * BATCH, b)
            hot(q, SEQ - BATCH, 1)
            gated(q, n + PART - 2, SEQ - 2 * BATCH, 0)
            gated(q, n + PART - 1, SEQ - BATCH, 1)
            dve.wait_ge(g_used, PARTS * PART)
            low_v(G_OF["V3"], 0, q)
            add_sum(2)
            down_quarter(3)
            dve.wait_ge(unit_done, GROUPS * R)
            take_sum(3)
            add_sum(3)
            dve.wait_ge(frs_done, 1)
            dve.wait_ge(gfin_ready, 16)
            for t in range(T):
                stt(X[:, t, :], X[:, t, :], rstd2[:, t:t + 1], gfin, ALU.mult, ALU.mult).then_inc(fin_ready, 1)


def rows_units(w):
    g = w.shape[1] // 512
    return w.reshape(4, 4, P, g, 512).transpose(3, 0, 2, 1, 4).reshape(4 * g, P, UNIT)


def cols_units(w):
    c = w.shape[1] // P
    return w.reshape(KD, P, c, P).transpose(2, 1, 0, 3).reshape(c, P, UNIT)


def padded(*parts):
    u = np.zeros((1, P, UNIT), np.float32)
    at = 0
    for p in parts:
        p = p.reshape(P, -1)
        u[0, :, at:at + p.shape[1]] = p
        at += p.shape[1]
    return u


def by_tile(w):
    return w.reshape(-1, P, w.shape[1]).transpose(1, 0, 2)


def col(vec):
    v = vec.reshape(-1, P)
    return np.ascontiguousarray(v.T)


def weight_stream(a):
    empty = np.zeros((1, P, UNIT), np.float32)
    units = []
    for l in range(LAYERS):
        w = a["w_in"][l]
        (aq, ak, av, ag, cq, ckv, kr, bg, q3, k3, v3, g3) = np.split(
            w, np.cumsum([1024, 256, 256, 1024, 512, 256, 64, 512, 512, 512, 512])[:11], axis=1)
        pad = np.zeros((DM, TM_W - 2880), np.float32)
        units.append(rows_units(np.concatenate([aq, ak, av, cq, v3, ckv, kr, pad], axis=1)))
        units.append(cols_units(np.concatenate([ag, bg, g3, q3, k3], axis=1)))
        uq = a["b_w_uq"][l].reshape(512, 4, 192)
        ukv = a["b_w_ukv"][l].reshape(256, 4, 256)
        units.append(padded(by_tile(uq[:, :, :128].reshape(512, 512))))
        units.append(padded(by_tile(uq[:, :, 128:].reshape(512, 256))))
        units.append(padded(by_tile(np.concatenate([ukv[:, :, :128].reshape(256, 512),
                                                    ukv[:, :, 128:].reshape(256, 512)], axis=1))))
        units.append(empty)
        units.append(rows_units(a["w_out"][l]))
    w = a["w_in_2"][0]
    (q, kc, vc, ks, vs, kw, vw, ga, qr, kr, vr, gr) = np.split(
        w, np.cumsum([1024] + [256] * 6 + [48, 1024, 1024, 1024])[:11], axis=1)
    units.append(rows_units(np.concatenate([vs, vw, vr], axis=1)))
    units += [padded(by_tile(ga)), empty, empty, empty]
    order = np.zeros((8, 2), np.int64)
    for h in range(NSA_HEADS):
        order[nsa_chunk(h)] = h
    qo = q.reshape(DM, NSA_HEADS, NSA_D)[:, order.reshape(-1)].reshape(DM, 1024)
    units.append(cols_units(np.concatenate([qo, kc, vc, ks, kw, qr, kr, gr], axis=1)))
    for name in ("cmp_k_w1_2", "cmp_v_w1_2"):
        w1 = a[name][0].reshape(2, 16, NSA_D, P).transpose(0, 2, 1, 3).reshape(2, NSA_D, UNIT)
        units.append(np.concatenate([w1, w1], axis=1))
    units.append(rows_units(a["w_out_2"][0]))
    units.append(cols_units(a["peer_w_q_2"][0]))
    u = a["peer_u_2"][0].reshape(KEYS, KEYS, KD, P).transpose(1, 3, 2, 0).reshape(KEYS, P, UNIT)
    v = a["peer_v_2"][0].reshape(KEYS, KEYS, DM).transpose(1, 0, 2)
    for name in EXPERT_ORDER:
        q = int(name[1])
        units.append((u if name[0] == "U" else v)[q * PART:(q + 1) * PART])
    s = np.concatenate(units, axis=0)
    assert s.shape[0] == GROUPS * R, (s.shape, GROUPS * R)
    return s


def fill(spec, width, values):
    o = np.zeros((P, width), np.float32)
    for name, (at, n) in spec.items():
        o[:, at:at + n] = values[name]
    return o


def rotary(n):
    half = n // 2
    inv = (1.0 / (np.float32(10000.0) ** (np.arange(0, half, 2, dtype=np.float32) / np.float32(half)))).astype(np.float32)
    t = np.arange(SEQ)
    cos, sin = [], []
    for pos in (t // GRID, t % GRID):
        ang = pos.astype(np.float32)[:, None] * inv[None, :]
        cos += [np.cos(ang), np.cos(ang)]
        sin += [-np.sin(ang), np.sin(ang)]
    return [np.concatenate(z, axis=1).astype(np.float32) for z in (cos, sin)]


def tiles(m):
    return m.reshape(T, P, -1).transpose(1, 0, 2).reshape(P, -1)


def host(a):
    rep = lambda r: np.broadcast_to(r.reshape(1, -1), (P, r.size))
    b_ada = a["b_ada_2"][0]
    t = np.arange(SEQ)
    small = fill(SMALL, SMALL_W, {
        "ident": np.eye(P, dtype=np.float32), "one": 1.0, "pow": -0.5,
        "g_pre": np.concatenate([col(a["norm_pre"]), col(a["g_norm_mix_2"]), col(a["g_norm_ffn_2"])], axis=1),
        "b_qn": col(a["b_q_norm"]), "b_kvn": col(a["b_kv_norm"]),
        "cond": col(a["c_2"]), "b_ada": col(b_ada), "iota": np.arange(P, dtype=np.float32)[None, :],
    })
    const3 = fill(CONST3, CONST3_W, {
        "g_nsa": col(a["g_nsa_out_2"]), "g_ret": col(a["g_ret_out_2"]),
        "row_ok": (t >= CMP_LEN - 1).astype(np.float32).reshape(T, P).T,
        "w2k": np.concatenate([a["cmp_k_w2_2"][0]] * 2, axis=1), "w2v": a["cmp_v_w2_2"][0],
        "pe": np.concatenate([np.concatenate([a[n][0].T] * 2, axis=0) for n in ("cmp_pe_k_2", "cmp_pe_v_2")], axis=1),
    })
    cos, sin = rotary(HD)
    cos_b, sin_b = rotary(64)
    c0 = np.clip(t % GRID - 8, 0, GRID - 16)
    kc = t % GRID
    near = (kc[None, :] >= c0[:P, None]) & (kc[None, :] < c0[:P, None] + 16)
    g_qk = np.stack([a["a_q_norm"], a["a_k_norm"]], axis=1).reshape(1, -1)
    const1 = fill(CONST1, CONST1_W, {
        "cos": tiles(cos), "sin": tiles(sin), "cos_b": tiles(cos_b), "sin_b": tiles(sin_b),
        "g_qk": rep(g_qk), "nbr": np.where(near, 0.0, MASKED)})
    d = (t[:, None] - t[None, :]).astype(np.float32)
    dist = np.where(d >= 0, d, np.float32(-MASKED))
    dc = (t[:, None] - (np.arange(NCMP) * CMP_STRIDE + CMP_LEN - 1)[None, :]).astype(np.float32)
    cb = np.where(dc[:, None, :] >= 0, -SLOPES[None, :, None] * dc[:, None, :], np.float32(MASKED))
    lg = np.log1p(-np.exp2(-5.0 - np.arange(RET_HEADS, dtype=np.float64)))
    dd = (t[None, :] - t[:, None]).astype(np.float64)
    decay = np.where(dd >= 0, np.exp(lg[:, None, None] * np.maximum(dd, 0)), 0.0) * HD ** -0.5
    decay = np.concatenate([decay[:, 0:P, :], decay[:, P:, P:]], axis=2).transpose(1, 0, 2).reshape(P, -1)
    const2 = fill(CONST2, CONST2_W, {
        "dist": np.concatenate([dist[0:P, 0:P], dist[P:, :]], axis=1),
        "cmp_bias": tiles(cb.reshape(SEQ, -1)), "decay": decay})
    rpb = np.pad(a["c_rpb"], ((0, 0), (0, 0), (0, 0), (48, 48)))
    win = np.stack([rpb[..., GRID - 1 - c:2 * GRID - 1 - c] for c in range(GRID)], axis=3)
    rows = t // GRID
    nbr = np.zeros((LAYERS, 2, GRID, 4, T, 4, GRID), np.float32)
    for qr in range(4):
        for kr in range(4):
            nbr[:, qr % 2, :, :, qr // 2, kr, :] = win[:, :, kr - qr + 7].transpose(0, 2, 1, 3)
    ada = a["w_ada_2"][0].reshape(ADA_H, 2, P, ADA_CG, 512).transpose(3, 0, 2, 1, 4).reshape(ADA_CG, ADA_H, P, ADA_UNIT)
    return {
        "stream": weight_stream(a), "ada": np.ascontiguousarray(ada), "small": small, "const1": const1,
        "const2": const2, "const3": const3,
        "keys": np.ascontiguousarray(a["peer_sub_keys_2"][0].reshape(16, KEYS, P).transpose(2, 0, 1).reshape(P, -1)),
        "nbr_bias": nbr.reshape(LAYERS, P, -1),
        "g_post": np.ascontiguousarray(np.broadcast_to(a["norm_post"][:, None, :], (LAYERS, P, DM))),
        "g_final": np.ascontiguousarray(rep(a["g_norm_final_2"])), "x": np.ascontiguousarray(a["x"]),
    }


def kernel(**inputs):
    import concourse.bacc as bacc
    from concourse.bass_utils import run_bass_kernel_spmd

    arrays = host({k: np.asarray(v) for k, v in inputs.items()})
    nc = bacc.Bacc("TRN2", target_bir_lowering=False, num_devices=1)
    args = [nc.dram_tensor(f"in_{n}", v.shape, F32, kind="ExternalInput").ap() for n, v in arrays.items()]
    out = nc.dram_tensor("out", (1, SEQ, DM), F32, kind="ExternalOutput").ap()
    block(nc, *args, out)
    r = run_bass_kernel_spmd(nc, [{f"in_{n}": v for n, v in arrays.items()}], core_ids=[0])
    return r.results[0]["out"]
```

```python
from contextlib import ExitStack

import numpy as np
import concourse.bass as bass
from concourse import mybir

P = 128
F32 = mybir.dt.float32
F32R = mybir.dt.float32r
BF16 = mybir.dt.bfloat16
U32 = mybir.dt.uint32
ALU = mybir.AluOpType
ACT = mybir.ActivationFunctionType
AX = mybir.AxisListType.X

SEQ, DM = 256, 2048
T = SEQ // P
KD = DM // P
LAYERS = 2
HD = 128
GRID = 64
EPS = 1e-6
MASKED = -1e30
NSA_HEADS, NSA_D = 16, 64
CMP_LEN, CMP_STRIDE = 32, 16
NCMP = (SEQ - CMP_LEN) // CMP_STRIDE + 1
RET_HEADS = 8
PEER_HEADS, KEYS, TOPK = 8, 128, 16
PAIRS = PEER_HEADS * TOPK
MODS = 6

R = 4
UNIT = 2048
TM_G, FM_G, LAT_G, WO_G = 6, 6, 1, 4
LAYER_G = TM_G + FM_G + LAT_G + WO_G
TM2_G, FM2_G, CMP_G, WQ_G = 3, 10, 1, 4
G_TM2 = LAYERS * LAYER_G
G_FM2 = G_TM2 + TM2_G
G_CMP = G_FM2 + FM2_G
G_WO2 = G_CMP + CMP_G
G_WQ = G_WO2 + WO_G
G_EXP = G_WQ + WQ_G
PARTS = 4
PART = KEYS // PARTS
PART_G = PART // R
EXPERT_ORDER = ("U0", "U1", "V0", "U2", "V1", "U3", "V2", "V3")
G_OF = {name: G_EXP + i * PART_G for i, name in enumerate(EXPERT_ORDER)}
HALVED = "V2"
PASS_G = PART_G // 2
GROUPS = G_EXP + len(EXPERT_ORDER) * PART_G
BATCH = 8
assert SEQ // BATCH == PART

ADA_CG = MODS * DM // 512
ADA_H = KD // 2
ADA_TM, ADA_FM, ADA_WO = 3, 2, 2
ADA_LAYER = ADA_TM + ADA_FM + ADA_WO
ADA_TM2, ADA_FM2, ADA_WO2 = 3, 5, 2
A_TM2 = LAYERS * ADA_LAYER
A_FM2 = A_TM2 + ADA_TM2
A_WO2 = A_FM2 + ADA_FM2
assert A_WO2 + ADA_WO2 == ADA_CG
ADA_UNIT = 2 * 512

A_Q, A_K, A_V, B_CQ, C_V, B_CKV, B_KR, TM_W = 0, 1024, 1280, 1536, 2048, 2560, 2816, 3072
QK_HEADS = 10
GATE_CHUNKS = 16
C_Q, C_K, FM_C = 16, 20, 24
V_S, V_W, V_R, TM2_W = 0, 256, 512, 1536
NQ, KC, VC, KS, KW, RQ, RK, RG, FM2_C = 0, 8, 10, 12, 14, 16, 24, 32, 40
NGATE = 3 * NSA_HEADS

SMALL = {}
_at = 0
for _name, _n in (("ident", P), ("one", 1), ("pow", 32), ("g_pre", 4 * KD), ("b_qn", 2 * 4), ("b_kvn", 2 * 2),
                  ("cond", KD), ("b_ada", MODS * KD), ("iota", P)):
    SMALL[_name] = (_at, _n)
    _at += _n
SMALL_W = _at
CONST1 = {}
_at = 0
for _name, _n in (("cos", T * 128), ("sin", T * 128), ("cos_b", T * 64), ("sin_b", T * 64),
                  ("g_qk", LAYERS * 2 * 128), ("nbr", SEQ)):
    CONST1[_name] = (_at, _n)
    _at += _n
CONST1_W = _at
CONST2 = {}
_at = 0
for _name, _n in (("dist", 3 * P), ("cmp_bias", NSA_HEADS * T * NCMP), ("w_gate", KD * NGATE), ("row_ok", T),
                  ("w2k", P), ("w2v", NSA_D), ("pe", 2 * CMP_LEN), ("g_nsa", 8), ("g_ret", 8)):
    CONST2[_name] = (_at, _n)
    _at += _n
CONST2_W = _at
DECAY_W = RET_HEADS * 3 * P

SLOPES = np.exp2(-8.0 * (np.arange(NSA_HEADS, dtype=np.float32) + 1.0) / NSA_HEADS).astype(np.float32)


def nsa_chunk(h):
    g, r = h // 4, h % 4
    return (g // 2) * 4 + r, g % 2


class Steps:

    def __init__(self, eng, sem):
        self.eng, self.sem, self.base, self.n = eng, sem, 0, 0

    def region(self, base):
        self.base, self.n = base, 0

    def __call__(self, ins):
        ins.then_inc(self.sem, 1)
        self.n += 1

    def done(self):
        self.eng.wait_ge(self.sem, self.base + self.n)


DVE_STEPS, POOL_STEPS = 52, 7


def block(nc, stream, ada, small, const1, const2, decays, keys, nbr_bias, g_post, g_final, x, out):
    ctx = ExitStack()

    def sb(name, shape, dt=F32):
        return ctx.enter_context(nc.sbuf_tensor(name, shape, dt))

    def sem(name):
        return ctx.enter_context(nc.semaphore(name))

    with ctx:
        X = sb("X", [P, T, DM])
        ring = sb("ring", [P, R, UNIT])
        aring = sb("aring", [P, 2, ADA_UNIT])
        SM = sb("SM", [P, SMALL_W])
        mod = sb("mod", [P, MODS * KD])
        csilu = sb("csilu", [P, KD])
        gsc = sb("gsc", [P, 2, KD])
        stat = sb("stat", [P, 384])
        with ExitStack() as before_experts:
            BIG = before_experts.enter_context(nc.sbuf_tensor("BIG", [P, 2 * PART * SEQ + 20736], F32))
        pairs = []
        with ExitStack() as before_stage:
            pairs.append(before_stage.enter_context(nc.sbuf_tensor("pairs0", [P, 2, 2, SEQ], F32R)))
        stage_h, stage_l = sb("stage_h", [P, 2, SEQ], F32R), sb("stage_l", [P, 2, SEQ], F32R)
        hot1 = sb("hot1", [P, 2, BATCH, KEYS], F32R)
        hot2 = sb("hot2", [P, BATCH, 2, PART], F32R)
        gate_parts = sb("gate_parts", [P, 2, SEQ], F32R)
        index = sb("index", [P, 2, SEQ], BF16)
        with ExitStack() as before_hh:
            pairs.append(before_hh.enter_context(nc.sbuf_tensor("pairs1", [P, 2, 2, SEQ], F32R)))
        hh, hl = sb("hh", [P, KD, SEQ], F32R), sb("hl", [P, KD, SEQ], F32R)
        wh, wl = sb("wh", [P, 2, UNIT], F32R), sb("wl", [P, 2, UNIT], F32R)
        act_e = [sb("act0", [P, PART, SEQ]), sb("act1", [P, PART, SEQ])]
        ps = ctx.enter_context(nc.psum_tensor("ps", [P, 8, 512], F32))

        def area(at, *dims, buf=BIG):
            n = int(np.prod(dims))
            v = buf[:, at:at + n]
            if len(dims) == 1:
                return v
            names = "abcd"[:len(dims)]
            spec = "p (" + " ".join(names) + ") -> p " + " ".join(names)
            return v.rearrange(spec, **dict(zip(names, dims)))

        def small_of(name, *dims):
            at, n = SMALL[name]
            return area(at, *(dims or (n,)), buf=SM)

        ident, one, power = small_of("ident"), small_of("one"), small_of("pow")
        g_pre = small_of("g_pre", 4, KD)
        g_cq, g_ckv = small_of("b_qn", 2, 4), small_of("b_kvn", 2, 2)

        HH, WH, WL, ACTS = 4352, 12544, 16640, 20736
        Xn = area(ACTS, T, DM)
        hT = area(ACTS + 6144, KD, SEQ)
        Y = area(ACTS, T, DM)
        acc = area(256, max(ADA_TM + ADA_FM, ADA_TM2 + ADA_FM2), 512)
        OT = area(0, KD, SEQ)

        PT = area(ACTS, T, TM_W)
        PF = area(ACTS + 6144, FM_C, SEQ)
        ROT, C1 = ACTS + 12288, ACTS + 14848
        rot1, rot2 = area(ROT, QK_HEADS, HD), area(ROT + 1280, QK_HEADS, HD)
        junk = [area(ROT + 1280, 512), area(ROT, 512)]
        krot = area(0, 2, T, 64)
        qkT = area(WH, QK_HEADS, SEQ)
        cqT, ckvT = area(WH + 2560, 4, SEQ), area(WH + 3584, 2, SEQ)
        qnT, qpT = area(WL, 4, SEQ), area(WL + 1024, 4, SEQ)
        knT, kpT = area(WL + 2048, 4, SEQ), area(WL + 3072, SEQ)
        prob, probT = area(HH, 4, T, SEQ), area(HH + 2048, 4, T, SEQ)
        nbias = area(HH + 4096, 4, T, SEQ)
        vB = area(HH + 6144, T, 512)
        qpe, qpe2 = area(HH + 7168, T, 4, 64), area(HH + 7680, T, 4, 64)
        gpost = area(ACTS + 6144, DM)
        lsquares = area(ACTS + 8192, T, DM)

        def c1(name, *dims):
            at, n = CONST1[name]
            return area(C1 + at, *(dims or (n,)))

        PT2 = area(ACTS, T, TM2_W)
        PF2 = area(ACTS + 3072, FM2_C, SEQ)
        C2 = ACTS + 13312
        KCZ = C2 + CONST2_W
        kcz = area(KCZ, 4, 16)
        hid = area(KCZ + 64, 2, 64)
        vcmp = area(KCZ + 192, 4, NSA_D)
        cprob = area(KCZ + 448, T * NSA_HEADS, NCMP)
        decay3 = area(0, RET_HEADS, 3 * P)
        cprobT = area(HH, T * NSA_HEADS, P)
        nprob = [area(HH, 4, 3 * P), area(HH + 1536, 4, 3 * P)]
        ntmp = area(HH + 3072, T, 4, NSA_D)
        cmp_in = [area(HH + 4096, 4, CMP_LEN, NCMP), area(HH + 6016, 4, CMP_LEN, NCMP)]
        yret = area(HH + 4096, T * RET_HEADS, HD)
        kz = area(WH, 2, 4, SEQ)
        square = area(WH, 2048)
        onsa = area(WH + 2048, T * NSA_HEADS, NSA_D)
        nprobT = area(WL, 4, 3 * P)

        def c2(name, *dims):
            at, n = CONST2[name]
            return area(C2 + at, *(dims or (n,)))

        flat = [act_e[i][:, :, :].rearrange("p a b -> p (a b)") for i in range(2)]
        table = area(2 * SEQ * 2, 2304)
        side = aring[:, :, :].rearrange("p a b -> p (a b)")
        qP = area(0, 16, SEQ, buf=flat[0])
        score = area(0, T, 16, KEYS, buf=flat[1])
        cand = area(4096, PEER_HEADS, TOPK, TOPK, buf=flat[1])
        match = area(6144, PEER_HEADS, TOPK, TOPK, buf=flat[1])
        half_v = area(0, 16, TOPK, buf=table)
        half_i = area(256, 16, TOPK, buf=table).bitcast(U32)
        half_f = area(512, 16, TOPK, buf=table)
        top_v = area(768, PEER_HEADS, TOPK, buf=table)
        pick = area(896, PEER_HEADS, TOPK, buf=table).bitcast(U32)
        pick_i = area(1024, PEER_HEADS, TOPK, buf=table).bitcast(U32)
        pick_j = area(1152, PEER_HEADS, TOPK, buf=table).bitcast(U32)
        pick_fi = area(1280, PEER_HEADS, TOPK, buf=table)
        pick_fj = area(1408, PEER_HEADS, TOPK, buf=table)
        route = area(1536, 3, T, PAIRS, buf=table)
        gsum = area(76, BATCH, PART, buf=stat)
        keyT = area(0, 16, KEYS, buf=side)
        gate2row = side
        gfin = area(0, DM, buf=flat[0])
        ysum = [area(4096, T, DM, buf=flat[i]) for i in range(2)]
        ysum2 = area(HH + KD * SEQ, T, DM // 2)
        squares = area(0, T, DM, buf=flat[1])

        ss2, rstd2 = stat[:, 0:2], stat[:, 2:4]
        ssq, msq, rsq = stat[:, 4:28], stat[:, 28:52], stat[:, 52:76]
        mx, nb = area(76, 2, 8, buf=stat), area(92, 2, 8, buf=stat)
        rs, rinv = area(108, 2, 8, buf=stat), area(124, 2, 8, buf=stat)
        ms2 = stat[:, 140:142]
        gw = area(144, T, NGATE, buf=stat)
        cmx, crs = stat[:, 240:272], stat[:, 272:304]
        cw = stat[:, 304:336]
        hs = stat[:, 336:368]
        ypart, yhalf = area(368, T, WO_G, buf=stat), area(376, T, 2, buf=stat)
        gcol, glat = gsc[:, 0, :], gsc[:, 1, 0:6]
        w_ready = [sem(f"w_ready{s}") for s in range(R)]
        unit_done = sem("unit_done")
        a_ready = [sem(f"a_ready{s}") for s in range(2)]
        a_used = sem("a_used")
        a_step = sem("a_step")
        loaded = sem("loaded")
        c1_ready, bias_ready, gpost_ready = sem("c1_ready"), sem("bias_ready"), sem("gpost_ready")
        bias_masked = sem("bias_masked")
        c_ready = sem("c_ready")
        x_done = sem("x_done")
        tm_free, fm_free = sem("tm_free"), sem("fm_free")
        sq_done, prs_done, xn_done = sem("sq_done"), sem("prs_done"), sem("xn_done")
        ht_full, ht_done = sem("ht_full"), sem("ht_done")
        mod_full, mod_done = sem("mod_full"), sem("mod_done")
        dve_step, pool_step = sem("dve_step"), sem("pool_step")
        qss_done, qrs_done = sem("qss_done"), sem("qrs_done")
        qk_ready, tr_full, tr_done = sem("qk_ready"), sem("tr_full"), sem("tr_done")
        lat_done, qpe_ready, kpe_full, kpe_done = sem("lat_done"), sem("qpe_ready"), sem("kpe_full"), sem("kpe_done")
        qpt_full, qpt_done = sem("qpt_full"), sem("qpt_done")
        s_full, nb_done, exp_done, p_ready = sem("s_full"), sem("nb_done"), sem("exp_done"), sem("p_ready")
        t_full, pt_done, pv_full, o_done = sem("t_full"), sem("pt_done"), sem("pv_full"), sem("o_done")
        s_masked = sem("s_masked")
        yrs_done = sem("yrs_done")
        pe_passed, pool_passed, dve_passed = sem("pe_passed"), sem("pool_passed"), sem("dve_passed")
        c2_ready, decay_ready, zeroed, gates_full, gw_done = sem("c2_ready"), sem("decay_ready"), sem("zeroed"), sem("gates_full"), sem("gw_done")
        gsc_done, kz_done, cin_done = sem("gsc_done"), sem("kz_done"), sem("cin_done")
        hid_done, kc_full, kc_done, vc_done = sem("hid_done"), sem("kc_full"), sem("kc_done"), sem("vc_done")
        cs_full, cs_done, ce_done, ct_full, ct_done = sem("cs_full"), sem("cs_done"), sem("ce_done"), sem("ct_full"), sem("ct_done")
        cpv_full, co_done = sem("cpv_full"), sem("co_done")
        n_full, n_nb, n_exp, n_t = sem("n_full"), sem("n_nb"), sem("n_exp"), sem("n_t")
        n_pt, n_pv, n_out = sem("n_pt"), sem("n_pv"), sem("n_out")
        r_ready, yret_done = sem("r_ready"), sem("yret_done")
        nss_done, nrs_done, n_normed, ot_full, ot_done = (sem("nss_done"), sem("nrs_done"), sem("n_normed"),
                                                          sem("ot_full"), sem("ot_done"))
        g1_full = sem("g1_full")
        sc_full, sc_done, routed, rexp_in, rexp_done = sem("sc_full"), sem("sc_done"), sem("routed"), sem("rexp_in"), sem("rexp_done")
        rt_full = sem("rt_full")
        keys_ready = sem("keys_ready")
        hi_done, lo_done = sem("hi_done"), sem("lo_done")
        hh_done, hl_done = sem("hh_done"), sem("hl_done")
        nh_done, nl_done = sem("nh_done"), sem("nl_done")
        hot_step, sum_step, hot_done, g_full, g_used = sem("hot_step"), sem("sum_step"), sem("hot_done"), sem("g_full"), sem("g_used")
        g2_full, g2_done = sem("g2_full"), sem("g2_done")
        y_used = sem("y_used")
        gfin_ready = sem("gfin_ready")
        frs_done, fss_done, out_done = sem("frs_done"), sem("fss_done"), sem("out_done")
        fin_ready = sem("fin_ready")

        TM_N = TM_G + WO_G
        N_TM2 = LAYERS * TM_N
        N_WO2 = N_TM2 + TM2_G
        N_FM = LAYERS * FM_G * R
        N_WQ = N_FM + FM2_G * R
        N_U = N_WQ + WQ_G * R

        blk = ctx.enter_context(nc.Block())

        @blk.sync
        def _(sp):
            sp.dma_start(ring[:, 0, :], stream[0]).then_inc(w_ready[0], 16)
            sp.dma_start(SM[:, :], small).then_inc(loaded, 16)
            sp.dma_start(X[:, :, :], x.rearrange("b (t p) d -> p (b t) d", p=P)).then_inc(loaded, 16)
            for s in range(1, R):
                sp.dma_start(ring[:, s, :], stream[s]).then_inc(w_ready[s], 16)
            with sp.Fori(1, GROUPS) as g:
                for s in range(R):
                    sp.wait_ge(lo_done, g * R + (s + 1 - R))
                    sp.dma_start(ring[:, s, :], stream[g * R + s]).then_inc(w_ready[s], 16)
            sp.wait_ge(unit_done, G_OF["V3"] * R)
            sp.dma_start(gfin, g_final).then_inc(gfin_ready, 16)
            for t in range(T):
                sp.wait_ge(fin_ready, t + 1)
                sp.dma_start(out[0, t * P:(t + 1) * P, :], X[:, t, :]).then_inc(out_done, 16)
            sp.wait_ge(out_done, 16 * T)

        @blk.tensor
        def _(pe):
            mm = pe.matmul

            def unit(g, s):
                pe.wait_ge(w_ready[s], 16 * (g + 1))

            def settle():
                pe.sem_inc(pe_passed, 1)

            def split(g, c):
                pe.wait_ge(lo_done, g * R + (c + 1))

            def rows_group(g, n, pair):
                pe.wait_ge(tm_free, n + 1)
                for s in range(R):
                    split(g, s)
                    for t in range(T):
                        tok = slice(t * P, (t + 1) * P)
                        for kk in range(4):
                            w, k = slice(kk * 512, (kk + 1) * 512), 4 * s + kk
                            first, end = k == 0, k == KD - 1
                            o = ps[:, 2 * pair + t, :]
                            mm(o, hh[:, k, tok], wh[:, s % 2, w], start=first, stop=False)
                            mm(o, hh[:, k, tok], wl[:, s % 2, w], start=False, stop=False)
                            last = mm(o, hl[:, k, tok], wh[:, s % 2, w], start=False, stop=end)
                    last.then_inc(unit_done, 1)

            def up(g, c, n):
                pe.wait_ge(fm_free, n + 1)
                split(g, c)
                o = ps[:, 4 + c, 0:SEQ]
                for k in range(KD):
                    w = slice(k * P, (k + 1) * P)
                    mm(o, wh[:, c % 2, w], hh[:, k, :], start=(k == 0), stop=False)
                    mm(o, wh[:, c % 2, w], hl[:, k, :], start=False, stop=False)
                    last = mm(o, wl[:, c % 2, w], hh[:, k, :], start=False, stop=(k == KD - 1))
                last.then_inc(unit_done, 1)

            def reduce_modulation(n, bank):
                for i in range(n):
                    for j in range(4):
                        last = mm(ps[:, bank, 4 * i + j:4 * i + j + 1], acc[:, i, j * P:(j + 1) * P], one,
                                  start=True, stop=True)
                last.then_inc(mod_full, 1)

            def prenorm(i):
                pe.wait_ge(xn_done, T * (i + 1))
                for b in range(8):
                    for kk in range(2):
                        k = 2 * b + kk
                        for t in range(T):
                            last = pe.transpose(ps[:, b, kk * SEQ + t * P:kk * SEQ + (t + 1) * P],
                                                Xn[:, t, k * P:(k + 1) * P], ident)
                    last.then_inc(ht_full, 1)

            def operand(use):
                pe.wait_ge(hl_done, use * 2 + 2)
                settle()

            pe.wait_ge(loaded, 32)
            with pe.Fori(0, LAYERS) as l:
                prenorm(l)
                pe.wait_ge(nl_done, l * 8 + 8)
                settle()
                with pe.Fori(0, TM_G // 2) as i:
                    for p in range(2):
                        rows_group(l * LAYER_G + i * 2 + p, l * TM_N + i * 2 + p, p)
                with pe.Fori(0, FM_G) as i:
                    for c in range(R):
                        up(l * LAYER_G + i + TM_G, c, l * FM_C + i * R + c)
                pe.wait_ge(qk_ready, 2 * (l + 1))
                pe.wait_ge(fm_free, (l + 1) * FM_C + R)
                pe.wait_ge(a_used, l * (ADA_LAYER * ADA_H) + ((ADA_TM + ADA_FM) * ADA_H + 2))
                reduce_modulation(ADA_TM + ADA_FM, 4)
                pe.wait_ge(mod_done, l * 2 + 1)
                for b in range(5):
                    for half in range(2):
                        for t in range(T):
                            at = (2 * b + half) * HD
                            last = pe.transpose(ps[:, b, half * SEQ + t * P:half * SEQ + (t + 1) * P],
                                                PT[:, t, at:at + HD], ident)
                    last.then_inc(tr_full, 1)
                for b in range(5, 8):
                    for half in range(2):
                        k = 2 * (b - 5) + half
                        at = B_CQ + k * P if k < 4 else B_CKV + (k - 4) * P
                        for t in range(T):
                            last = pe.transpose(ps[:, b, half * SEQ + t * P:half * SEQ + (t + 1) * P],
                                                PT[:, t, at:at + P], ident)
                    last.then_inc(tr_full, 1)
                pe.wait_ge(tr_done, 11 * (l + 1))
                gl = l * LAYER_G + TM_G + FM_G
                unit(gl, 0)
                for c in range(4):
                    for k in range(4):
                        last = mm(ps[:, c // 2, (c % 2) * SEQ:(c % 2 + 1) * SEQ],
                                  ring[:, 0, k * 512 + c * P:k * 512 + (c + 1) * P], cqT[:, k, :],
                                  start=(k == 0), stop=(k == 3))
                last.then_inc(unit_done, 1)
                unit(gl, 1)
                for t in range(T):
                    for k in range(4):
                        last = mm(ps[:, 4, t * 256:(t + 1) * 256], cqT[:, k, t * P:(t + 1) * P],
                                  ring[:, 1, k * 256:(k + 1) * 256], start=(k == 0), stop=(k == 3))
                last.then_inc(unit_done, 1)
                for t in range(T):
                    last = pe.transpose(ps[0:64, 7, t * P:(t + 1) * P], krot[:, 0, t, :], ident)
                last.then_inc(kpe_full, 1)
                unit(gl, 2)
                unit(gl, 3)
                for c in range(4):
                    for k in range(2):
                        last = mm(ps[:, 2 + c // 2, (c % 2) * SEQ:(c % 2 + 1) * SEQ],
                                  ring[:, 2, k * 1024 + c * P:k * 1024 + (c + 1) * P], ckvT[:, k, :],
                                  start=(k == 0), stop=(k == 1))
                for t in range(T):
                    for k in range(2):
                        last = mm(ps[:, 5 + t, :], ckvT[:, k, t * P:(t + 1) * P],
                                  ring[:, 2, k * 1024 + 512:(k + 1) * 1024], start=(k == 0), stop=(k == 1))
                last.then_inc(unit_done, 2)
                pe.wait_ge(qpe_ready, l + 1)
                pe.wait_ge(lat_done, 3 * (l + 1))
                settle()
                for h in range(4):
                    for t in range(T):
                        last = pe.transpose(ps[0:64, h // 2, (h % 2) * SEQ + t * P:(h % 2) * SEQ + (t + 1) * P],
                                            qpe[:, t, h, :], ident)
                last.then_inc(qpt_full, 1)
                pe.wait_ge(qpt_done, l + 1)
                pe.wait_ge(kpe_done, l + 1)

                def scores(i):
                    for h in range(4):
                        for t in range(T):
                            o = ps[:, h, t * SEQ:(t + 1) * SEQ]
                            q = slice(t * P, (t + 1) * P)
                            if i < 2:
                                last = mm(o, qkT[:, 4 * i + h, q], qkT[:, 8 + i, :], start=True, stop=True)
                            elif i == 2:
                                mm(o, qnT[:, h, q], knT[:, h, :], start=True, stop=False)
                                last = mm(o, qpT[0:64, h, q], kpT[0:64, :], start=False, stop=True)
                            else:
                                last = mm(o, PF[:, C_Q + h, q], PF[:, C_K + h, :], start=True, stop=True)
                    last.then_inc(s_full, 1)

                scores(0)
                for i in range(4):
                    if i < 3:
                        pe.wait_ge(exp_done, 4 * l + (i + 1))
                        scores(i + 1)
                    pe.wait_ge(p_ready, 4 * l + (i + 1))
                    for h in range(4):
                        for kt in range(T):
                            for t in range(T):
                                last = pe.transpose(ps[:, 4 + h, kt * SEQ + t * P:kt * SEQ + (t + 1) * P],
                                                    prob[:, h, t, kt * P:(kt + 1) * P], ident)
                    last.then_inc(t_full, 1)
                    pe.wait_ge(pt_done, 8 * l + 2 * (i + 1))
                    for h in range(4):
                        for kt in range(T):
                            v = (PT[:, kt, A_V + i * HD:A_V + (i + 1) * HD] if i < 2 else
                                 vB[:, kt, h * HD:(h + 1) * HD] if i == 2 else
                                 PT[:, kt, C_V + h * HD:C_V + (h + 1) * HD])
                            last = mm(ps[:, 4 + h // 2, (h % 2) * SEQ:(h % 2 + 1) * SEQ], v, probT[:, h, kt, :],
                                      start=(kt == 0), stop=(kt == 1))
                    last.then_inc(pv_full, 1)
                    pe.wait_ge(o_done, 4 * l + (i + 1))
                operand(l)
                with pe.Fori(0, WO_G // 2) as i:
                    for p in range(2):
                        rows_group(l * LAYER_G + i * 2 + (TM_G + FM_G + LAT_G + p), l * TM_N + i * 2 + (TM_G + p), p)
                pe.wait_ge(a_used, (l + 1) * (ADA_LAYER * ADA_H) + 2)
                reduce_modulation(ADA_WO, 4)

            prenorm(LAYERS)
            operand(LAYERS)
            for i in range(TM2_G):
                rows_group(G_TM2 + i, N_TM2 + i, i % 2)
            pe.wait_ge(c2_ready, 16)
            for t in range(T):
                for k in range(KD):
                    last = mm(ps[:, 4, t * NGATE:(t + 1) * NGATE], hT[:, k, t * P:(t + 1) * P],
                              c2("w_gate", KD, NGATE)[:, k, :], start=(k == 0), stop=(k == KD - 1))
            last.then_inc(gates_full, 1)
            pe.wait_ge(gw_done, 1)
            with pe.Fori(0, FM2_G) as i:
                for c in range(R):
                    up(i + G_FM2, c, i * R + (N_FM + c))
            pe.wait_ge(a_used, A_WO2 * ADA_H + 2)
            pe.wait_ge(fm_free, N_WQ + R)
            reduce_modulation(ADA_TM2 + ADA_FM2, 5)
            pe.wait_ge(mod_done, 2 * LAYERS + 1)
            for w in range(2):
                pe.wait_ge(cin_done, w + 1)
                for u in range(2):
                    unit(G_CMP, 2 * w + u)
                    for j in range(16):
                        last = mm(ps[:, 4 + 3 * w, 0:4 * NCMP], ring[:, 2 * w + u, j * P:(j + 1) * P],
                                  cmp_in[w][:, :, 16 * u + j, :], start=(u == 0 and j == 0), stop=(u == 1 and j == 15))
                    last.then_inc(unit_done, 1)
            pe.wait_ge(hid_done, 1)
            mm(ps[:, 5, 0:4 * NCMP], c2("w2k"), hid[:, 0, 0:4 * NCMP], start=True, stop=True).then_inc(kc_full, 1)
            pe.wait_ge(hid_done, 2)
            for q in range(4):
                last = mm(ps[0:NCMP, 6, q * NSA_D:(q + 1) * NSA_D], hid[:, 1, q * NCMP:(q + 1) * NCMP],
                          c2("w2v"), start=True, stop=True)
            last.then_inc(kc_full, 1)
            pe.wait_ge(kc_done, 2)
            pe.wait_ge(vc_done, 1)
            for t in range(T):
                for h in range(NSA_HEADS):
                    c, half = nsa_chunk(h)
                    at = (t * NSA_HEADS + h) * NCMP
                    last = mm(ps[:, 7, at:at + NCMP], PF2[:, NQ + c, t * P:(t + 1) * P],
                              kcz[:, half * 2 + h // 8, 0:NCMP], start=True, stop=True)
            last.then_inc(cs_full, 1)
            pe.wait_ge(ce_done, 1)
            for j in range(T * NSA_HEADS):
                last = pe.transpose(ps[0:NCMP, j // 4, (j % 4) * P:(j % 4 + 1) * P], cprob[:, j, :], ident)
            last.then_inc(ct_full, 1)
            pe.wait_ge(ct_done, 2)
            for j in range(T * NSA_HEADS):
                h = j % NSA_HEADS
                last = mm(ps[:, j // 8, (j % 8) * NSA_D:(j % 8 + 1) * NSA_D], cprobT[0:NCMP, j, :],
                          vcmp[0:NCMP, nsa_chunk(h)[1] * 2 + h // 8, :], start=True, stop=True)
            last.then_inc(cpv_full, 1)
            pe.wait_ge(co_done, 1)
            pe.wait_ge(kz_done, 1)

            def nscores(i):
                g, br = i // 2, i % 2
                for r in range(4):
                    c, half = nsa_chunk(4 * g + r)
                    k = kz[:, br, half * 2 + g // 2, :]
                    mm(ps[:, r, 0:P], PF2[:, NQ + c, 0:P], k[:, 0:P], start=True, stop=True)
                    last = mm(ps[:, r, P:3 * P], PF2[:, NQ + c, P:SEQ], k, start=True, stop=True)
                last.then_inc(n_full, 1)

            def rscores(i):
                for r in range(4):
                    q, k = PF2[:, RQ + 4 * i + r, :], PF2[:, RK + 4 * i + r, :]
                    mm(ps[:, r, 0:SEQ], k[:, 0:P], q, start=True, stop=True)
                    last = mm(ps[:, r, SEQ:3 * P], k[:, P:SEQ], q[:, P:SEQ], start=True, stop=True)
                last.then_inc(n_full, 1)

            nscores(0)
            pe.wait_ge(n_nb, 1)
            nscores(1)
            for i in range(8):
                g, br = i // 2, i % 2
                pe.wait_ge(n_exp, i + 1)
                for r in range(4):
                    for j in range(3):
                        last = pe.transpose(ps[:, 4 + r, j * P:(j + 1) * P], nprob[i % 2][:, r, j * P:(j + 1) * P], ident)
                last.then_inc(n_t, 1)
                if i < 7:
                    pe.wait_ge(n_nb, i + 2)
                    if i < 6:
                        nscores(i + 2)
                    else:
                        rscores(0)
                pe.wait_ge(n_pt, 2 * (i + 1))
                v = [PT2[:, kt, (V_W if br else V_S) + g * NSA_D:(V_W if br else V_S) + (g + 1) * NSA_D] for kt in range(2)]
                for r in range(4):
                    mm(ps[:, 4, r * NSA_D:(r + 1) * NSA_D], nprobT[:, r, 0:P], v[0], start=True, stop=True)
                    o = ps[:, 4, (4 + r) * NSA_D:(5 + r) * NSA_D]
                    mm(o, nprobT[:, r, P:2 * P], v[0], start=True, stop=False)
                    last = mm(o, nprobT[:, r, 2 * P:3 * P], v[1], start=False, stop=True)
                last.then_inc(n_pv, 1)
                pe.wait_ge(n_out, i + 1)
            for i in range(2):
                pe.wait_ge(r_ready, i + 1)
                if i == 0:
                    rscores(1)
                else:
                    pe.wait_ge(yret_done, 1)
                for r in range(4):
                    h = 4 * i + r
                    v = [PT2[:, st, V_R + h * HD:V_R + (h + 1) * HD] for st in range(2)]
                    o = ps[:, 4 + r // 2, (r % 2) * SEQ:(r % 2 + 1) * SEQ]
                    a = nprob[i % 2][:, r, :]
                    mm(o[:, 0:P], a[:, 0:P], v[0], start=True, stop=True)
                    mm(o[:, P:SEQ], a[:, P:SEQ], v[0], start=True, stop=False)
                    last = mm(o[:, P:SEQ], a[:, SEQ:3 * P], v[1], start=False, stop=True)
                last.then_inc(n_pv, 1)
            for kind in range(2):
                pe.wait_ge(n_normed, kind + 1)
                if kind == 0:
                    pe.wait_ge(yret_done, 2)
                for c in range(8):
                    for t in range(T):
                        src = (onsa[:, t * NSA_HEADS + 2 * c:t * NSA_HEADS + 2 * c + 2, :].rearrange("p a b -> p (a b)")
                               if kind == 0 else yret[:, t * RET_HEADS + c, :])
                        last = pe.transpose(ps[:, 4 * kind + c // 2, (c % 2) * SEQ + t * P:(c % 2) * SEQ + (t + 1) * P],
                                            src, ident)
                    if c % 2:
                        last.then_inc(ot_full, 1)
            pe.wait_ge(ot_done, 16)
            def gate_row(j, bank):
                for k in range(KD):
                    last = mm(ps[:, bank + k // 4, (k % 4) * P:(k % 4 + 1) * P],
                              mod[:, j * KD + k:j * KD + k + 1].to_broadcast([P, P]), ident, start=True, stop=True)
                return last

            gate_row(2, 4).then_inc(g1_full, 1)
            operand(LAYERS + 1)
            for i in range(WO_G):
                rows_group(G_WO2 + i, N_WO2 + i, i % 2)
            pe.wait_ge(a_used, ADA_CG * ADA_H + 2)
            pe.wait_ge(tm_free, N_WO2 + WO_G + 1)
            reduce_modulation(ADA_WO2, 0)
            prenorm(LAYERS + 1)

            def batch(n, b, bank):
                pe.wait_ge(hot_done, n + 1)
                for j in range(BATCH):
                    last = mm(ps[:, bank, j * 2 * PART:(j + 1) * 2 * PART], hot1[:, b, j, :],
                              hot2[:, j, :, :].rearrange("p a b -> p (a b)"), start=True, stop=True)
                last.then_inc(g_full, 1)

            def up_quarter(q):
                g0, n0 = G_OF[f"U{q}"], N_U + q * PART
                b0 = (q - 1) * PART
                if q > 1:
                    pe.wait_ge(y_used, 2 * (q - 1))
                with pe.Fori(0, PART_G) as i:
                    for c in range(R):
                        if q:
                            batch(i * R + (b0 + c), c % 2, c % 2)
                        up(i + g0, c, i * R + (n0 + c))

            def down(g, c, first, last_unit):
                split(g, c)
                for t in range(T):
                    tok = slice(t * P, (t + 1) * P)
                    passes = [(stage_h, wh), (stage_h, wl), (stage_l, wh)]
                    for j, (lhs, rhs) in enumerate(passes):
                        for d in range(4):
                            last = mm(ps[:, 4 * t + d, :], lhs[:, c % 2, tok], rhs[:, c % 2, d * 512:(d + 1) * 512],
                                      start=first and j == 0, stop=last_unit and j == 2, skip_group_check=True)
                last.then_inc(unit_done, 1)

            def down_quarter(q):
                pe.wait_ge(g_used, (q + 1) * PART)
                pe.wait_ge(fm_free, N_U + min(q + 2, PARTS) * PART + R)
                if q == PARTS - 1:
                    pe.wait_ge(y_used, 2 * PARTS)
                g0 = G_OF[f"V{q}"]
                for c in range(R):
                    down(g0, c, c == 0, False)
                with pe.Fori(g0 + 1, g0 + PART_G - 1) as g:
                    for c in range(R):
                        down(g, c, False, False)
                for c in range(R):
                    down(g0 + PART_G - 1, c, False, c == R - 1)

            def down_half_unit(g, c, p, first, last_unit):
                split(g, c)
                for i2 in range(2):
                    for t in range(T):
                        tok = slice(t * P, (t + 1) * P)
                        for j, (part, rhs) in enumerate(((0, wh), (0, wl), (1, wh))):
                            for d in range(2):
                                at = i2 * (DM // 2) + d * 512
                                last = mm(ps[:, 4 * t + 2 * p + d, :], pairs[c % 2][:, part, i2, tok], rhs[:, c % 2, at:at + 512],
                                          start=first and i2 == 0 and j == 0, stop=last_unit and i2 == 1 and j == 2,
                                          skip_group_check=True)
                last.then_inc(unit_done, 1)

            def down_halves(q):
                pe.wait_ge(g_used, (q + 1) * PART)
                pe.wait_ge(fm_free, N_U + PARTS * PART + R)
                for p in range(2):
                    g0, n0 = G_OF[HALVED] + p * PASS_G, (q + 1) * PART + p * PASS_G * R
                    if p:
                        pe.wait_ge(g_used, n0)
                        pe.wait_ge(y_used, 2 * q + 2)

                    def slots(i, first, end):
                        for c in range(R):
                            batch(i * R + (n0 + c), c % 2, c % 2 + 2 * (1 - p))
                            down_half_unit(i + g0, c, p, first and c == 0, end and c == R - 1)

                    slots(0, True, False)
                    with pe.Fori(1, PASS_G - 1) as i:
                        slots(i, False, False)
                    slots(PASS_G - 1, False, True)

            operand(LAYERS + 2)
            with pe.Fori(0, WQ_G) as i:
                for c in range(R):
                    up(i + G_WQ, c, i * R + (N_WQ + c))
            pe.wait_ge(fm_free, N_U + R)
            pe.wait_ge(keys_ready, 16)
            for t in range(T):
                for j in range(16):
                    last = mm(ps[:, 4 * t + j // 4, (j % 4) * P:(j % 4 + 1) * P], qP[:, j, t * P:(t + 1) * P],
                              keyT[:, j, :], start=True, stop=True)
            last.then_inc(sc_full, 1)
            pe.wait_ge(sc_done, 2)
            gate_row(5, 0).then_inc(g2_full, 1)
            up_quarter(0)
            pe.wait_ge(g2_done, 1)
            pe.wait_ge(routed, T)
            for a in range(3):
                for t in range(T):
                    last = pe.transpose(ps[:, a, t * P:(t + 1) * P], route[:, a, t, :], ident)
            last.then_inc(rt_full, 1)
            up_quarter(1)
            down_quarter(0)
            up_quarter(2)
            down_quarter(1)
            up_quarter(3)
            down_halves(2)
            down_quarter(PARTS - 1)

        @blk.scalar
        def _(act):
            def f(o, i, func, **kw):
                return nc.scalar.activation(o, i, func, **kw)

            def square_sums(i):
                for t in range(T):
                    act.wait_ge(x_done, T * i + (t + 1))
                    f(Xn[:, t, :], X[:, t, :], ACT.Square, accum_out=ss2[:, t:t + 1]).then_inc(sq_done, 1)

            def prenorm(i, scale, shift):
                square_sums(i)
                for b in range(1, 8, 2):
                    act.wait_ge(ht_full, 8 * i + (b + 1))
                    for kk in range(2):
                        k = 2 * b + kk
                        f(hT[:, k, :], ps[:, b, kk * SEQ:(kk + 1) * SEQ], ACT.Identity, scale=scale(k),
                          bias=shift(k)).then_inc(ht_done, 1)

            def high_operand(src):
                for half in range(2):
                    k = slice(half * 8, half * 8 + 8)
                    f(hh[:, k, :], src[:, k, :], ACT.Copy).then_inc(hh_done, 1)

            def high(g, c, free=False):
                act.wait_ge(w_ready[c], 16 * (g + 1))
                if not free:
                    act.wait_ge(unit_done, g * R + (c - 1))
                return f(wh[:, c % 2, :], ring[:, c, :], ACT.Copy)

            def next_high(g, c, free=False):
                high(g + (c + 1) // R, (c + 1) % R, free).then_inc(hi_done, 1)

            def rows_slots(dst, g, col, pair, free=False):
                for c in range(R):
                    next_high(g, c, free and c == 0)
                rows_out(dst, g, col, pair)

            def rows_out(dst, g, col, pair):
                act.wait_ge(unit_done, g * R + R)
                f(dst[:, :, bass.ds(col, 512)], ps[:, 2 * pair:2 * pair + 2, :], ACT.Copy).then_inc(tm_free, 1)

            def up_out(dst, g, c, chunk, func):
                act.wait_ge(unit_done, g * R + (c + 1))
                f(dst[:, chunk, :], ps[:, 4 + c, 0:SEQ], func).then_inc(fm_free, 1)

            def up_slots(dst, g, chunk, func, follows=True):
                for c in range(R):
                    if follows or c < R - 1:
                        next_high(g, c)
                    up_out(dst, g, c, chunk + c, func)

            high(0, 0, True).then_inc(hi_done, 1)
            act.wait_ge(loaded, 32)
            f(csilu[:, :], small_of("cond"), ACT.Silu).then_inc(c_ready, 1)
            with act.Fori(0, LAYERS) as l:
                square_sums(l)
                for b in range(8):
                    act.wait_ge(ht_full, l * 8 + (b + 1))
                    for k in (2 * b, 2 * b + 1):
                        ins = f(hh[:, k, :], ps[:, b, (k % 2) * SEQ:(k % 2 + 1) * SEQ], ACT.Copy, scale=gcol[:, k:k + 1])
                    ins.then_inc(nh_done, 1)
                for p in range(2):
                    rows_slots(PT, l * LAYER_G + p, p * 512, p, free=p == 0)
                with act.Fori(1, TM_G // 2) as i:
                    for p in range(2):
                        rows_slots(PT, l * LAYER_G + i * 2 + p, i * 1024 + p * 512, p)
                with act.Fori(0, GATE_CHUNKS // R) as i:
                    up_slots(PF, l * LAYER_G + i + TM_G, i * R, ACT.Silu)
                for i in range(GATE_CHUNKS // R, FM_G):
                    up_slots(PF, l * LAYER_G + (i + TM_G), i * R, ACT.Copy, follows=i < FM_G - 1)
                for b in range(0, 5, 2):
                    act.wait_ge(tr_full, 8 * l + (b + 1))
                    f(qkT[:, 2 * b:2 * b + 2, :], ps[:, b, :], ACT.Copy).then_inc(tr_done, 1)
                gl = l * LAYER_G + TM_G + FM_G
                act.wait_ge(unit_done, gl * R + 1)
                f(qnT, ps[:, 0:2, :], ACT.Copy).then_inc(lat_done, 1)
                act.wait_ge(unit_done, gl * R + 4)
                f(knT, ps[:, 2:4, :], ACT.Copy).then_inc(lat_done, 1)
                f(vB, ps[:, 5:7, :], ACT.Copy).then_inc(lat_done, 1)
                act.sem_inc(hi_done, R)

                def exps(i):
                    act.wait_ge(nb_done, 4 * l + (i + 1))
                    if i:
                        act.wait_ge(t_full, 4 * l + i)
                    scale = {0: HD ** -0.5, 1: HD ** -0.5, 2: (HD + 64) ** -0.5, 3: 1.0}[i]
                    for h in range(4):
                        for t in range(T):
                            src = prob[:, h, t, :] if i == 3 else ps[:, h, t * SEQ:(t + 1) * SEQ]
                            last = f(prob[:, h, t, :], src, ACT.Exp, scale=scale,
                                     bias=nb[:, i % 2, 2 * h + t:2 * h + t + 1],
                                     accum_out=rs[:, i % 2, 2 * h + t:2 * h + t + 1])
                    last.then_inc(exp_done, 1)

                exps(0)
                for i in range(4):
                    act.wait_ge(t_full, 4 * l + (i + 1))
                    f(probT[:, 0:2], ps[:, 4:6, :], ACT.Copy).then_inc(pt_done, 1)
                    if i < 3:
                        exps(i + 1)
                gw0 = l * LAYER_G + (TM_G + FM_G + LAT_G)
                high(gw0, 0).then_inc(hi_done, 1)
                act.wait_ge(o_done, 4 * l + 4)
                high_operand(OT)
                for i in range(WO_G):
                    g = l * LAYER_G + (TM_G + FM_G + LAT_G + i)
                    for c in range(R):
                        next_high(g, c)
                    act.wait_ge(unit_done, g * R + R)
                    pair = ps[:, 2 * (i % 2):2 * (i % 2) + 2, :]
                    f(Y[:, :, i * 512:(i + 1) * 512], pair, ACT.Copy)
                    for t in range(T):
                        last = f(lsquares[:, t, 0:512], pair[:, t, :], ACT.Square, accum_out=ypart[:, t, i:i + 1])
                    last.then_inc(tm_free, 1)

            act.wait_ge(gsc_done, 1)
            prenorm(LAYERS, lambda k: gsc[:, 0, k:k + 1], lambda k: mod[:, k:k + 1])
            act.wait_ge(ht_done, KD)
            high_operand(hT)
            for i in range(TM2_G):
                rows_slots(PT2, G_TM2 + i, i * 512, i % 2)
            act.wait_ge(gates_full, 1)
            f(gw, ps[:, 4, 0:T * NGATE], ACT.Sigmoid).then_inc(gw_done, 1)
            with act.Fori(0, RG // R) as i:
                up_slots(PF2, i + G_FM2, i * R, ACT.Copy)
            for i in range(RG // R, FM2_G):
                up_slots(PF2, i + G_FM2, i * R, ACT.Silu, follows=i < FM2_G - 1)
            for w in range(2):
                act.wait_ge(unit_done, G_CMP * R + 2 * (w + 1))
                f(hid[:, w, 0:4 * NCMP], ps[:, 4 + 3 * w, 0:4 * NCMP], ACT.Gelu_apprx_tanh).then_inc(hid_done, 1)
            act.sem_inc(hi_done, R)
            act.wait_ge(cs_done, 1)
            f(cprob, cprob, ACT.Exp).then_inc(ce_done, 1)
            act.wait_ge(ct_full, 1)
            f(cprobT[0:NCMP, 0:16, :], ps[0:NCMP, 0:4, :], ACT.Copy).then_inc(ct_done, 1)

            def nexps(i):
                act.wait_ge(n_nb, i + 1)
                for t in range(T):
                    for r in range(4):
                        p = nprob[i % 2][:, r, 0:P] if t == 0 else nprob[i % 2][:, r, P:3 * P]
                        j = 4 * t + r
                        last = f(p, p, ACT.Exp, scale=NSA_D ** -0.5, bias=nb[:, i % 2, j:j + 1],
                                 accum_out=rs[:, i % 2, j:j + 1])
                last.then_inc(n_exp, 1)

            nexps(0)
            nexps(1)
            for i in range(8):
                act.wait_ge(n_t, i + 1)
                f(nprobT[:, 0:2, :], ps[:, 4:6, 0:3 * P], ACT.Copy).then_inc(n_pt, 1)
                if i < 6:
                    nexps(i + 2)
            for i in range(2):
                act.wait_ge(n_pv, 8 + i + 1)
                src = ps[:, 4:6, :].rearrange("p b (r t e) -> p t (b r) e", r=2, t=T)
                for t in range(T):
                    last = f(yret[:, t * RET_HEADS + 4 * i:t * RET_HEADS + 4 * i + 4, :], src[:, t], ACT.Copy)
                last.then_inc(yret_done, 1)
            for c in range(8):
                act.wait_ge(ot_full, c // 2 + 1)
                f(OT[:, c, :], ps[:, c // 2, (c % 2) * SEQ:(c % 2 + 1) * SEQ], ACT.Copy,
                  scale=c2("g_nsa")[:, c:c + 1]).then_inc(ot_done, 1)
            act.wait_ge(n_normed, 2)
            high(G_WO2, 0).then_inc(hi_done, 1)
            act.wait_ge(ot_done, 16)
            high_operand(OT)
            for i in range(WO_G):
                rows_slots(Y, G_WO2 + i, i * 512, i % 2)
            act.wait_ge(gsc_done, 2)
            prenorm(LAYERS + 1, lambda k: gsc[:, 1, k:k + 1], lambda k: mod[:, 3 * KD + k:3 * KD + k + 1])
            act.wait_ge(ht_done, KD * 2)
            high_operand(hT)

            def high_v(g, c, q):
                high(g, c)
                chunk = (g - G_OF[f"V{q}"]) * R + c
                f(stage_h[:, c % 2, :], act_e[q % 2][:, chunk, :], ACT.Copy).then_inc(hi_done, 1)

            def high_pair(g, c, chunk):
                high(g, c)
                f(pairs[c % 2][:, 0, :, :], act_e[0][:, bass.ds(chunk, 2), :], ACT.Copy).then_inc(hi_done, 1)

            def down_halves(q):
                for p in range(2):
                    g0 = G_OF[HALVED] + p * PASS_G
                    with act.Fori(0, PASS_G - 1) as i:
                        for c in range(R):
                            high_pair(i + (g0 + (c + 1) // R), (c + 1) % R, i * (2 * R) + 2 * (c + 1))
                    for c in range(R - 1):
                        high_pair(g0 + PASS_G - 1, c + 1, PART - 2 * R + 2 * (c + 1))
                    if p == 0:
                        high_pair(g0 + PASS_G, 0, 0)
                    else:
                        high(G_OF["V3"], 0)
                        act.wait_ge(g_used, PARTS * PART)
                        f(stage_h[:, 0, :], act_e[1][:, 0, :], ACT.Copy).then_inc(hi_done, 1)
                        act.wait_ge(x_done, T * (LAYERS + 5))
                    act.wait_ge(unit_done, (g0 + PASS_G) * R)
                    f(ysum2[:, 0, :], ps[:, 2 * p:2 * p + 2, :], ACT.Copy).then_inc(y_used, 1)

            def down_slots(g, q):
                for c in range(R):
                    high_v(g + (c + 1) // R, (c + 1) % R, q)

            def up_quarter(q):
                g0, dst = G_OF[f"U{q}"], act_e[q % 2]
                if q > 1:
                    act.wait_ge(unit_done, g0 * R)
                    f(ysum[q % 2][:, 0, :], ps[:, 0:4, :], ACT.Copy).then_inc(y_used, 1)
                up_slots(dst, g0, 0, ACT.Gelu_apprx_tanh)
                if q == 0:
                    act.wait_ge(g2_full, 1)
                    f(gate2row, ps[:, 0:4, :], ACT.Copy).then_inc(g2_done, 1)
                with act.Fori(1, PART_G - 1) as i:
                    up_slots(dst, i + g0, i * R, ACT.Gelu_apprx_tanh)
                g, chunk = g0 + PART_G - 1, PART - R
                for c in range(R - 1):
                    high(g, c + 1).then_inc(hi_done, 1)
                    up_out(dst, g, c, chunk + c, ACT.Gelu_apprx_tanh)
                if q == 0:
                    high(g + 1, 0).then_inc(hi_done, 1)
                    for t in range(T):
                        act.wait_ge(rexp_in, t + 1)
                        f(route[:, 2, t, :], route[:, 2, t, :], ACT.Exp).then_inc(rexp_done, 1)
                    act.wait_ge(unit_done, g * R + R)
                elif q == PARTS - 1:
                    act.wait_ge(g_used, q * PART)
                    high_pair(g + 1, 0, 0)
                else:
                    high(g + 1, 0)
                    act.wait_ge(g_used, q * PART)
                    f(stage_h[:, 0, :], act_e[(q - 1) % 2][:, 0, :], ACT.Copy).then_inc(hi_done, 1)
                up_out(dst, g, R - 1, chunk + R - 1, ACT.Gelu_apprx_tanh)

            def down_quarter(q):
                g0 = G_OF[f"V{q}"]
                with act.Fori(g0, g0 + PART_G - 1) as g:
                    down_slots(g, q)
                g = g0 + PART_G - 1
                for c in range(R - 1):
                    high_v(g, c + 1, q)
                if q < PARTS - 2:
                    high(g + 1, 0).then_inc(hi_done, 1)

            with act.Fori(0, WQ_G) as i:
                up_slots(qP, i + G_WQ, i * R, ACT.Copy)
            act.wait_ge(sc_full, 1)
            f(score[:, 0], ps[:, 0:4, :], ACT.Copy).then_inc(sc_done, 1)
            up_quarter(0)
            act.wait_ge(routed, T)
            up_quarter(1)
            down_quarter(0)
            up_quarter(2)
            down_quarter(1)
            up_quarter(3)
            down_halves(2)
            down_quarter(3)
            act.wait_ge(unit_done, GROUPS * R)
            f(ysum[1][:, 0, :], ps[:, 0:4, :], ACT.Copy).then_inc(y_used, 1)
            act.wait_ge(x_done, T * (LAYERS + 3 + PARTS))
            for t in range(T):
                f(squares[:, t, :], X[:, t, :], ACT.Square, accum_out=ss2[:, t:t + 1]).then_inc(fss_done, 1)

        @blk.gpsimd
        def _(pool):
            steps = Steps(pool, pool_step)
            pl = nc.gpsimd

            def rsqrt(parts, mean, out_ap, signal):
                pool.sem_inc(pool_passed, 1)
                for o, src, n in parts:
                    steps(pl.tensor_scalar(o, src, 1.0 / n, EPS, ALU.mult, ALU.add))
                steps.done()
                pl.tensor_tensor(out_ap, mean, power[:, 0:mean.shape[-1]], ALU.pow).then_inc(signal, 1)

            def rstd_of(i, wait_sem, signal):
                pool.wait_ge(wait_sem, T * (i + 1))
                rsqrt([(ms2, ss2, DM)], ms2, rstd2, signal)

            def modulation(first, n):
                with pool.Fori(0, n) as i:
                    for h in range(ADA_H):
                        pool.wait_ge(a_used, (first + i) * ADA_H + (h + 1))
                        pool.sem_inc(pool_passed, 1)
                        pool.dma_start(aring[:, h % 2, :], ada[first + i, h]).then_inc(a_ready[h % 2], 16)

            pool.dma_start(area(C1, CONST1_W), const1).then_inc(c1_ready, 16)
            pool.wait_ge(loaded, 32)
            with pool.Fori(0, LAYERS) as l:
                steps.region(l * POOL_STEPS)
                rstd_of(l, sq_done, prs_done)
                modulation(l * ADA_LAYER, ADA_TM)
                pool.wait_ge(qss_done, l + 1)
                rsqrt([(msq[:, 0:20], ssq[:, 0:20], HD), (msq[:, 20:22], ssq[:, 20:22], 512),
                       (msq[:, 22:24], ssq[:, 22:24], 256)], msq, rsq, qrs_done)
                modulation(l * ADA_LAYER + ADA_TM, ADA_FM)
                pool.wait_ge(unit_done, l * (LAYER_G * R) + (TM_G + FM_G) * R)
                pool.sem_inc(pool_passed, 1)
                pool.dma_start(nbias, nbr_bias[l]).then_inc(bias_ready, 16)
                pool.wait_ge(bias_ready, 16 * l + 16)
                pool.wait_ge(c1_ready, 16)
                nb8 = nbias.rearrange("p a b c -> p (a b) c")
                pl.tensor_tensor(nb8, nb8, c1("nbr")[:, None, :].to_broadcast([P, 8, SEQ]), ALU.add).then_inc(bias_masked, 1)
                pool.wait_ge(o_done, 4 * l + 4)
                pool.sem_inc(pool_passed, 1)
                pool.dma_start(gpost, g_post[l]).then_inc(gpost_ready, 16)
                modulation(l * ADA_LAYER + (ADA_TM + ADA_FM), ADA_WO)
                pool.wait_ge(tm_free, l * TM_N + (TM_N + 2))
                pool.sem_inc(pool_passed, 1)
                steps(pl.tensor_tensor(yhalf, ypart[:, :, 0:2], ypart[:, :, 2:4], ALU.add))
                steps.done()
                steps(pl.tensor_tensor(ss2, yhalf[:, :, 0], yhalf[:, :, 1], ALU.add))
                steps.done()
                rsqrt([(ms2, ss2, DM)], ms2, rstd2, yrs_done)
                assert steps.n == POOL_STEPS, steps.n
            steps.region(LAYERS * POOL_STEPS)
            pool.wait_ge(x_done, T * (LAYERS + 1))
            pool.dma_start(area(C2, CONST2_W), const2).then_inc(c2_ready, 16)
            pl.memset(kcz, 0.0).then_inc(zeroed, 1)
            rstd_of(LAYERS, sq_done, prs_done)
            modulation(A_TM2, ADA_TM2 + ADA_FM2)
            pool.wait_ge(unit_done, G_CMP * R)
            for w in range(2):
                pl.memset(cmp_in[w], 0.0).then_inc(zeroed, 1)
            pl.memset(kz, 0.0).then_inc(zeroed, 1)
            pool.wait_ge(mod_done, 2 * LAYERS + 1)
            pool.dma_start(area(0, DECAY_W), decays).then_inc(decay_ready, 16)
            pool.wait_ge(nss_done, 1)
            rsqrt([(hs, hs, NSA_D)], hs, cw, nrs_done)
            pool.wait_ge(nss_done, 2)
            rsqrt([(hs[:, 0:16], hs[:, 0:16], HD)], hs[:, 0:16], cw[:, 0:16], nrs_done)
            modulation(A_WO2, ADA_WO2)
            rstd_of(LAYERS + 1, sq_done, prs_done)
            pool.wait_ge(a_used, ADA_CG * ADA_H + 2)
            pool.dma_start(side, keys).then_inc(keys_ready, 16)
            pool.wait_ge(fss_done, T)
            rsqrt([(ms2, ss2, DM)], ms2, rstd2, frs_done)

        @blk.vector
        def _(dve):
            v = nc.vector
            st = Steps(dve, dve_step)
            tt, ts, stt = v.tensor_tensor, v.tensor_scalar, v.scalar_tensor_tensor

            def normed(i):
                dve.wait_ge(prs_done, i + 1)
                for t in range(T):
                    ts(Xn[:, t, :], X[:, t, :], rstd2[:, t:t + 1], None, ALU.mult).then_inc(xn_done, 1)

            def prenorm(i, scale, shift):
                normed(i)
                for b in range(0, 8, 2):
                    dve.wait_ge(ht_full, 8 * i + (b + 1))
                    for kk in range(2):
                        k = 2 * b + kk
                        o, src = hT[:, k, :], ps[:, b, kk * SEQ:(kk + 1) * SEQ]
                        ts(o, src, scale(k), shift(k), ALU.mult, ALU.add).then_inc(ht_done, 1)

            def low_operand(src, use):
                for half in range(2):
                    k = slice(half * 8, half * 8 + 8)
                    dve.wait_ge(hh_done, use * 2 + (half + 1))
                    tt(hl[:, k, :], src[:, k, :], hh[:, k, :].bitcast(F32), ALU.subtract).then_inc(hl_done, 1)
                dve.wait_ge(hl_done, use * 2 + 2)
                dve.sem_inc(dve_passed, 1)

            def low(g, c):
                dve.wait_ge(hi_done, g * R + (c + 1))
                return tt(wl[:, c % 2, :], ring[:, c, :], wh[:, c % 2, :].bitcast(F32), ALU.subtract)

            def next_low(g, c):
                low(g + (c + 1) // R, (c + 1) % R).then_inc(lo_done, 1)

            def modulation(cg, h, i):
                dve.wait_ge(a_ready[h % 2], cg * 64 + 16 * (h // 2 + 1))
                for kk in range(2):
                    w = aring[:, h % 2, kk * 512:(kk + 1) * 512]
                    k = 2 * h + kk
                    if k == 0:
                        ins = ts(acc[:, i, :], w, csilu[:, k:k + 1], None, ALU.mult)
                    else:
                        if kk:
                            dve.wait_ge(a_step, cg * ADA_H + (h + 1))
                        else:
                            dve.wait_ge(a_used, cg * ADA_H + (h + 2))
                        ins = stt(acc[:, i, :], w, csilu[:, k:k + 1], acc[:, i, :], ALU.mult, ALU.add)
                    ins.then_inc(a_used if kk else a_step, 1)

            def take_modulation(count, n, cols, bank):
                dve.wait_ge(mod_full, count)
                tt(mod[:, cols], ps[:, bank, 0:4 * n], small_of("b_ada")[:, cols], ALU.add).then_inc(mod_done, 1)

            def rotate(dst, src, tmp, cos, sin, heads, half):
                def split(a):
                    return a.rearrange("p h (a s n) -> p h a s n", a=2, s=2)
                n = cos.shape[-1]
                c3 = cos[:, None, :].to_broadcast([P, heads, n])
                s5 = sin.rearrange("p (a s n) -> p a s n", a=2, s=2)
                for s in range(2):
                    st(tt(split(tmp)[:, :, :, s, :], split(src)[:, :, :, 1 - s, :],
                          s5[:, None, :, s, :].to_broadcast([P, heads, 2, half]), ALU.mult))
                st.done()
                st(tt(dst, src, c3, ALU.mult))
                st.done()
                return tt(dst, dst, tmp, ALU.add)

            low(0, 0).then_inc(lo_done, 1)
            dve.wait_ge(loaded, 32)
            dve.sem_inc(tm_free, 2)
            dve.sem_inc(fm_free, 4)
            dve.sem_inc(a_used, 2)
            dve.sem_inc(x_done, 2)
            dve.wait_ge(c_ready, 1)
            dve.wait_ge(c1_ready, 16)
            with dve.Fori(0, LAYERS) as l:
                st.region(l * DVE_STEPS)
                st(v.tensor_copy(gcol, g_pre[:, l, :]))
                st(v.tensor_copy(glat[:, 0:4], g_cq[:, l, :]))
                st(v.tensor_copy(glat[:, 4:6], g_ckv[:, l, :]))
                st.done()
                normed(l)
                for b in range(8):
                    dve.wait_ge(nh_done, l * 8 + (b + 1))
                    for k in (2 * b, 2 * b + 1):
                        ins = stt(hl[:, k, :], ps[:, b, (k % 2) * SEQ:(k % 2 + 1) * SEQ], gcol[:, k:k + 1],
                                  hh[:, k, :].bitcast(F32), ALU.mult, ALU.subtract)
                    ins.then_inc(nl_done, 1)
                dve.wait_ge(nl_done, l * 8 + 8)
                dve.sem_inc(dve_passed, 1)

                with dve.Fori(0, ADA_TM) as i:
                    for p in range(2):
                        for c in range(R):
                            next_low(l * LAYER_G + i * 2 + p, c)
                            modulation(l * ADA_LAYER + i, p * R + c, i)

                def squares_of(t):
                    sq = (rot1, rot2)[t]
                    qk = PT[:, t, 0:QK_HEADS * HD].rearrange("p (h d) -> p h d", d=HD)
                    st(tt(sq, qk, qk, ALU.mult))
                    cq, ckv = PT[:, t, B_CQ:B_CQ + 512], PT[:, t, B_CKV:B_CKV + 256]
                    st(stt(junk[t], cq, 1.0, cq, ALU.mult, ALU.mult, accum_out=ssq[:, 20 + t:21 + t]))
                    st.done()
                    st(stt(junk[t][:, 0:256], ckv, 1.0, ckv, ALU.mult, ALU.mult, accum_out=ssq[:, 22 + t:23 + t]))
                    st(v.tensor_reduce(ssq[:, 10 * t:10 * t + 10], sq, AX, ALU.add))
                    st.done()

                def latents():
                    for t in range(T):
                        for at, n, j in ((B_CQ, 512, 20), (B_CKV, 256, 22)):
                            st(ts(PT[:, t, at:at + n], PT[:, t, at:at + n], rsq[:, j + t:j + t + 1], None, ALU.mult))

                def positions():
                    for t in range(T):
                        st(rotate(krot[:, 0, t:t + 1, :], PT[:, t:t + 1, B_KR:B_KR + 64], krot[:, 1, t:t + 1, :],
                                  c1("cos_b", T, 64)[:, t, :], c1("sin_b", T, 64)[:, t, :], 1, 16))

                g_qk = c1("g_qk", LAYERS, 2, HD)

                def gains(t):
                    qk = PT[:, t, 0:QK_HEADS * HD].rearrange("p (h d) -> p h d", d=HD)
                    st(tt(rot1, qk, rsq[:, 10 * t:10 * t + 10].unsqueeze(2).to_broadcast([P, QK_HEADS, HD]), ALU.mult))
                    st.done()
                    st(tt(rot1[:, 0:8], rot1[:, 0:8], g_qk[:, l, 0, :].unsqueeze(1).to_broadcast([P, 8, HD]), ALU.mult))
                    st(tt(rot1[:, 8:10], rot1[:, 8:10], g_qk[:, l, 1, :].unsqueeze(1).to_broadcast([P, 2, HD]), ALU.mult))
                    st.done()

                def turn(t):
                    qk = PT[:, t, 0:QK_HEADS * HD].rearrange("p (h d) -> p h d", d=HD)
                    rotate(qk, rot1, rot2, c1("cos", T, HD)[:, t, :], c1("sin", T, HD)[:, t, :], QK_HEADS, 32).then_inc(qk_ready, 1)
                    dve.wait_ge(qk_ready, l * 2 + (t + 1))

                for j in range(FM_G * R):
                    if j < FM_G * R - 1:
                        next_low(l * LAYER_G + (TM_G + j // R), j % R)
                    if j == 1:
                        dve.wait_ge(tm_free, l * TM_N + (TM_G + 2))
                        squares_of(0)
                    elif j == 2:
                        squares_of(1)
                        dve.sem_inc(qss_done, 1)
                    elif j == 3:
                        positions()
                    elif j == 4:
                        dve.wait_ge(qrs_done, l + 1)
                        latents()
                    elif j in (5, 7):
                        gains((j - 5) // 2)
                    elif j in (6, 8):
                        turn((j - 6) // 2)
                    a = j - (FM_G * R - ADA_FM * ADA_H)
                    if a >= 0:
                        modulation(l * ADA_LAYER + (ADA_TM + a // ADA_H), a % ADA_H, ADA_TM + a // ADA_H)
                take_modulation(l * 2 + 1, ADA_TM + ADA_FM, bass.ds(l * (4 * ADA_LAYER), 4 * (ADA_TM + ADA_FM)), 4)
                for b in (1, 3):
                    dve.wait_ge(tr_full, 8 * l + (b + 1))
                    v.tensor_copy(qkT[:, 2 * b:2 * b + 2, :], ps[:, b, :].rearrange("p (a b) -> p a b", a=2)).then_inc(tr_done, 1)
                for k in range(6):
                    dve.wait_ge(tr_full, 8 * l + (6 + k // 2))
                    o = cqT[:, k, :] if k < 4 else ckvT[:, k - 4, :]
                    ts(o, ps[:, 5 + k // 2, (k % 2) * SEQ:(k % 2 + 1) * SEQ], glat[:, k:k + 1], None,
                       ALU.mult).then_inc(tr_done, 1)
                gl = l * LAYER_G + TM_G + FM_G
                dve.wait_ge(unit_done, gl * R + 2)
                for t in range(T):
                    ins = rotate(qpe[:, t], ps[:, 4, t * 256:(t + 1) * 256].rearrange("p (h n) -> p h n", h=4), qpe2[:, t],
                                 c1("cos_b", T, 64)[:, t, :], c1("sin_b", T, 64)[:, t, :], 4, 16)
                    if t < T - 1:
                        st(ins)
                    else:
                        st.done()
                        ins.then_inc(qpe_ready, 1)
                dve.wait_ge(kpe_full, l + 1)
                v.tensor_copy(kpT[0:64, :], ps[0:64, 7, 0:SEQ]).then_inc(kpe_done, 1)
                dve.wait_ge(qpt_full, l + 1)
                v.tensor_copy(qpT[0:64].rearrange("p a b -> p (a b)"), ps[0:64, 0:2, :].rearrange("p a b -> p (a b)")).then_inc(qpt_done, 1)
                dve.wait_ge(unit_done, gl * R + R)
                dve.sem_inc(lo_done, R)

                def maxima(i):
                    dve.wait_ge(s_full, 4 * l + (i + 1))
                    src = ps[:, 0:4, :].rearrange("p h (t k) -> p (h t) k", t=T)
                    p8 = prob.rearrange("p h t k -> p (h t) k")
                    scale = {0: HD ** -0.5, 1: HD ** -0.5, 2: (HD + 64) ** -0.5, 3: 1.0}[i]
                    if i == 3:
                        dve.wait_ge(bias_masked, l + 1)
                        dve.wait_ge(t_full, 4 * l + 3)
                        stt(prob.rearrange("p h t k -> p (h t k)"), ps[:, 0:4, :].rearrange("p h k -> p (h k)"), HD ** -0.5,
                            nbias.rearrange("p h t k -> p (h t k)"), ALU.mult, ALU.add).then_inc(s_masked, 1)
                        dve.wait_ge(s_masked, l + 1)
                        src = p8
                    st(v.tensor_reduce(mx[:, i % 2, :], src, AX, ALU.max))
                    st.done()
                    ts(nb[:, i % 2, :], mx[:, i % 2, :], -scale, None, ALU.mult).then_inc(nb_done, 1)

                maxima(0)
                for i in range(4):
                    dve.wait_ge(exp_done, 4 * l + (i + 1))
                    st(v.reciprocal(rinv[:, i % 2, :], rs[:, i % 2, :]))
                    st.done()
                    p8 = prob.rearrange("p h t k -> p (h t) k")
                    tt(p8, p8, rinv[:, i % 2, :].unsqueeze(2).to_broadcast([P, 8, SEQ]), ALU.mult).then_inc(p_ready, 1)
                    if i < 2:
                        maxima(i + 1)
                    dve.wait_ge(t_full, 4 * l + (i + 1))
                    v.tensor_copy(probT[:, 2:4].rearrange("p h t k -> p (h t k)"),
                                  ps[:, 6:8, :].rearrange("p h k -> p (h k)")).then_inc(pt_done, 1)
                    if i == 2:
                        maxima(3)
                    elif i == 3:
                        low(gl + LAT_G, 0).then_inc(lo_done, 1)
                    dve.wait_ge(pv_full, 4 * l + (i + 1))
                    heads = slice(4 * i, 4 * i + 4)
                    tt(OT[:, heads, :].rearrange("p h k -> p (h k)"), ps[:, 4:6, :].rearrange("p h k -> p (h k)"),
                       PF[:, heads, :].rearrange("p h k -> p (h k)"), ALU.mult).then_inc(o_done, 1)

                dve.wait_ge(o_done, 4 * l + 4)
                low_operand(OT, l)
                with dve.Fori(0, ADA_WO) as i:
                    for p in range(2):
                        for c in range(R):
                            next_low(l * LAYER_G + i * 2 + (TM_G + FM_G + LAT_G + p), c)
                            modulation(l * ADA_LAYER + i + (ADA_TM + ADA_FM), p * R + c, i)
                take_modulation(l * 2 + 2, ADA_WO, bass.ds(l * (4 * ADA_LAYER) + 4 * (ADA_TM + ADA_FM), 4 * ADA_WO), 4)

                dve.wait_ge(yrs_done, l + 1)
                dve.wait_ge(gpost_ready, 16 * l + 16)
                for t in range(T):
                    st(stt(Y[:, t, :], Y[:, t, :], rstd2[:, t:t + 1], gpost, ALU.mult, ALU.mult))
                    st.done()
                    tt(X[:, t, :], X[:, t, :], Y[:, t, :], ALU.add).then_inc(x_done, 1)
                dve.wait_ge(x_done, T * l + 2 * T)
                assert st.n == DVE_STEPS, st.n

            st.region(LAYERS * DVE_STEPS)
            dve.wait_ge(mod_done, 2 * LAYERS)

            def scales(a, j):
                stt(gsc[:, a, :], mod[:, j * KD:(j + 1) * KD], 1.0, g_pre[:, LAYERS + a, :], ALU.add, ALU.mult).then_inc(gsc_done, 1)
                dve.wait_ge(gsc_done, a + 1)

            scales(0, 1)
            prenorm(LAYERS, lambda k: gsc[:, 0, k:k + 1], lambda k: mod[:, k:k + 1])
            dve.wait_ge(ht_done, KD)
            low_operand(hT, LAYERS)
            with dve.Fori(0, TM2_G) as i:
                for c in range(R):
                    next_low(i + G_TM2, c)
                    for h in (2 * c, 2 * c + 1):
                        modulation(i + A_TM2, h, i)

            def column_slots(i, end):
                for j in range(2 * R):
                    if j < 2 * R - 1 or not end:
                        next_low(i * 2 + (G_FM2 + j // R), j % R)
                    modulation(i + A_FM2, j, i + ADA_TM2)

            with dve.Fori(0, ADA_FM2 - 1) as i:
                column_slots(i, False)
            column_slots(ADA_FM2 - 1, True)
            dve.wait_ge(c2_ready, 16)
            dve.wait_ge(fm_free, N_WQ + R)
            pe_cols = c2("pe", 2, CMP_LEN)
            for w, chunk in ((0, KC), (1, VC)):
                dve.wait_ge(zeroed, w + 2)
                for half in range(2):
                    rows = slice(half * 64, half * 64 + 64)
                    for gp in range(2):
                        for a in range(2):
                            src = PF2[rows, chunk + gp, :].rearrange("p (n b) -> p b n", b=16)[:, :, a:a + NCMP]
                            last = tt(cmp_in[w][rows, half * 2 + gp, 16 * a:16 * a + 16, :], src,
                                      pe_cols[rows, w, 16 * a:16 * a + 16].unsqueeze(2).to_broadcast([64, 16, NCMP]), ALU.add)
                last.then_inc(cin_done, 1)
                if w == 0:
                    take_modulation(2 * LAYERS + 1, ADA_TM2 + ADA_FM2,
                                    slice(4 * A_TM2, 4 * A_WO2), 5)
            dve.wait_ge(zeroed, 4)
            for br, chunk in ((0, KS), (1, KW)):
                for half in range(2):
                    rows = slice(half * 64, half * 64 + 64)
                    last = v.tensor_copy(kz[rows, br, half * 2:half * 2 + 2, :], PF2[rows, chunk:chunk + 2, :])
            last.then_inc(kz_done, 1)
            dve.wait_ge(kc_full, 1)
            for half in range(2):
                rows = slice(half * 64, half * 64 + 64)
                v.tensor_copy(kcz[rows, half * 2:half * 2 + 2, 0:NCMP],
                              ps[rows, 5, half * 2 * NCMP:(half * 2 + 2) * NCMP].rearrange("p (a b) -> p a b", a=2)).then_inc(kc_done, 1)
            dve.wait_ge(kc_full, 2)
            dve.wait_ge(unit_done, G_CMP * R + R)
            dve.sem_inc(lo_done, R)
            v.tensor_copy(vcmp[0:NCMP].rearrange("p a b -> p (a b)"), ps[0:NCMP, 6, 0:4 * NSA_D]).then_inc(vc_done, 1)
            dve.wait_ge(cs_full, 1)
            cp = cprob.rearrange("p a b -> p (a b)")
            st(stt(cp, ps[:, 7, 0:T * NSA_HEADS * NCMP], NSA_D ** -0.5, c2("cmp_bias"), ALU.mult, ALU.add))
            st.done()
            st(v.tensor_reduce(cmx, cprob, AX, ALU.max))
            st.done()
            tt(cprob, cprob, cmx.unsqueeze(2).to_broadcast([P, 32, NCMP]), ALU.subtract).then_inc(cs_done, 1)
            dve.wait_ge(ce_done, 1)
            dve.wait_ge(gw_done, 1)
            st(v.tensor_reduce(crs, cprob, AX, ALU.add))
            st.done()
            st(v.reciprocal(cmx, crs))
            st.done()
            gwv = gw.rearrange("p t (h b) -> p t h b", b=3)
            for t in range(T):
                cols = slice(t * NSA_HEADS, (t + 1) * NSA_HEADS)
                st(stt(cw[:, cols], cmx[:, cols], c2("row_ok")[:, t:t + 1], gwv[:, t, :, 0], ALU.mult, ALU.mult))
            dve.wait_ge(ct_full, 1)
            v.tensor_copy(cprobT[0:NCMP, 16:32, :].rearrange("p a b -> p (a b)"),
                          ps[0:NCMP, 4:8, :].rearrange("p a b -> p (a b)")).then_inc(ct_done, 1)
            dve.wait_ge(cpv_full, 1)
            st.done()
            tt(onsa, ps[:, 0:4, :].rearrange("p b (j d) -> p (b j) d", d=NSA_D),
               cw.unsqueeze(2).to_broadcast([P, 32, NSA_D]), ALU.mult).then_inc(co_done, 1)
            dve.wait_ge(co_done, 1)

            dist = c2("dist")

            def nmax(i):
                g = i // 2
                dve.wait_ge(n_full, i + 1)
                if i >= 2:
                    dve.wait_ge(n_t, i - 1)
                buf = nprob[i % 2]
                for r in range(4):
                    st(stt(buf[:, r, :], dist, float(-SLOPES[4 * g + r] * NSA_D ** 0.5), ps[:, r, 0:3 * P], ALU.mult, ALU.add))
                st.done()
                st(v.tensor_reduce(mx[:, i % 2, 0:4], buf[:, :, 0:P], AX, ALU.max))
                st(v.tensor_reduce(mx[:, i % 2, 4:8], buf[:, :, P:3 * P], AX, ALU.max))
                st.done()
                ts(nb[:, i % 2, :], mx[:, i % 2, :], -NSA_D ** -0.5, None, ALU.mult).then_inc(n_nb, 1)

            def retain(i):
                dve.wait_ge(n_full, 8 + i + 1)
                dve.wait_ge(n_t, 7 + i)
                dve.wait_ge(decay_ready, 16)
                tt(nprob[i % 2], ps[:, 0:4, 0:3 * P], decay3[:, 4 * i:4 * i + 4, :], ALU.mult).then_inc(r_ready, 1)

            nmax(0)
            nmax(1)
            for i in range(8):
                g, br = i // 2, i % 2
                dve.wait_ge(n_exp, i + 1)
                st(v.reciprocal(rinv[:, i % 2, :], rs[:, i % 2, :]))
                st.done()
                wts = rinv[:, i % 2, :].rearrange("p (t r) -> p t r", t=T)
                st(tt(wts, wts, gwv[:, :, 4 * g:4 * g + 4, 1 + br], ALU.mult))
                dve.wait_ge(n_t, i + 1)
                v.tensor_copy(nprobT[:, 2:4, :], ps[:, 6:8, 0:3 * P]).then_inc(n_pt, 1)
                if i < 6:
                    nmax(i + 2)
                elif i == 6:
                    retain(0)
                dve.wait_ge(n_pv, i + 1)
                st.done()
                st(tt(ntmp.rearrange("p t r d -> p (t r) d"), ps[:, 4, :].rearrange("p (j d) -> p j d", d=NSA_D),
                      rinv[:, i % 2, :].unsqueeze(2).to_broadcast([P, 8, NSA_D]), ALU.mult))
                st.done()
                o = onsa.rearrange("p (t h) d -> p t (h d)", t=T)[:, :, 4 * g * NSA_D:(4 * g + 4) * NSA_D]
                tt(o, o, ntmp.rearrange("p t r d -> p t (r d)"), ALU.add).then_inc(n_out, 1)
                dve.wait_ge(n_out, i + 1)
            retain(1)
            sq32 = square.rearrange("p (a b) -> p a b", a=32)
            st(tt(sq32, onsa, onsa, ALU.mult))
            st.done()
            v.tensor_reduce(hs, sq32, AX, ALU.add).then_inc(nss_done, 1)
            dve.wait_ge(nrs_done, 1)
            tt(onsa, onsa, cw.unsqueeze(2).to_broadcast([P, 32, NSA_D]), ALU.mult).then_inc(n_normed, 1)
            dve.wait_ge(yret_done, 2)
            st(v.tensor_reduce(crs[:, 0:16], yret, AX, ALU.add))
            st.done()
            st(ts(crs[:, 0:16], crs[:, 0:16], 1.0 / HD, None, ALU.mult))
            st.done()
            st(tt(yret, yret, crs[:, 0:16].unsqueeze(2).to_broadcast([P, 16, HD]), ALU.subtract))
            st.done()
            dve.wait_ge(n_normed, 1)
            sq16 = square.rearrange("p (a b) -> p a b", a=16)
            st(tt(sq16, yret, yret, ALU.mult))
            st.done()
            v.tensor_reduce(hs[:, 0:16], sq16, AX, ALU.add).then_inc(nss_done, 1)
            dve.wait_ge(nrs_done, 2)
            tt(yret, yret, cw[:, 0:16].unsqueeze(2).to_broadcast([P, 16, HD]), ALU.mult).then_inc(n_normed, 1)
            for c in range(8):
                dve.wait_ge(ot_full, 4 + c // 2 + 1)
                stt(OT[:, 8 + c, :], ps[:, 4 + c // 2, (c % 2) * SEQ:(c % 2 + 1) * SEQ], c2("g_ret")[:, c:c + 1],
                    PF2[:, RG + c, :], ALU.mult, ALU.mult).then_inc(ot_done, 1)
            low(G_WO2, 0).then_inc(lo_done, 1)
            dve.wait_ge(ot_done, 16)
            low_operand(OT, LAYERS + 1)
            with dve.Fori(0, ADA_WO2) as i:
                for j in range(2 * R):
                    next_low(i * 2 + (G_WO2 + j // R), j % R)
                    modulation(i + A_WO2, j, i)
            take_modulation(2 * LAYERS + 2, ADA_WO2, slice(4 * A_WO2, 4 * ADA_CG), 0)
            dve.wait_ge(mod_done, 2 * LAYERS + 2)
            scales(1, 4)
            dve.wait_ge(tm_free, N_WO2 + WO_G + 2)
            dve.wait_ge(g1_full, 1)
            row = ps[:, 4:8, :].rearrange("p a b -> p (a b)")
            for t in range(T):
                st(tt(Y[:, t, :], Y[:, t, :], row, ALU.mult))
                st.done()
                tt(X[:, t, :], X[:, t, :], Y[:, t, :], ALU.add).then_inc(x_done, 1)
            dve.wait_ge(x_done, T * (LAYERS + 2))

            prenorm(LAYERS + 1, lambda k: gsc[:, 1, k:k + 1], lambda k: mod[:, 3 * KD + k:3 * KD + k + 1])

            def low_v(g, c, q):
                low(g, c)
                chunk = (g - G_OF[f"V{q}"]) * R + c
                tt(stage_l[:, c % 2, :], act_e[q % 2][:, chunk, :], stage_h[:, c % 2, :].bitcast(F32),
                   ALU.subtract).then_inc(lo_done, 1)

            dve.wait_ge(ht_done, KD * 2)
            low_operand(hT, LAYERS + 2)
            with dve.Fori(G_WQ, G_WQ + WQ_G) as g:
                for c in range(R):
                    low(g + (c + 1) // R, (c + 1) % R).then_inc(lo_done, 1)
            dve.wait_ge(sc_full, 1)
            v.tensor_copy(score[:, 1].rearrange("p a b -> p (a b)"), ps[:, 4:8, :].rearrange("p a b -> p (a b)")).then_inc(sc_done, 1)
            dve.wait_ge(sc_done, 2)

            ahead_n = [0]

            def ahead():
                if ahead_n[0] < PART:
                    ahead_n[0] += 1
                    u = G_OF["U0"] * R + ahead_n[0]
                    low(u // R, u % R).then_inc(lo_done, 1)

            def top16(rows, values, indices):
                n = len(rows)
                for j in range(n):
                    st(v.max(values[j][:, 0:8], rows[j]))
                ahead()
                st.done()
                for j in range(n):
                    st(v.max_index(indices[j][:, 0:8], values[j][:, 0:8], rows[j]))
                ahead()
                st.done()
                for j in range(n):
                    st(v.match_replace(rows[j], values[j][:, 0:8], rows[j], -3.0e38))
                ahead()
                st.done()
                for j in range(n):
                    st(v.max(values[j][:, 8:16], rows[j]))
                ahead()
                st.done()
                for j in range(n):
                    st(v.max_index(indices[j][:, 8:16], values[j][:, 8:16], rows[j]))
                ahead()
                st.done()

            iota16 = small_of("iota")[:, 0:TOPK]
            for t in range(T):
                top16([score[:, t, j, :] for j in range(16)], [half_v[:, j, :] for j in range(16)],
                      [half_i[:, j, :] for j in range(16)])
                st(v.tensor_copy(half_f, half_i))
                hv = half_v.rearrange("p (h s) k -> p h s k", s=2)
                st(tt(cand, hv[:, :, 0, :].unsqueeze(3).to_broadcast([P, PEER_HEADS, TOPK, TOPK]),
                      hv[:, :, 1, :].unsqueeze(2).to_broadcast([P, PEER_HEADS, TOPK, TOPK]), ALU.add))
                st.done()
                top16([cand[:, h].rearrange("p a b -> p (a b)") for h in range(PEER_HEADS)],
                      [top_v[:, h, :] for h in range(PEER_HEADS)], [pick[:, h, :] for h in range(PEER_HEADS)])
                st(ts(pick_i, pick, 4, None, ALU.logical_shift_right))
                st(ts(pick_j, pick, 15, None, ALU.bitwise_and))
                st.done()
                st(v.tensor_copy(pick_fi, pick_i))
                st(v.tensor_copy(pick_fj, pick_j))
                st.done()
                hf = half_f.rearrange("p (h s) k -> p h s k", s=2)
                for s, which in ((0, pick_fi), (1, pick_fj)):
                    shape = [P, PEER_HEADS * TOPK, TOPK]
                    m3 = match.rearrange("p h a b -> p (h a) b")
                    st(tt(m3, which.rearrange("p h k -> p (h k)").unsqueeze(2).to_broadcast(shape),
                          iota16[:, None, :].to_broadcast(shape), ALU.is_equal))
                    st.done()
                    st(tt(match, match, hf[:, :, s, :].unsqueeze(2).to_broadcast([P, PEER_HEADS, TOPK, TOPK]), ALU.mult))
                    st.done()
                    st(v.tensor_reduce(route[:, s, t, :], m3, AX, ALU.add))
                    ahead()
                    st.done()
                gates = route[:, 2, t, :].rearrange("p (h k) -> p h k", h=PEER_HEADS)
                tt(gates, top_v, top_v[:, :, 0:1].to_broadcast([P, PEER_HEADS, TOPK]), ALU.subtract).then_inc(rexp_in, 1)
            while ahead_n[0] < PART:
                ahead()
            for t in range(T):
                gates = route[:, 2, t, :].rearrange("p (h k) -> p h k", h=PEER_HEADS)
                dve.wait_ge(rexp_done, t + 1)
                st(v.tensor_reduce(hs[:, 0:8], gates, AX, ALU.add))
                st.done()
                st(v.reciprocal(hs[:, 8:16], hs[:, 0:8]))
                st.done()
                tt(gates, gates, hs[:, 8:16].unsqueeze(2).to_broadcast([P, PEER_HEADS, TOPK]), ALU.mult).then_inc(routed, 1)
                dve.wait_ge(routed, t + 1)
            dve.wait_ge(rt_full, 1)
            st(v.tensor_copy(gate_parts[:, 0, :], ps[:, 2, 0:SEQ]))
            st(v.tensor_copy(index[:, :, :], ps[:, 0:2, 0:SEQ]))
            st.done()
            st(tt(gate_parts[:, 1, :], ps[:, 2, 0:SEQ], gate_parts[:, 0, :].bitcast(F32), ALU.subtract))
            st.done()

            def token(table, t0, n):
                return table[:, bass.ds(t0, BATCH)].unsqueeze(2).to_broadcast([P, BATCH, n])

            def hot_first(t0, b):
                return tt(hot1[:, b, :, :], token(index[:, 0, :], t0, KEYS),
                          small_of("iota")[:, None, :].to_broadcast([P, BATCH, KEYS]), ALU.is_equal)

            def second_equal(q, t0):
                tt(hot2[:, :, 0, :], token(index[:, 1, :], t0, PART),
                   small_of("iota")[:, None, q * PART:(q + 1) * PART].to_broadcast([P, BATCH, PART]), ALU.is_equal).then_inc(hot_step, 1)

            def second_low(n, t0):
                dve.wait_ge(hot_step, n * 2 + 1)
                tt(hot2[:, :, 1, :], hot2[:, :, 0, :].bitcast(F32), token(gate_parts[:, 1, :].bitcast(F32), t0, PART),
                   ALU.mult).then_inc(hot_step, 1)

            def second_high(n, t0):
                dve.wait_ge(hot_step, n * 2 + 2)
                tt(hot2[:, :, 0, :], hot2[:, :, 0, :].bitcast(F32), token(gate_parts[:, 0, :].bitcast(F32), t0, PART),
                   ALU.mult).then_inc(hot_done, 1)

            def gate_sum(n, bank):
                dve.wait_ge(g_full, n + 1)
                v.tensor_reduce(gsum, ps[:, bank, :].rearrange("p (t s i) -> p t i s", t=BATCH, s=2), AX, ALU.add).then_inc(sum_step, 1)

            def gated(q, n, t0):
                dve.wait_ge(sum_step, n + 1)
                o = act_e[q % 2][:, :, bass.ds(t0, BATCH)].rearrange("p i t -> p t i")
                tt(o, o, gsum, ALU.mult).then_inc(g_used, 1)

            def first_batch(q):
                hot_first(0, 0)
                second_equal(q, 0)
                second_low(q * PART, 0)
                second_high(q * PART, 0)

            def gate_slot(q, n, t0, c, bank=0):
                hot_first(t0 + BATCH, (c + 1) % 2)
                gate_sum(n, bank + c % 2)
                second_equal(q, t0 + BATCH)
                gated(q, n, t0)
                second_low(n + 1, t0 + BATCH)
                second_high(n + 1, t0 + BATCH)

            def gate_slots(q, g, i):
                for c in range(R):
                    gate_slot(q, i * R + (q * PART + c), i * R * BATCH + c * BATCH, c)
                    low(g + (c + 1) // R, (c + 1) % R).then_inc(lo_done, 1)

            def take_sum(q):
                y = ysum[q % 2]
                dve.wait_ge(g2_done, 1)
                tt(y[:, 1, :], ps[:, 4:8, :].rearrange("p a b -> p (a b)"), gate2row, ALU.mult).then_inc(y_used, 1)

            def add_sum(q):
                y = ysum[q % 2]
                dve.wait_ge(y_used, 2 * (q + 1) + 2 * (q // 3))
                st(tt(y[:, 0, :], y[:, 0, :], gate2row, ALU.mult))
                st.done()
                for t in range(T):
                    tt(X[:, t, :], X[:, t, :], y[:, t, :], ALU.add).then_inc(x_done, 1)
                dve.wait_ge(x_done, T * (LAYERS + 3 + q + q // 3))

            def low_pair(g, c, chunk):
                low(g, c)
                tt(pairs[c % 2][:, 1, :, :], act_e[0][:, bass.ds(chunk, 2), :], pairs[c % 2][:, 0, :, :].bitcast(F32),
                   ALU.subtract).then_inc(lo_done, 1)

            def take_half(p):
                dve.wait_ge(unit_done, (G_OF[HALVED] + (p + 1) * PASS_G) * R)
                tt(ysum2[:, 1, :], ps[:, 4 + 2 * p:6 + 2 * p, :].rearrange("p a b -> p (a b)"),
                   gate2row[:, p * (DM // 2):(p + 1) * (DM // 2)], ALU.mult).then_inc(y_used, 1)

            def add_half(p):
                cols = slice(p * (DM // 2), (p + 1) * (DM // 2))
                dve.wait_ge(y_used, 2 * (PARTS - 2) + 2 * (p + 1))
                st(tt(ysum2[:, 0, :], ysum2[:, 0, :], gate2row[:, cols], ALU.mult))
                st.done()
                for t in range(T):
                    tt(X[:, t, cols], X[:, t, cols], ysum2[:, t, :], ALU.add).then_inc(x_done, 1)
                dve.wait_ge(x_done, T * (LAYERS + 5 + p))

            def down_halves(q):
                for p in range(2):
                    g0, b0 = G_OF[HALVED] + p * PASS_G, p * PASS_G * R
                    n0, bank = (q + 1) * PART + b0, 2 * (1 - p)
                    if p:
                        take_half(0)
                    with dve.Fori(0, PASS_G - 1) as i:
                        for c in range(R):
                            gate_slot(q + 1, i * R + (n0 + c), i * (R * BATCH) + (b0 + c) * BATCH, c, bank)
                            low_pair(i + (g0 + (c + 1) // R), (c + 1) % R, i * (2 * R) + 2 * (c + 1))
                    if p:
                        add_half(0)
                    i = PASS_G - 1
                    for c in range(R):
                        n, t0 = n0 + i * R + c, (b0 + i * R + c) * BATCH
                        if p == 0 or c < R - 1:
                            gate_slot(q + 1, n, t0, c, bank)
                        if c < R - 1:
                            low_pair(g0 + i, c + 1, PART - 2 * R + 2 * (c + 1))
                        elif p == 0:
                            low_pair(g0 + i + 1, 0, 0)
                        else:
                            gate_sum(n, bank + c % 2)
                            gated(q + 1, n, t0)
                            dve.wait_ge(g_used, PARTS * PART)
                            low_v(G_OF["V3"], 0, q + 1)

            def up_quarter(q):
                g0 = G_OF[f"U{q}"]
                if q > 1:
                    dve.wait_ge(unit_done, g0 * R)
                    take_sum(q - 2)
                dve.wait_ge(fm_free, N_U + q * PART + R)
                gate_slots(q - 1, g0, 0)
                if q > 1:
                    add_sum(q - 2)
                with dve.Fori(1, PART_G - 1) as i:
                    gate_slots(q - 1, i + g0, i)
                g, n, t0 = g0 + PART_G - 1, q * PART - R, SEQ - R * BATCH
                for c in range(R - 1):
                    gate_slot(q - 1, n + c, t0 + c * BATCH, c)
                    low(g, c + 1).then_inc(lo_done, 1)
                gate_sum(n + R - 1, (R - 1) % 2)
                gated(q - 1, n + R - 1, t0 + (R - 1) * BATCH)
                dve.wait_ge(g_used, q * PART)
                if q == PARTS - 1:
                    low_pair(g + 1, 0, 0)
                    first_batch(q)
                else:
                    low_v(g + 1, 0, q - 1)

            def down_quarter(q):
                g0 = G_OF[f"V{q}"]
                with dve.Fori(g0, g0 + PART_G - 1) as g:
                    for c in range(R):
                        low_v(g + (c + 1) // R, (c + 1) % R, q)
                for c in range(R - 1):
                    low_v(g0 + PART_G - 1, c + 1, q)
                if q < PARTS - 2:
                    first_batch(q + 1)
                    low(g0 + PART_G, 0).then_inc(lo_done, 1)

            first_batch(0)
            up_quarter(1)
            down_quarter(0)
            up_quarter(2)
            down_quarter(1)
            up_quarter(3)
            dve.wait_ge(fm_free, N_U + PARTS * PART + R)
            down_halves(2)
            take_half(1)
            add_half(1)
            down_quarter(3)
            dve.wait_ge(unit_done, GROUPS * R)
            take_sum(3)
            add_sum(3)
            dve.wait_ge(frs_done, 1)
            dve.wait_ge(gfin_ready, 16)
            for t in range(T):
                stt(X[:, t, :], X[:, t, :], rstd2[:, t:t + 1], gfin, ALU.mult, ALU.mult).then_inc(fin_ready, 1)


def rows_units(w):
    g = w.shape[1] // 512
    return w.reshape(4, 4, P, g, 512).transpose(3, 0, 2, 1, 4).reshape(4 * g, P, UNIT)


def cols_units(w):
    c = w.shape[1] // P
    return w.reshape(KD, P, c, P).transpose(2, 1, 0, 3).reshape(c, P, UNIT)


def padded(*parts):
    u = np.zeros((1, P, UNIT), np.float32)
    at = 0
    for p in parts:
        p = p.reshape(P, -1)
        u[0, :, at:at + p.shape[1]] = p
        at += p.shape[1]
    return u


def by_tile(w):
    return w.reshape(-1, P, w.shape[1]).transpose(1, 0, 2)


def col(vec):
    v = vec.reshape(-1, P)
    return np.ascontiguousarray(v.T)


def weight_stream(a):
    empty = np.zeros((1, P, UNIT), np.float32)
    units = []
    for l in range(LAYERS):
        w = a["w_in"][l]
        (aq, ak, av, ag, cq, ckv, kr, bg, q3, k3, v3, g3) = np.split(
            w, np.cumsum([1024, 256, 256, 1024, 512, 256, 64, 512, 512, 512, 512])[:11], axis=1)
        pad = np.zeros((DM, TM_W - 2880), np.float32)
        units.append(rows_units(np.concatenate([aq, ak, av, cq, v3, ckv, kr, pad], axis=1)))
        units.append(cols_units(np.concatenate([ag, bg, g3, q3, k3], axis=1)))
        uq = a["b_w_uq"][l].reshape(512, 4, 192)
        ukv = a["b_w_ukv"][l].reshape(256, 4, 256)
        units.append(padded(by_tile(uq[:, :, :128].reshape(512, 512))))
        units.append(padded(by_tile(uq[:, :, 128:].reshape(512, 256))))
        units.append(padded(by_tile(np.concatenate([ukv[:, :, :128].reshape(256, 512),
                                                    ukv[:, :, 128:].reshape(256, 512)], axis=1))))
        units.append(empty)
        units.append(rows_units(a["w_out"][l]))
    w = a["w_in_2"][0]
    (q, kc, vc, ks, vs, kw, vw, ga, qr, kr, vr, gr) = np.split(
        w, np.cumsum([1024] + [256] * 6 + [48, 1024, 1024, 1024])[:11], axis=1)
    units.append(rows_units(np.concatenate([vs, vw, vr], axis=1)))
    order = np.zeros((8, 2), np.int64)
    for h in range(NSA_HEADS):
        order[nsa_chunk(h)] = h
    qo = q.reshape(DM, NSA_HEADS, NSA_D)[:, order.reshape(-1)].reshape(DM, 1024)
    units.append(cols_units(np.concatenate([qo, kc, vc, ks, kw, qr, kr, gr], axis=1)))
    for name in ("cmp_k_w1_2", "cmp_v_w1_2"):
        w1 = a[name][0].reshape(2, 16, NSA_D, P).transpose(0, 2, 1, 3).reshape(2, NSA_D, UNIT)
        units.append(np.concatenate([w1, w1], axis=1))
    units.append(rows_units(a["w_out_2"][0]))
    units.append(cols_units(a["peer_w_q_2"][0]))
    u = a["peer_u_2"][0].reshape(KEYS, KEYS, KD, P).transpose(1, 3, 2, 0).reshape(KEYS, P, UNIT)
    v = a["peer_v_2"][0].reshape(KEYS, KEYS, DM).transpose(1, 0, 2)
    for name in EXPERT_ORDER:
        q = int(name[1])
        w = (u if name[0] == "U" else v)[q * PART:(q + 1) * PART]
        if name == HALVED:
            w = w.reshape(PART // 2, 2, P, 2, DM // 2).transpose(3, 0, 2, 1, 4).reshape(PART, P, UNIT)
        units.append(w)
    s = np.concatenate(units, axis=0)
    assert s.shape[0] == GROUPS * R, (s.shape, GROUPS * R)
    return s


def fill(spec, width, values):
    o = np.zeros((P, width), np.float32)
    for name, (at, n) in spec.items():
        o[:, at:at + n] = values[name]
    return o


def rotary(n):
    half = n // 2
    inv = (1.0 / (np.float32(10000.0) ** (np.arange(0, half, 2, dtype=np.float32) / np.float32(half)))).astype(np.float32)
    t = np.arange(SEQ)
    cos, sin = [], []
    for pos in (t // GRID, t % GRID):
        ang = pos.astype(np.float32)[:, None] * inv[None, :]
        cos += [np.cos(ang), np.cos(ang)]
        sin += [-np.sin(ang), np.sin(ang)]
    return [np.concatenate(z, axis=1).astype(np.float32) for z in (cos, sin)]


def tiles(m):
    return m.reshape(T, P, -1).transpose(1, 0, 2).reshape(P, -1)


def host(a):
    rep = lambda r: np.broadcast_to(r.reshape(1, -1), (P, r.size))
    b_ada = a["b_ada_2"][0]
    t = np.arange(SEQ)
    small = fill(SMALL, SMALL_W, {
        "ident": np.eye(P, dtype=np.float32), "one": 1.0, "pow": -0.5,
        "g_pre": np.concatenate([col(a["norm_pre"]), col(a["g_norm_mix_2"]), col(a["g_norm_ffn_2"])], axis=1),
        "b_qn": col(a["b_q_norm"]), "b_kvn": col(a["b_kv_norm"]),
        "cond": col(a["c_2"]), "b_ada": col(b_ada), "iota": np.arange(P, dtype=np.float32)[None, :],
    })
    w_gate = a["w_in_2"][0][:, 2560:2560 + NGATE]
    second = {
        "w_gate": by_tile(w_gate).reshape(P, -1),
        "g_nsa": col(a["g_nsa_out_2"]), "g_ret": col(a["g_ret_out_2"]),
        "row_ok": (t >= CMP_LEN - 1).astype(np.float32).reshape(T, P).T,
        "w2k": np.concatenate([a["cmp_k_w2_2"][0]] * 2, axis=1), "w2v": a["cmp_v_w2_2"][0],
        "pe": np.concatenate([np.concatenate([a[n][0].T] * 2, axis=0) for n in ("cmp_pe_k_2", "cmp_pe_v_2")], axis=1),
    }
    cos, sin = rotary(HD)
    cos_b, sin_b = rotary(64)
    c0 = np.clip(t % GRID - 8, 0, GRID - 16)
    kc = t % GRID
    near = (kc[None, :] >= c0[:P, None]) & (kc[None, :] < c0[:P, None] + 16)
    g_qk = np.stack([a["a_q_norm"], a["a_k_norm"]], axis=1).reshape(1, -1)
    const1 = fill(CONST1, CONST1_W, {
        "cos": tiles(cos), "sin": tiles(sin), "cos_b": tiles(cos_b), "sin_b": tiles(sin_b),
        "g_qk": rep(g_qk), "nbr": np.where(near, 0.0, MASKED)})
    d = (t[:, None] - t[None, :]).astype(np.float32)
    dist = np.where(d >= 0, d, np.float32(-MASKED))
    dc = (t[:, None] - (np.arange(NCMP) * CMP_STRIDE + CMP_LEN - 1)[None, :]).astype(np.float32)
    cb = np.where(dc[:, None, :] >= 0, -SLOPES[None, :, None] * dc[:, None, :], np.float32(MASKED))
    lg = np.log1p(-np.exp2(-5.0 - np.arange(RET_HEADS, dtype=np.float64)))
    dd = (t[None, :] - t[:, None]).astype(np.float64)
    decay = np.where(dd >= 0, np.exp(lg[:, None, None] * np.maximum(dd, 0)), 0.0) * HD ** -0.5
    decay = np.concatenate([decay[:, 0:P, :], decay[:, P:, P:]], axis=2).transpose(1, 0, 2).reshape(P, -1)
    const2 = fill(CONST2, CONST2_W, {
        **second,
        "dist": np.concatenate([dist[0:P, 0:P], dist[P:, :]], axis=1),
        "cmp_bias": tiles(cb.reshape(SEQ, -1))})
    rpb = np.pad(a["c_rpb"], ((0, 0), (0, 0), (0, 0), (48, 48)))
    win = np.stack([rpb[..., GRID - 1 - c:2 * GRID - 1 - c] for c in range(GRID)], axis=3)
    rows = t // GRID
    nbr = np.zeros((LAYERS, 2, GRID, 4, T, 4, GRID), np.float32)
    for qr in range(4):
        for kr in range(4):
            nbr[:, qr % 2, :, :, qr // 2, kr, :] = win[:, :, kr - qr + 7].transpose(0, 2, 1, 3)
    ada = a["w_ada_2"][0].reshape(ADA_H, 2, P, ADA_CG, 512).transpose(3, 0, 2, 1, 4).reshape(ADA_CG, ADA_H, P, ADA_UNIT)
    return {
        "stream": weight_stream(a), "ada": np.ascontiguousarray(ada), "small": small, "const1": const1,
        "const2": const2, "decays": np.ascontiguousarray(decay.astype(np.float32)),
        "keys": np.ascontiguousarray(a["peer_sub_keys_2"][0].reshape(16, KEYS, P).transpose(2, 0, 1).reshape(P, -1)),
        "nbr_bias": nbr.reshape(LAYERS, P, -1),
        "g_post": np.ascontiguousarray(np.broadcast_to(a["norm_post"][:, None, :], (LAYERS, P, DM))),
        "g_final": np.ascontiguousarray(rep(a["g_norm_final_2"])), "x": np.ascontiguousarray(a["x"]),
    }


def kernel(**inputs):
    import concourse.bacc as bacc
    from concourse.bass_utils import run_bass_kernel_spmd

    arrays = host({k: np.asarray(v) for k, v in inputs.items()})
    nc = bacc.Bacc("TRN2", target_bir_lowering=False, num_devices=1)
    args = [nc.dram_tensor(f"in_{n}", v.shape, F32, kind="ExternalInput").ap() for n, v in arrays.items()]
    out = nc.dram_tensor("out", (1, SEQ, DM), F32, kind="ExternalOutput").ap()
    block(nc, *args, out)
    r = run_bass_kernel_spmd(nc, [{f"in_{n}": v for n, v in arrays.items()}], core_ids=[0])
    return r.results[0]["out"]
```
